# Optimizing a Trainium2 kernel written in Bass

```python
import math
import jax
import jax.numpy as jnp
from jax import lax
import numpy as np

D_MODEL = 1024
BATCH = 1
SEQ = 256
DEPTH = 2

HEAD_DIM = 64
ATTN_WIDTH = D_MODEL // 2
N_Q_HEADS = ATTN_WIDTH // HEAD_DIM
N_KV_HEADS = 2
GQA_GROUP = N_Q_HEADS // N_KV_HEADS
KV_WIDTH = N_KV_HEADS * HEAD_DIM
WINDOW = 128
BLOCK = 128
N_BUCKETS = 32
MAX_DISTANCE = 128
SSM_GROUP_CH = 16
SSM_WIDTH = D_MODEL // 2
SSM_GROUPS = SSM_WIDTH // SSM_GROUP_CH
SSM_STATE = 64
DT_MIN = 1e-3
DT_MAX = 1e-1
N_BRANCHES = 2
IN_COLS = ATTN_WIDTH + 2 * KV_WIDTH + SSM_WIDTH + N_BRANCHES * D_MODEL
D_FF = 2816
N_EXPERTS = 8
TOP_K = 2
D_FF_EXPERT = 3584
N_DENSE = (DEPTH + 1) // 2
N_MOE = DEPTH // 2
PLE_DIM = 256
DEEPNORM_ALPHA = (2 * DEPTH) ** 0.25
DEEPNORM_BETA = (8 * DEPTH) ** -0.25
LN_EPS = 1e-5
NEG_INF = -1e30

kernel_name = "hybrid_swa_s5_moe_deepnorm"

def layer_norm(x, g, b):
    xf = x.astype(jnp.float32)
    mu = jnp.mean(xf, axis=-1, keepdims=True)
    var = jnp.mean(jnp.square(xf - mu), axis=-1, keepdims=True)
    y = (xf - mu) * lax.rsqrt(var + LN_EPS) * g.astype(jnp.float32) + b.astype(jnp.float32)
    return y.astype(x.dtype)

def t5_causal_bucket(dist):
    dist = jnp.maximum(dist, 0)
    max_exact = N_BUCKETS // 2
    d_f = jnp.maximum(dist, 1).astype(jnp.float32)
    large = max_exact + (jnp.log(d_f / max_exact) / math.log(MAX_DISTANCE / max_exact)
                         * (N_BUCKETS - max_exact)).astype(jnp.int32)
    large = jnp.minimum(large, N_BUCKETS - 1)
    return jnp.where(dist < max_exact, dist, large)

def sliding_window_attention(q, k, v, sinks, rel_bias):
    bsz, seq, _ = q.shape
    nb = seq // BLOCK
    q = q.reshape(bsz, nb, BLOCK, N_KV_HEADS, GQA_GROUP, HEAD_DIM) * (HEAD_DIM ** -0.5)
    k = k.reshape(bsz, seq, N_KV_HEADS, HEAD_DIM)
    v = v.reshape(bsz, seq, N_KV_HEADS, HEAD_DIM)
    pad = ((0, 0), (BLOCK, 0), (0, 0), (0, 0))
    kp = jnp.pad(k, pad)
    vp = jnp.pad(v, pad)
    blk = (bsz, nb, BLOCK, N_KV_HEADS, HEAD_DIM)
    kb = jnp.concatenate([kp[:, :seq].reshape(blk), k.reshape(blk)], axis=2)
    vb = jnp.concatenate([vp[:, :seq].reshape(blk), v.reshape(blk)], axis=2)

    logits = jnp.einsum('bnqhgd,bnshd->bnhgqs', q, kb).astype(jnp.float32)

    qi = jnp.arange(BLOCK, dtype=jnp.int32)[:, None]
    kj = jnp.arange(2 * BLOCK, dtype=jnp.int32)[None, :]
    dist = qi + BLOCK - kj
    bias = rel_bias.astype(jnp.float32)[t5_causal_bucket(dist)]
    bias = jnp.transpose(bias, (2, 0, 1)).reshape(N_KV_HEADS, GQA_GROUP, BLOCK, 2 * BLOCK)
    key_pos = jnp.arange(nb, dtype=jnp.int32)[:, None, None] * BLOCK - BLOCK + kj[None]
    mask = (dist >= 0)[None] & (dist < WINDOW)[None] & (key_pos >= 0)
    logits = jnp.where(mask[None, :, None, None], logits + bias, NEG_INF)

    s = sinks.astype(jnp.float32).reshape(N_KV_HEADS, GQA_GROUP)[None, None, :, :, None]
    m = jnp.maximum(jnp.max(logits, axis=-1), s)
    e = jnp.exp(logits - m[..., None])
    denom = jnp.sum(e, axis=-1) + jnp.exp(s - m)
    w = (e / denom[..., None]).astype(v.dtype)
    o = jnp.einsum('bnhgqs,bnshd->bnqhgd', w, vb)
    return o.reshape(bsz, seq, ATTN_WIDTH)

def s5_mixer(u, lam_re, lam_im, log_dt, b_re, b_im, c_re, c_im, d, w_glu, b_glu):
    bsz, seq, _ = u.shape
    f32 = jnp.float32
    uf = u.astype(f32).reshape(bsz, seq, SSM_GROUPS, SSM_GROUP_CH)
    lam = lax.complex(lam_re.astype(f32), lam_im.astype(f32))
    dt = jnp.exp(log_dt.astype(f32))[:, None]
    lam_bar = jnp.exp(lam * dt)
    b = lax.complex(b_re.astype(f32), b_im.astype(f32))
    b_bar = ((lam_bar - 1.0) / lam)[..., None] * b
    bu = jnp.einsum('bsgh,gph->bsgp', uf.astype(jnp.complex64), b_bar)
    a = jnp.broadcast_to(lam_bar, (1, seq, SSM_GROUPS, SSM_STATE))

    def combine(left, right):
        a_l, x_l = left
        a_r, x_r = right
        return a_r * a_l, a_r * x_l + x_r

    _, states = lax.associative_scan(combine, (a, bu), axis=1)
    c = lax.complex(c_re.astype(f32), c_im.astype(f32))
    y = jnp.real(jnp.einsum('bsgp,ghp->bsgh', states, c))
    y = y + d.astype(f32).reshape(SSM_GROUPS, SSM_GROUP_CH) * uf
    y = jax.nn.gelu(y.reshape(bsz, seq, SSM_WIDTH)).astype(u.dtype)
    return y * jax.nn.sigmoid(y @ w_glu + b_glu)

def swiglu(h, w_gate_up, w_down):
    gate, up = jnp.split(h @ w_gate_up, 2, axis=-1)
    return (jax.nn.silu(gate) * up) @ w_down

def moe_swiglu(h, router, w_gate_up, w_down):
    bsz, seq, dm = h.shape
    hf = h.reshape(bsz * seq, dm)
    logits = (hf @ router).astype(jnp.float32)
    top_v, top_i = lax.top_k(logits, TOP_K)
    gates = jax.nn.softmax(top_v, axis=-1)
    combine = jnp.sum(jax.nn.one_hot(top_i, N_EXPERTS, dtype=jnp.float32) * gates[..., None], axis=1)
    combine = combine.astype(h.dtype)
    out = jnp.zeros_like(hf)
    for e in range(N_EXPERTS):
        out = out + combine[:, e:e + 1] * swiglu(hf, w_gate_up[e], w_down[e])
    return out.reshape(bsz, seq, dm)

def setup_inputs(seed: int = 0) -> dict:
    key = jax.random.key(seed)
    ks = jax.random.split(key, 32)
    nrm = lambda k, shape, scale: jax.random.normal(k, shape, jnp.float32) * scale
    n_idx = jnp.arange(SSM_STATE, dtype=jnp.float32)
    return {
        "x": nrm(ks[0], (BATCH, SEQ, D_MODEL), 1.0),
        "p": nrm(ks[1], (DEPTH, BATCH, SEQ, PLE_DIM), 1.0),
        "rel_bias": nrm(ks[2], (N_BUCKETS, N_Q_HEADS), 0.5),
        "w_in": nrm(ks[3], (DEPTH, D_MODEL, IN_COLS), D_MODEL ** -0.5),
        "attn_sinks": nrm(ks[4], (DEPTH, N_Q_HEADS), 0.5),
        "ssm_lambda_re": -0.5 + nrm(ks[5], (DEPTH, SSM_GROUPS, SSM_STATE), 0.01),
        "ssm_lambda_im": math.pi * n_idx + nrm(ks[6], (DEPTH, SSM_GROUPS, SSM_STATE), 0.01),
        "ssm_log_dt": jax.random.uniform(ks[7], (DEPTH, SSM_GROUPS), jnp.float32,
                                         math.log(DT_MIN), math.log(DT_MAX)),
        "ssm_b_re": nrm(ks[8], (DEPTH, SSM_GROUPS, SSM_STATE, SSM_GROUP_CH), (2 * SSM_GROUP_CH) ** -0.5),
        "ssm_b_im": nrm(ks[9], (DEPTH, SSM_GROUPS, SSM_STATE, SSM_GROUP_CH), (2 * SSM_GROUP_CH) ** -0.5),
        "ssm_c_re": nrm(ks[10], (DEPTH, SSM_GROUPS, SSM_GROUP_CH, SSM_STATE), SSM_STATE ** -0.5),
        "ssm_c_im": nrm(ks[11], (DEPTH, SSM_GROUPS, SSM_GROUP_CH, SSM_STATE), SSM_STATE ** -0.5),
        "ssm_d": nrm(ks[12], (DEPTH, SSM_WIDTH), 1.0),
        "w_glu": nrm(ks[13], (DEPTH, SSM_WIDTH, SSM_WIDTH), SSM_WIDTH ** -0.5),
        "b_glu": nrm(ks[14], (DEPTH, SSM_WIDTH), 0.02),
        "w_branch_attn": nrm(ks[15], (DEPTH, ATTN_WIDTH, D_MODEL), ATTN_WIDTH ** -0.5),
        "w_branch_ssm": nrm(ks[16], (DEPTH, SSM_WIDTH, D_MODEL), SSM_WIDTH ** -0.5),
        "w_out": nrm(ks[17], (DEPTH, D_MODEL, D_MODEL), DEEPNORM_BETA * D_MODEL ** -0.5),
        "ln1_g": 1.0 + nrm(ks[18], (DEPTH, D_MODEL), 0.02),
        "ln1_b": nrm(ks[19], (DEPTH, D_MODEL), 0.02),
        "ffn_w_gate_up": nrm(ks[20], (N_DENSE, D_MODEL, 2 * D_FF), D_MODEL ** -0.5),
        "ffn_w_down": nrm(ks[21], (N_DENSE, D_FF, D_MODEL), DEEPNORM_BETA * D_FF ** -0.5),
        "moe_router": nrm(ks[22], (N_MOE, D_MODEL, N_EXPERTS), D_MODEL ** -0.5),
        "moe_w_gate_up": nrm(ks[23], (N_MOE, N_EXPERTS, D_MODEL, 2 * D_FF_EXPERT), D_MODEL ** -0.5),
        "moe_w_down": nrm(ks[24], (N_MOE, N_EXPERTS, D_FF_EXPERT, D_MODEL), DEEPNORM_BETA * D_FF_EXPERT ** -0.5),
        "ple_w_proj": nrm(ks[25], (DEPTH, PLE_DIM, D_MODEL), DEEPNORM_BETA * PLE_DIM ** -0.5),
        "ple_w_gate": nrm(ks[26], (DEPTH, D_MODEL, D_MODEL), D_MODEL ** -0.5),
        "ln2_g": 1.0 + nrm(ks[27], (DEPTH, D_MODEL), 0.02),
        "ln2_b": nrm(ks[28], (DEPTH, D_MODEL), 0.02),
    }

def reference(x, p, rel_bias, w_in, attn_sinks, ssm_lambda_re, ssm_lambda_im, ssm_log_dt,
              ssm_b_re, ssm_b_im, ssm_c_re, ssm_c_im, ssm_d, w_glu, b_glu,
              w_branch_attn, w_branch_ssm, w_out, ln1_g, ln1_b,
              ffn_w_gate_up, ffn_w_down, moe_router, moe_w_gate_up, moe_w_down,
              ple_w_proj, ple_w_gate, ln2_g, ln2_b):
    splits = np.cumsum([ATTN_WIDTH, KV_WIDTH, KV_WIDTH, SSM_WIDTH, D_MODEL])[:].tolist()
    for i in range(DEPTH):
        z = x @ w_in[i]
        q, k, v, u, g_attn, g_ssm = jnp.split(z, splits, axis=-1)
        a_out = sliding_window_attention(q, k, v, attn_sinks[i], rel_bias)
        s_out = s5_mixer(u, ssm_lambda_re[i], ssm_lambda_im[i], ssm_log_dt[i],
                         ssm_b_re[i], ssm_b_im[i], ssm_c_re[i], ssm_c_im[i], ssm_d[i],
                         w_glu[i], b_glu[i])
        merged = (jax.nn.sigmoid(g_attn) * (a_out @ w_branch_attn[i])
                  + jax.nn.sigmoid(g_ssm) * (s_out @ w_branch_ssm[i]))
        x = layer_norm(DEEPNORM_ALPHA * x + merged @ w_out[i], ln1_g[i], ln1_b[i])
        if i % 2 == 0:
            ffn = swiglu(x, ffn_w_gate_up[i // 2], ffn_w_down[i // 2])
        else:
            ffn = moe_swiglu(x, moe_router[i // 2], moe_w_gate_up[i // 2], moe_w_down[i // 2])
        ple = jax.nn.sigmoid(x @ ple_w_gate[i]) * (p[i] @ ple_w_proj[i])
        x = layer_norm(DEEPNORM_ALPHA * x + ffn + ple, ln2_g[i], ln2_b[i])
    return x


_drawn_inputs = setup_inputs


def setup_inputs(seed=0):
    import zlib

    import numpy as np

    out = dict(_drawn_inputs(seed))
    spreads = {}
    factors = {'attn_sinks': 8.0,
     'ssm_lambda_re': 64.0,
     'ssm_lambda_im': 36.136,
     'ssm_log_dt': 31.584,
     'ssm_b_re': 38.208,
     'ssm_b_im': 47.816,
     'ssm_c_re': 44.952,
     'ssm_c_im': 42.304,
     'b_glu': 36.353}
    for name, (base, spread) in spreads.items():
        noise = np.random.default_rng([zlib.crc32(name.encode()), seed]).standard_normal(out[name].shape)
        drawn = base * np.exp(spread * noise) if base else spread * noise
        out[name] = jnp.asarray(drawn.astype(out[name].dtype))
    for name, factor in factors.items():
        out[name] = (out[name] * factor).astype(out[name].dtype)
    return out
```

```python
from contextlib import ExitStack

import numpy as np

import concourse.bass as bass
from concourse import mybir

F32 = mybir.dt.float32
I32 = mybir.dt.int32
U32 = mybir.dt.uint32
ALU = mybir.AluOpType
ACT = mybir.ActivationFunctionType
AX = mybir.AxisListType.X

P = 128
D = 1024
SEQ = 256
DEPTH = 2
KD = D // P
NB = SEQ // P
HEADS, HD, BUCKETS = 8, 64, 32
AW = 512
KA = AW // P
SG, SCH, SST = 32, 16, 64
ST = SG * SST // P
DFF, DFE, NE, PLE = 2816, 3584, 8, 256
ALPHA = (2 * DEPTH) ** 0.25
EPS = 1e-5
NEG = -1e30
UNIT = 2048
RING = 6
FSTEPS = DFF // 256
ESTEPS = DFE // 512
DENSE_UNITS = 27
FFN_UNITS = 3 * FSTEPS
EXPERT_UNITS = 6 * ESTEPS
MOE_BASE = 2 * DENSE_UNITS + FFN_UNITS
GEMM_GROUPS = 32
SLOT_GROUPS = 14
GELU_C = 0.7978845608028654
BIAS_W = 3 * P


def constants():
    import math
    c = np.zeros((P, 4 * P + 8), np.float32)
    c[:, 0:P] = np.eye(P)
    c[:, P:2 * P] = np.arange(P)[None, :]
    c[:, 2 * P:3 * P] = np.arange(P)[:, None] < np.arange(P)[None, :]
    c[:, 3 * P:4 * P] = 1.0
    c[:, 4 * P:] = np.arange(8)[None, :]
    hot = np.zeros((BUCKETS + 1, BIAS_W), np.float32)
    for m in range(BIAS_W):
        dist = 2 * P - 1 - m
        if not 0 <= dist < P:
            hot[BUCKETS, m] = NEG
            continue
        half = BUCKETS // 2
        large = half + int(np.float32(np.log(np.float32(max(dist, 1)) / np.float32(half)))
                           / np.float32(math.log(128 / half)) * np.float32(BUCKETS - half))
        hot[dist if dist < half else min(large, BUCKETS - 1), m] = 1.0
    return c, hot


def program(nc, x, xT_in, pT_in, relb, hot_in, const_in, sinks, lre_in, lim_in, ldt_in, b_in, c_in,
            d_in, bglu_in, w_in, w_glu, w_ba, w_bs, w_out, ln_in, w_gu, w_dn, router, moe_gu, moe_dn,
            w_pp, w_pg, bias_scratch, out):
    ctx = ExitStack()
    with ctx:
        def sb(name, shape, dt=F32):
            return ctx.enter_context(nc.sbuf_tensor(name, shape, dt))

        def sem(name):
            return ctx.enter_context(nc.semaphore(name))

        ring = sb("ring", [P, RING, UNIT])
        xa = sb("xa", [P, NB, D])
        xb = sb("xb", [P, NB, D])
        xT = sb("xT", [P, KD, SEQ])
        bias = sb("bias", [P, HEADS, SEQ])
        phase = sb("phase", [P, 2, 2, 4, SEQ])
        bmat = sb("bmat", [P, DEPTH, 2, 4, P])
        cmat = sb("cmat", [P, 2, DEPTH * ST, 32])
        lnp = sb("lnp", [P, 2, D])
        pT = sb("pT", [P, 2, SEQ])
        cst = sb("cst", [P, 4 * P + 8])
        small = sb("small", [P, 40, 32])
        ptm = sb("ptm", [P, 2, 512])
        arena = sb("arena", [P, 18176])
        npass = sb("npass", [1, 1], I32)
        topi = sb("topi", [P, NB, 8], U32)

        ident, iota = cst[:, 0:P], cst[:, P:2 * P]
        below, ones = cst[:, 2 * P:3 * P], cst[:, 3 * P:4 * P]
        iota8 = cst[:, 4 * P:4 * P + 8]

        at = [0]

        def cut(n, *dims, reset=None):
            if reset is not None:
                at[0] = reset
            v = arena[:, at[0]:at[0] + n]
            at[0] += n
            if len(dims) == 1:
                return v.rearrange("p (a b) -> p a b", a=dims[0])
            if len(dims) == 2:
                return v.rearrange("p (a b c) -> p a b c", a=dims[0], b=dims[1])
            return v

        gth = cut(16 * SEQ, 16, reset=0)
        qT = cut(4 * SEQ, 4)
        kT = cut(2 * SEQ, 2)
        vt = cut(2 * P, 2)
        uT = cut(4 * SEQ, 4)
        lg = cut(4 * SEQ, 4)
        pr = cut(8 * P, 8)
        aT = cut(4 * SEQ, 4)
        yT = cut(4 * SEQ, 4)
        ga = qT
        sT = lg
        prod = cut(4 * 2 * SEQ, 4)
        vw = cut(4 * 2 * SEQ, 4)
        rot = cut(4 * 2 * SEQ, 4)
        xs = cut(2 * 2 * SEQ, 2)
        mT = rot.rearrange("p a b -> p (a b)").rearrange("p (a b) -> p a b", a=KD)
        mtmp = prod.rearrange("p a b -> p (a b)")[:, 0:2 * SEQ].rearrange("p (a b) -> p a b", a=2)
        assert at[0] <= 18176
        craw = cut(2 * DEPTH * ST * 32, 2, reset=0)
        relb_sb = cut(HEADS * P, HEADS)
        hot_sb = cut(BIAS_W)
        rows = cut(BIAS_W)
        pth = cut(4 * 512, 4, reset=0)
        hth = cut(2 * 512, 2)
        hga = cut(512)
        hid = cut(2 * 512, 2)
        hidT = cut(2 * 512, 2)
        xg = cut(KD * P, KD)
        ye = cut(D)
        pick = cut(2 * P, 2)
        pickw = cut(2 * P, 2)
        spread = cut(2 * P, 2)
        rt = cut(KD * 8, KD)
        assert at[0] <= 18176
        ptmp = hth

        def sm(i, n=32, j=0):
            return small[:, i, j:j + n]

        (LRE, LIM, LDT, DT, RR, TH, K1, K2, SN, SH, CS, NR, NI, DEN, CRE, CIM) = range(16)
        PWR, PWI = 16, 24
        sm_d, sm_hb = sm(32, 8), sm(33, 8)
        sink = sm(34, 16)
        stat = small[:, 35, 0:12].rearrange("p (a b) -> p a b", a=2)
        mv, veps, rstd, half_neg = sm(35, 2, 12), sm(35, 1, 14), sm(35, 1, 15), sm(35, 1, 16)
        mx, esk, den = sm(36, 4), sm(36, 4, 4), sm(36, 4, 8)
        sm_t = small[:, 37, 0:32]
        lgt = small[:, 38, 0:16].rearrange("p (a b) -> p a b", a=2)
        top = small[:, 38, 16:32].rearrange("p (a b) -> p a b", a=2)
        selm = small[:, 39, 0:16].rearrange("p (a b) -> p a b", a=2)
        comb = small[:, 39, 16:32].rearrange("p (a b) -> p a b", a=2)
        posm = small[:, 34, 16:32].rearrange("p (a b) -> p a b", a=2)
        oh = small[:, 33, 8:24].rearrange("p (a b) -> p a b", a=2)
        topf = small[:, 32, 8:24].rearrange("p (a b) -> p a b", a=2)
        gts = sm(35, 6, 20)
        cnt = sm(36, 2, 12)

        psum = ctx.enter_context(nc.psum_tensor("psum", [P, 8, 512], F32))
        bank = [psum[:, i, :] for i in range(8)]

        def halves(b):
            return bank[b][:, :].rearrange("p (a b) -> p a b", a=2)

        OUT_BANKS = (2, 3, 5, 6)
        HIDDEN_BANKS = ((0, 1), (4, 7))

        landed = [sem(f"unit_landed{i}") for i in range(RING)]
        unit_used = sem("unit_used")
        prep_in, const_dma, x_dma, bias_dma = sem("prep_landed"), sem("const_landed"), sem("x_landed"), sem("bias_moved")
        bias_ps, bias_row, bias_out = sem("bias_row_ready"), sem("bias_row_copied"), sem("bias_row_stored")
        pt_dma, ln_dma, rt_dma, out_dma = sem("ple_input_landed"), sem("ln_landed"), sem("router_landed"), sem("out_stored")
        dve_step, pool_step, final_step = sem("vector_step"), sem("pool_step"), sem("vector_final_step")
        exp_in, exp_out = sem("prep_for_scalar"), sem("prep_from_scalar")
        params_ready, phase_ready, phase_used = sem("params_ready"), sem("phase_ready"), sem("phase_used")
        g_full = sem("gemm_group_full")
        g_free = [sem("gemm_bank0_free"), sem("gemm_bank1_free")]
        u_ready, bu_full, bu_free = sem("u_ready"), sem("bu_full"), sem("bu_free")
        rot_ready, rot_used, xs_ready, y_full, y_free = (sem("rotated_back"), sem("rotated_back_used"), sem("states_ready"),
                                                         sem("y_full"), sem("y_free"))
        gelu_in, gelu_th, gelu_ready = sem("gelu_arg_ready"), sem("gelu_tanh_ready"), sem("gelu_ready")
        glu_th, s_ready = sem("glu_tanh_ready"), sem("s_ready")
        qk_ready = sem("qkv_ready")
        sc_full, sc_read = sem("scores_full"), sem("scores_read")
        soft_in, soft_exp, probs = sem("logits_ready"), sem("exp_ready"), sem("probs_ready")
        pt_full, pt_ready, av_full, a_ready = sem("probsT_full"), sem("probsT_ready"), sem("av_full"), sem("a_ready")
        m_ready, o_full, var_ready, rstd_ready = sem("merged_ready"), sem("out_full"), sem("var_ready"), sem("rstd_ready")
        ln_ready, xT_ready, ln_used = sem("ln_ready"), sem("xT_ready"), sem("ln_used")
        pg_full, pg_th, pp_full, res_ready = sem("ple_gate_full"), sem("ple_tanh_ready"), sem("ple_proj_full"), sem("residual_ready")
        h_full, h_th, h_ready, h_used = sem("hidden_full"), sem("hidden_tanh_ready"), sem("hidden_ready"), sem("hidden_used")
        r_full, sel_ready, pos_full, pass_ready = sem("router_full"), sem("selection_ready"), sem("positions_full"), sem("passes_ready")
        pick_ready, x_free = sem("pick_ready"), [sem("slot_bank5_free"), sem("slot_bank6_free")]
        x_full, xg_ready, hT_ready, spread_ready = sem("slot_group_full"), sem("gathered_ready"), sem("hiddenT_ready"), sem("spread_ready")
        ye_full, ye_ready = sem("expert_out_full"), sem("expert_out_ready")

        block = ctx.enter_context(nc.Block())

        def arrived(eng, u):
            eng.wait_ge(landed[u % RING], 16 * (u // RING + 1))

        class Chain:

            def __init__(self, eng, s):
                self.eng, self.sem, self.n, self.base = eng, s, 0, 0

            def link(self, ins):
                ins.then_inc(self.sem, 1)
                self.n += 1
                self.eng.wait_ge(self.sem, self.base + self.n)

        def dense_units(l):
            def cols(w, c, n=256):
                return w.rearrange("(k p) n -> p k n", p=P)[:, :, c:c + n]
            def krows(w, k, n=2):
                return w.rearrange("(k p) n -> p k n", p=P)[:, k:k + n, :]
            wi = w_in[l]
            yield from (cols(wi, c) for c in (768, 1024, 0, 256, 512))
            yield from (cols(wi, c) for c in range(1280, 3328, 256))
            yield cols(w_glu[l], 0, 512)
            yield from (cols(w_ba[l], c, 512) for c in (0, 512))
            yield from (cols(w_bs[l], c, 512) for c in (0, 512))
            yield from (krows(w_out[l], k) for k in range(0, KD, 2))
            yield krows(w_pp[l], 0)
            yield from (krows(w_pg[l], k) for k in range(0, KD, 2))

        @block.sync
        def _(sp):
            sp.dma_start(xT[:], xT_in.rearrange("(k p) n -> p k n", p=P)).then_inc(const_dma, 16)
            sp.dma_start(cst[:], const_in[:, :]).then_inc(const_dma, 16)

            def load(u, src, slot):
                if not isinstance(u, int) or u >= RING:
                    sp.wait_ge(unit_used, u - RING + 1)
                a, b = src.shape[-2:]
                sp.dma_start(ring[:, slot, :].rearrange("p (a b) -> p a b", a=a), src).then_inc(landed[slot], 16)

            def small_loads():
                for dst, src in ((relb_sb[0:BUCKETS + 1], relb), (hot_sb[0:BUCKETS + 1], hot_in),
                                 (craw.rearrange("p a b -> p (a b)"), c_in), (bmat[:].rearrange("p a b c d -> p (a b c d)"), b_in),
                                 (small[:, LRE, :], lre_in), (small[:, LIM, :], lim_in), (small[:, LDT, :], ldt_in),
                                 (sm_d, d_in), (sm_hb, bglu_in), (sink, sinks)):
                    sp.dma_start(dst, src).then_inc(prep_in, 16)

            u = 0
            for l in range(DEPTH):
                for src in dense_units(l):
                    load(u, src, u % RING)
                    u += 1
                    if u == 2:
                        small_loads()
                        sp.dma_start(xa[:], x.rearrange("(b p) d -> p b d", p=P)).then_inc(x_dma, 16)
                if l == 0:
                    gu = w_gu.rearrange("(k p) n -> p k n", p=P)
                    dn = w_dn.rearrange("(k p) n -> p k n", p=P)
                    def hidden(u, i, slot):
                        load(u, gu[:, :, bass.ds(i * 256, 256)], slot)
                        load(u + 1, gu[:, :, bass.ds(DFF + i * 256, 256)], (slot + 1) % RING)
                    def down(u, i, slot):
                        load(u, dn[:, bass.ds(i * 2, 2), :], slot)
                    hidden(u, 0, u % RING)
                    hidden(u + 2, 1, (u + 2) % RING)
                    down(u + 4, 0, (u + 4) % RING)
                    hidden(u + 5, 2, (u + 5) % RING)
                    down(u + 7, 1, (u + 7) % RING)
                    u += 8
                    with sp.Fori(1, FSTEPS // 2) as m:
                        v = u + (m - 1) * 6
                        hidden(v, 2 * m + 1, u % RING)
                        down(v + 2, 2 * m, (u + 2) % RING)
                        hidden(v + 3, 2 * m + 2, (u + 3) % RING)
                        down(v + 5, 2 * m + 1, (u + 5) % RING)
                    u += (FSTEPS // 2 - 1) * 6
                    down(u, FSTEPS - 1, u % RING)
                    u += 1
            assert u == MOE_BASE
            sp.wait_ge(pass_ready, 1)
            passes = sp.value_load(npass[0:1, 0:1], min_val=1, max_val=2)
            with sp.Fori(0, passes) as ps:
                with sp.Fori(0, NE) as e:
                    v = MOE_BASE + (ps * NE + e) * EXPERT_UNITS
                    gu = moe_gu.rearrange("(m p) n -> p m n", p=P)
                    dn = moe_dn.rearrange("(m p) n -> p m n", p=P)
                    q = 0
                    for j in range(ESTEPS + 1):
                        if j < ESTEPS:
                            for c in (j * 512, DFE + j * 512):
                                for k in (0, 4):
                                    load(v + q, gu[:, bass.ds(e * KD + k, 4), c:c + 512], (MOE_BASE + q) % RING)
                                    q += 1
                        if j >= 1:
                            for k in (0, 2):
                                load(v + q, dn[:, bass.ds(e * (DFE // P) + (j - 1) * 4 + k, 2), :], (MOE_BASE + q) % RING)
                                q += 1
            for b in range(NB):
                sp.wait_ge(ln_ready, 3 * NB + b + 1)
                sp.dma_start(out.rearrange("(b p) d -> p b d", p=P)[:, b, :], xa[:, b, :]).then_inc(out_dma, 16)
            sp.wait_ge(out_dma, 16 * NB)

        @block.tensor
        def _(pe):
            def slot(u, k):
                return ring[:, u % RING, :].rearrange("p (k n) -> p k n", k=k)

            def open_group(g):
                if g >= 2:
                    pe.wait_ge(g_free[g % 2], g // 2)
                return bank[g % 2]

            pe.wait_ge(prep_in, 160)
            for h in range(HEADS):
                if h:
                    pe.wait_ge(bias_row, h)
                pe.matmul(bank[7][:, 0:BIAS_W], relb_sb[0:BUCKETS + 1, h, :], hot_sb[0:BUCKETS + 1, :],
                          start=True, stop=True).then_inc(bias_ps, 1)
            pe.wait_ge(const_dma, 32)

            for l in range(DEPTH):
                U, G = l * (DENSE_UNITS + FFN_UNITS), l * GEMM_GROUPS
                state = {"u": U, "g": G}
                if l:
                    pe.wait_ge(xT_ready, 8 * (2 * l - 1) + 8)

                def project(kind):
                    u, g = state["u"], state["g"]
                    w = slot(u, KD)
                    arrived(pe, u)
                    b = open_group(g)
                    for t in range(2):
                        for q, m in ((0, HD), (HD, HD)) if kind == "kv" else ((0, P),):
                            for k in range(KD):
                                mm = pe.matmul(b[q:q + m, t * SEQ:(t + 1) * SEQ], w[:, k, t * m:(t + 1) * m], xT[:, k, :],
                                               start=(k == 0), stop=(k == KD - 1))
                    mm.then_inc(g_full, 1)
                    state["g"] += 1
                    if kind == "kv":
                        b = open_group(g + 1)
                        for t in range(NB):
                            for k in range(KD):
                                mm = pe.matmul(b[:, t * P:(t + 1) * P], xT[:, k, t * P:(t + 1) * P], w[:, k, P:2 * P],
                                               start=(k == 0), stop=(k == KD - 1))
                        mm.then_inc(g_full, 1)
                        state["g"] += 1
                    pe.drain().then_inc(unit_used, 1)
                    state["u"] += 1

                def input_states(b):
                    if b == 0:
                        pe.wait_ge(u_ready, 2 * (l + 1))
                        pe.wait_ge(params_ready, 1)
                    if 8 * l + b >= 1:
                        pe.wait_ge(bu_free, 8 * l + b)
                    for t in range(2):
                        i = 2 * b + t
                        q, c = 32 * (i % 4), i // 4
                        for ri in range(2):
                            mm = pe.matmul(bank[2 + t][:, ri * SEQ:(ri + 1) * SEQ], bmat[q:q + 32, l, ri, c, :],
                                           uT[q:q + 32, c, :], start=True, stop=True)
                    mm.then_inc(bu_full, 1)

                def output_states(b):
                    c = b // 2
                    pe.wait_ge(xs_ready, 2 * (8 * l + b + 1))
                    if b % 2 == 0 and 4 * l + c >= 1:
                        pe.wait_ge(y_free, 4 * l + c)
                    for t in range(2):
                        i = 2 * b + t
                        q = 32 * (i % 4)
                        for ri in range(2):
                            mm = pe.matmul(bank[4][q:q + 32, 0:SEQ], cmat[:, ri, l * ST + i, :],
                                           xs[:, ri, t * SEQ:(t + 1) * SEQ], start=(ri == 0), stop=(ri == 1))
                    mm.then_inc(y_full, 1)

                def scores(i):
                    n, kv = i // 2, i % 2
                    if i == 0:
                        pe.wait_ge(qk_ready, 4 * (l + 1))
                    if 4 * l + i >= 1:
                        pe.wait_ge(pt_ready, 4 * l + i)
                    keys = SEQ if n else P
                    for j in range(4):
                        h = 4 * kv + j
                        q = HD * (h % 2)
                        mm = pe.matmul(halves(5 + j % 2)[:, j // 2, SEQ - keys:SEQ], qT[q:q + HD, h // 2, n * P:(n + 1) * P],
                                       kT[q:q + HD, kv, 0:keys], start=True, stop=True)
                    mm.then_inc(sc_full, 1)

                def transpose_probs(i):
                    n = i // 2
                    pe.wait_ge(probs, 4 * l + i + 1)
                    for j in range(4):
                        for s in range(1 - n, 2):
                            mm = pe.transpose(bank[5 + j // 2][:, (2 * (j % 2) + s) * P:(2 * (j % 2) + s + 1) * P],
                                              lg[:, j, s * P:(s + 1) * P], ident)
                    mm.then_inc(pt_full, 1)

                def attend(i):
                    n, kv = i // 2, i % 2
                    pe.wait_ge(pt_ready, 4 * l + i + 1)
                    if 4 * l + i >= 1:
                        pe.wait_ge(a_ready, 4 * l + i)
                    for j in range(4):
                        blocks = range(1 - n, 2)
                        for s in blocks:
                            mm = pe.matmul(bank[7][HD * (j % 2):HD * (j % 2) + HD, (j // 2) * P:(j // 2 + 1) * P],
                                           vt[:, s - 1 + n, kv * HD:(kv + 1) * HD], pr[:, 2 * j + s, :],
                                           start=(s == blocks[0]), stop=(s == 1))
                    mm.then_inc(av_full, 1)

                project("u"), project("u")
                input_states(0)
                project("q"), project("q"), project("kv")
                input_states(1)
                scores(0)
                project("g")
                output_states(0), input_states(2)
                project("g")
                transpose_probs(0), output_states(1), input_states(3)
                project("g")
                attend(0), scores(1)
                project("g")
                output_states(2), input_states(4)
                project("g")
                transpose_probs(1), output_states(3), input_states(5)
                project("g")
                attend(1), scores(2)
                project("g")
                output_states(4), input_states(6)
                project("g")
                transpose_probs(2), output_states(5), input_states(7)
                attend(2), scores(3)
                output_states(6), output_states(7)
                transpose_probs(3), attend(3)

                u, g = state["u"], state["g"]
                arrived(pe, u)
                pe.wait_ge(gelu_ready, l + 1)
                w = slot(u, KA)
                for m in range(4):
                    if m % 2 == 0:
                        b = open_group(g + m // 2)
                    for k in range(KA):
                        mm = pe.matmul(b[:, (m % 2) * SEQ:(m % 2 + 1) * SEQ], w[:, k, m * P:(m + 1) * P], ga[:, k, :],
                                       start=(k == 0), stop=(k == KA - 1))
                    if m % 2:
                        mm.then_inc(g_full, 1)
                pe.drain().then_inc(unit_used, 1)
                u, g = u + 1, g + 2

                pe.wait_ge(a_ready, 4 * (l + 1))
                pe.wait_ge(s_ready, l + 1)
                for i in range(4):
                    arrived(pe, u + i)
                for c in range(KD):
                    b = open_group(g + c)
                    for s, act in ((0, aT), (1, sT)):
                        w = slot(u + 2 * s + c // 4, KA)
                        for k in range(KA):
                            mm = pe.matmul(b[:, s * SEQ:(s + 1) * SEQ], w[:, k, (c % 4) * P:(c % 4 + 1) * P], act[:, k, :],
                                           start=(k == 0), stop=(k == KA - 1))
                    mm.then_inc(g_full, 1)
                pe.drain().then_inc(unit_used, 4)
                u, g = u + 4, g + KD

                def by_token(u, n, banks, act, parts):
                    for i in range(n):
                        arrived(pe, u + i)
                        w = slot(u + i, 2)
                        for k in range(2):
                            for o, b in enumerate(banks):
                                mm = pe.matmul(bank[b][:, :], act[:, 2 * i + k, (o // 2) * P:(o // 2 + 1) * P],
                                               w[:, k, (o % 2) * 512:(o % 2 + 1) * 512],
                                               start=(i == 0 and k == 0), stop=(i == n - 1 and k == 1))
                        if i == n - 1:
                            mm.then_inc(parts, 1)
                            pe.drain().then_inc(unit_used, 1)
                        else:
                            mm.then_inc(unit_used, 1)

                pe.wait_ge(m_ready, KD * (l + 1))
                by_token(u, 4, OUT_BANKS, mT, o_full)
                u += 4

                def turn(src, which):
                    nonlocal g
                    for b in range(NB):
                        pe.wait_ge(ln_ready, which * NB + b + 1)
                        for q in range(2):
                            ps = open_group(g)
                            for k in range(4):
                                mm = pe.transpose(ps[:, k * P:(k + 1) * P], src[:, b, (4 * q + k) * P:(4 * q + k + 1) * P], ident)
                            mm.then_inc(g_full, 1)
                            g += 1

                turn(xb, 2 * l)
                for par in range(2):
                    pe.wait_ge(g_free[par], g // 2)
                if l == 0:
                    pe.wait_ge(pt_dma, 16)
                else:
                    pe.wait_ge(pt_dma, 32)
                by_token(u, 1, (0, 1, 4, 7), pT, pp_full)
                pe.wait_ge(xT_ready, 8 * 2 * l + 8)
                by_token(u + 1, 4, OUT_BANKS, xT, pg_full)
                u += 5
                pe.wait_ge(res_ready, l + 1)

                if l == 0:
                    def up(s, lap, par, free):
                        if free is not None:
                            pe.wait_ge(h_ready, free)
                        for o in range(2):
                            pe.wait_ge(landed[(s + o) % RING], 16 * ((s + o) // RING + 1) + lap)
                            w = slot(s + o, KD)
                            for f in range(2):
                                for k in range(KD):
                                    mm = pe.matmul(bank[HIDDEN_BANKS[par][o]][:, f * SEQ:(f + 1) * SEQ], w[:, k, f * P:(f + 1) * P],
                                                   xT[:, k, :], start=(k == 0), stop=(k == KD - 1))
                            if o:
                                mm.then_inc(h_full, 1)
                                pe.drain().then_inc(unit_used, 1)
                            else:
                                mm.then_inc(unit_used, 1)

                    def down(s, lap, par, ready, first=False, last=False):
                        pe.wait_ge(h_ready, ready)
                        pe.wait_ge(landed[s % RING], 16 * (s // RING + 1) + lap)
                        w = slot(s, 2)
                        for k in range(2):
                            for o, b in enumerate(OUT_BANKS):
                                mm = pe.matmul(bank[b][:, :], hid[:, par, k * SEQ + (o // 2) * P:k * SEQ + (o // 2 + 1) * P],
                                               w[:, k, (o % 2) * 512:(o % 2 + 1) * 512],
                                               start=(first and k == 0), stop=(last and k == 1), skip_group_check=True)
                        mm.then_inc(h_used, 1)
                        pe.drain().then_inc(unit_used, 1)

                    up(u, 0, 0, None)
                    up(u + 2, 0, 1, None)
                    down(u + 4, 0, 0, 1, first=True)
                    up(u + 5, 0, 0, 1)
                    down(u + 7, 0, 1, 2)
                    u += 8
                    with pe.Fori(1, FSTEPS // 2) as m:
                        lap = (m - 1) * 16
                        up(u, lap, 1, 2 * m)
                        down(u + 2, lap, 0, 2 * m + 1)
                        up(u + 3, lap, 0, 2 * m + 1)
                        down(u + 5, lap, 1, 2 * m + 2)
                    u += (FSTEPS // 2 - 1) * 6
                    down(u, 0, 0, FSTEPS, last=True)
                    pe.nop().then_inc(o_full, 1)
                    u += 1
                    turn(xa, 1)
                    assert g == GEMM_GROUPS

            pe.wait_ge(rt_dma, 16)
            for b in range(NB):
                for k in range(KD):
                    mm = pe.matmul(bank[0][:, b * 8:b * 8 + 8], xT[:, k, b * P:(b + 1) * P], rt[:, k, :],
                                   start=(k == 0), stop=(k == KD - 1))
            mm.then_inc(r_full, 1)
            pe.wait_ge(sel_ready, 1)
            pe.matmul(bank[1][:, 0:8], below, selm[:, 0, :], start=True, stop=True)
            pe.matmul(bank[1][:, 8:16], below, selm[:, 1, :], start=True, stop=False)
            pe.matmul(bank[1][:, 8:16], ones, selm[:, 0, :], start=False, stop=True)
            pe.matmul(bank[1][:, 16:24], ones, selm[:, 0, :], start=True, stop=False)
            pe.matmul(bank[1][:, 16:24], ones, selm[:, 1, :], start=False, stop=True).then_inc(pos_full, 1)

            pe.wait_ge(pass_ready, 1)
            passes = pe.value_load(npass[0:1, 0:1], min_val=1, max_val=2)
            with pe.Fori(0, passes) as ps:
                with pe.Fori(0, NE) as e:
                    it = ps * NE + e
                    lap = it * (16 * EXPERT_UNITS // RING)

                    def slot_group(x):
                        pe.wait_ge(x_free[x % 2], it * (SLOT_GROUPS // 2) + x // 2 + 1)
                        return bank[5 + x % 2]

                    def take(q):
                        v = MOE_BASE + q
                        pe.wait_ge(landed[v % RING], 16 * (v // RING + 1) + lap)
                        return v

                    pe.wait_ge(pick_ready, it + 1)
                    ps5 = slot_group(0)
                    for b in range(NB):
                        mm = pe.transpose(ps5[:, b * P:(b + 1) * P], pickw[:, b, :], ident)
                    mm.then_inc(x_full, 1)
                    for x in (1, 2):
                        psx = slot_group(x)
                        for k in range(4):
                            for b in range(NB):
                                dc = 4 * (x - 1) + k
                                mm = pe.matmul(psx[:, k * P:(k + 1) * P], xb[:, b, dc * P:(dc + 1) * P], pick[:, b, :],
                                               start=(b == 0), stop=(b == NB - 1))
                        mm.then_inc(x_full, 1)
                    pe.wait_ge(xg_ready, 2 * it + 2)
                    q = 0
                    for j in range(ESTEPS + 1):
                        if j < ESTEPS:
                            if j >= 2:
                                pe.wait_ge(h_ready, FSTEPS + it * ESTEPS + j - 1)
                            for o in range(2):
                                for kk in (0, 4):
                                    w = slot(take(q), 4)
                                    for k in range(4):
                                        mm = pe.matmul(bank[HIDDEN_BANKS[j % 2][o]][:, :], xg[:, kk + k, :], w[:, k, :],
                                                       start=(kk + k == 0), stop=(kk + k == KD - 1))
                                    if o and kk:
                                        mm.then_inc(h_full, 1)
                                        pe.drain().then_inc(unit_used, 1)
                                    else:
                                        mm.then_inc(unit_used, 1)
                                    q += 1
                        if j >= 1:
                            i = j - 1
                            pe.wait_ge(h_ready, FSTEPS + it * ESTEPS + i + 1)
                            psx = slot_group(3 + i)
                            for k in range(4):
                                mm = pe.transpose(psx[:, k * P:(k + 1) * P], hid[:, i % 2, k * P:(k + 1) * P], ident)
                            mm.then_inc(x_full, 1)
                            pe.wait_ge(hT_ready, it * ESTEPS + i + 1)
                            for kk in range(2):
                                w = slot(take(q), 2)
                                for k in range(2):
                                    for o in range(2):
                                        first, last = (i == 0 and kk + k == 0), (i == ESTEPS - 1 and kk + k == 2)
                                        c = 2 * kk + k
                                        mm = pe.matmul(bank[2 + o][:, :], hidT[:, i % 2, c * P:(c + 1) * P],
                                                       w[:, k, o * 512:(o + 1) * 512], start=first, stop=last)
                                if i == ESTEPS - 1 and kk:
                                    mm.then_inc(ye_full, 1)
                                    pe.drain().then_inc(unit_used, 1)
                                else:
                                    mm.then_inc(unit_used, 1)
                                q += 1
                    pe.wait_ge(ye_ready, it + 1)
                    pe.wait_ge(spread_ready, it + 1)
                    for o in range(4):
                        psx = slot_group(10 + o)
                        pe.matmul(psx[:, :], spread[:, o // 2, :], ye[:, (o % 2) * 512:(o % 2 + 1) * 512],
                                  start=True, stop=True).then_inc(x_full, 1)

        @block.scalar
        def _(act):
            act.wait_ge(exp_in, 1)
            act.activation(sm(SN), sm(TH), ACT.Sin).then_inc(exp_out, 1)
            act.activation(sm(SH), sm(TH), ACT.Sin, scale=0.5).then_inc(exp_out, 1)
            for h in range(HEADS):
                act.wait_ge(bias_ps, h + 1)
                if h:
                    act.wait_ge(bias_out, 16 * h)
                act.activation(rows, bank[7][:, 0:BIAS_W], ACT.Copy).then_inc(bias_row, 1)
            for l in range(DEPTH):
                G = l * GEMM_GROUPS
                gate = [0]

                def group(g):
                    act.wait_ge(g_full, G + g + 1)
                    return halves(g % 2)

                def gates():
                    g = 6 + gate[0]
                    act.activation(gth[:, 2 * gate[0]:2 * gate[0] + 2, :], group(g), ACT.Tanh, scale=0.5).then_inc(g_free[g % 2], 1)
                    gate[0] += 1

                def exp_probs(i):
                    act.wait_ge(soft_in, 2 * (4 * l + i + 1))
                    act.activation(esk, esk, ACT.Exp).then_inc(soft_exp, 1)
                    act.activation(lg[:, :, (1 - i // 2) * P:], lg[:, :, (1 - i // 2) * P:], ACT.Exp).then_inc(soft_exp, 1)

                def copy_probs(i):
                    act.wait_ge(pt_full, 4 * l + i + 1)
                    if 4 * l + i >= 1:
                        act.wait_ge(av_full, 4 * l + i)
                    n = i // 2
                    for j in range(2):
                        src = bank[5 + j][:, :].rearrange("p (h s n) -> p h s n", h=2, s=2)
                        dst = pr[:, 4 * j:4 * j + 4, :].rearrange("p (h s) n -> p h s n", h=2)
                        ins = act.activation(dst[:, :, 1 - n:, :], src[:, :, 1 - n:, :], ACT.Copy)
                    ins.then_inc(pt_ready, 1)

                def copy_attended(i):
                    n, kv = i // 2, i % 2
                    act.wait_ge(av_full, 4 * l + i + 1)
                    src = bank[7][:, 0:2 * P].rearrange("p (c n) -> p c n", c=2)
                    act.activation(aT[:, 2 * kv:2 * kv + 2, n * P:(n + 1) * P], src, ACT.Copy).then_inc(a_ready, 1)

                for g in (2, 3):
                    src = group(g)
                    act.activation(qT[:, 2 * (g - 2):2 * (g - 1), :], src, ACT.Copy, scale=HD ** -0.5).then_inc(qk_ready, 1)
                    act.wait_ge(qk_ready, 4 * l + g - 1)
                    act.nop().then_inc(g_free[g % 2], 1)
                act.activation(kT, group(4), ACT.Copy).then_inc(qk_ready, 1)
                act.wait_ge(qk_ready, 4 * l + 3)
                act.nop().then_inc(g_free[0], 1)
                act.wait_ge(g_full, G + 6)
                act.activation(vt, bank[1][:, 0:2 * P].rearrange("p (a b) -> p a b", a=2), ACT.Copy).then_inc(qk_ready, 1)
                act.wait_ge(qk_ready, 4 * l + 4)
                act.nop().then_inc(g_free[1], 1)
                gates(), exp_probs(0), gates(), copy_probs(0), gates(), copy_attended(0), gates(), exp_probs(1), gates()
                copy_probs(1), gates(), copy_attended(1), gates(), exp_probs(2), gates(), copy_probs(2), copy_attended(2)
                exp_probs(3), copy_probs(3), copy_attended(3)

                act.wait_ge(gelu_in, l + 1)
                act.activation(ga, ga, ACT.Tanh, scale=GELU_C).then_inc(gelu_th, 1)
                for m in range(4):
                    g = 14 + m // 2
                    act.wait_ge(g_full, G + g + 1)
                    ins = act.activation(uT[:, m, :], bank[g % 2][:, (m % 2) * SEQ:(m % 2 + 1) * SEQ], ACT.Tanh,
                                         bias=sm_hb[:, 4 * l + m:4 * l + m + 1], scale=0.5)
                    ins.then_inc(glu_th, 1)
                    if m % 2:
                        act.wait_ge(glu_th, 4 * l + m + 1)
                        act.nop().then_inc(g_free[g % 2], 1)

                def turned(g0, which):
                    for i in range(4):
                        g = G + g0 + i
                        act.wait_ge(g_full, g + 1)
                        b, q = i // 2, i % 2
                        src = bank[g % 2][:, :].rearrange("p (k n) -> p k n", k=4)
                        act.activation(xT[:, 4 * q:4 * q + 4, b * P:(b + 1) * P], src, ACT.Copy).then_inc(xT_ready, 1)
                        act.wait_ge(xT_ready, 8 * which + i + 1)
                        act.nop().then_inc(g_free[g % 2], 1)
                    act.nop().then_inc(xT_ready, 4)

                turned(24, 2 * l)
                act.wait_ge(pg_full, l + 1)
                for o, b in enumerate(OUT_BANKS):
                    ins = act.activation(pth[:, o, :], bank[b][:, :], ACT.Tanh, scale=0.5)
                ins.then_inc(pg_th, 1)
                if l == 0:
                    def hidden_tanh(i, par, used):
                        act.wait_ge(h_full, i)
                        if used is not None:
                            act.wait_ge(h_ready, used)
                        act.activation(hth[:, par, :], bank[HIDDEN_BANKS[par][0]][:, :], ACT.Tanh, scale=0.5).then_inc(h_th, 1)
                    act.wait_ge(res_ready, 1)
                    hidden_tanh(1, 0, None)
                    hidden_tanh(2, 1, None)
                    hidden_tanh(3, 0, 1)
                    with act.Fori(1, FSTEPS // 2) as m:
                        hidden_tanh(2 * m + 2, 1, 2 * m)
                        hidden_tanh(2 * m + 3, 0, 2 * m + 1)
                    turned(28, 1)

            act.wait_ge(soft_in, 2 * 4 * DEPTH + 1)
            act.activation(gts[:, 0:2], gts[:, 0:2], ACT.Exp).then_inc(soft_exp, 1)
            act.wait_ge(pass_ready, 1)
            passes = act.value_load(npass[0:1, 0:1], min_val=1, max_val=2)
            with act.Fori(0, passes) as ps:
                with act.Fori(0, NE) as e:
                    it = ps * NE + e
                    F = it * ESTEPS

                    def slot_group(x):
                        act.wait_ge(x_full, it * SLOT_GROUPS + x + 1)
                        return bank[5 + x % 2]

                    act.activation(spread, slot_group(0)[:, 0:2 * P].rearrange("p (a b) -> p a b", a=2),
                                   ACT.Copy).then_inc(spread_ready, 1)
                    act.wait_ge(spread_ready, it + 1)
                    act.nop().then_inc(x_free[0], 1)
                    for x in (1, 2):
                        act.activation(xg[:, 4 * (x - 1):4 * x, :], slot_group(x)[:, :].rearrange("p (a b) -> p a b", a=4),
                                       ACT.Copy).then_inc(xg_ready, 1)
                        act.wait_ge(xg_ready, it * 2 + x)
                        act.nop().then_inc(x_free[x % 2], 1)
                    for j in range(ESTEPS + 1):
                        if j < ESTEPS:
                            act.wait_ge(h_full, FSTEPS + F + j + 1)
                            act.wait_ge(h_ready, FSTEPS + F + max(j - 1, 0))
                            act.activation(hth[:, j % 2, :], bank[HIDDEN_BANKS[j % 2][0]][:, :], ACT.Tanh, scale=0.5).then_inc(h_th, 1)
                        if j >= 1:
                            i = j - 1
                            act.activation(hidT[:, i % 2, :], slot_group(3 + i)[:, :], ACT.Copy).then_inc(hT_ready, 1)
                            act.wait_ge(hT_ready, F + i + 1)
                            act.nop().then_inc(x_free[(3 + i) % 2], 1)
                    act.wait_ge(ye_full, it + 1)
                    act.activation(ye[:, 0:512], bank[2][:, :], ACT.Copy)
                    act.activation(ye[:, 512:1024], bank[3][:, :], ACT.Copy).then_inc(ye_ready, 1)

        @block.gpsimd
        def _(pool):
            c = Chain(pool, pool_step)
            c.link(pool.memset(half_neg, -0.5))

            def load_ln(n):
                if n:
                    pool.wait_ge(ln_used, 2 * n)
                pool.dma_start(lnp[:], ln_in[n]).then_inc(ln_dma, 16)

            pool.dma_start(pT[:], pT_in[0].rearrange("(k p) n -> p k n", p=P)).then_inc(pt_dma, 16)
            load_ln(0)
            for h in range(HEADS):
                pool.wait_ge(bias_row, h + 1)
                pool.dma_start(bias_scratch[h, 0:P, :], rows).then_inc(bias_out, 16)
            pool.wait_ge(bias_out, 16 * HEADS)
            for h in range(HEADS):
                flat = bias_scratch[h].rearrange("q m -> (q m)")
                band = flat[P - 1:P - 1 + P * (BIAS_W - 1)].rearrange("(q m) -> q m", m=BIAS_W - 1)[:, 0:SEQ]
                pool.dma_start(bias[:, h, :], band).then_inc(bias_dma, 16)
            pool.wait_ge(params_ready, 1)

            def phases(l, ch):
                n = 4 * l + ch
                if n >= 2:
                    pool.wait_ge(phase_used, 2 * (n - 1))
                co, si = phase[:, n % 2, 0], phase[:, n % 2, 1]
                pool.memset(co[:, :, 0:1], 1.0)
                c.link(pool.memset(si[:, :, 0:1], 0.0))
                for j in range(8):
                    k = 1 << j
                    s0 = l * ST + 4 * ch
                    wr = small[:, PWR + j, s0:s0 + 4].unsqueeze(2).to_broadcast([P, 4, k])
                    wi = small[:, PWI + j, s0:s0 + 4].unsqueeze(2).to_broadcast([P, 4, k])
                    t1, t2 = ptm[:, 0, 0:4 * k].rearrange("p (a b) -> p a b", a=4), ptm[:, 1, 0:4 * k].rearrange("p (a b) -> p a b", a=4)
                    pool.tensor_tensor(co[:, :, k:2 * k], co[:, :, 0:k], wr, ALU.mult)
                    pool.tensor_tensor(t1, si[:, :, 0:k], wi, ALU.mult)
                    pool.tensor_tensor(si[:, :, k:2 * k], si[:, :, 0:k], wr, ALU.mult)
                    c.link(pool.tensor_tensor(t2, co[:, :, 0:k], wi, ALU.mult))
                    pool.tensor_tensor(co[:, :, k:2 * k], co[:, :, k:2 * k], t1, ALU.subtract)
                    c.link(pool.tensor_tensor(si[:, :, k:2 * k], si[:, :, k:2 * k], t2, ALU.add))
                pool.nop().then_inc(phase_ready, 1)

            def states(l, b):
                n = 8 * l + b
                pool.wait_ge(rot_ready, n + 1)
                if n:
                    pool.wait_ge(y_full, n)
                pool.tensor_tensor(xs[:, 0, :], rot[:, 0, :], rot[:, 1, :], ALU.subtract).then_inc(xs_ready, 1)
                pool.tensor_tensor(xs[:, 1, :], rot[:, 2, :], rot[:, 3, :], ALU.add).then_inc(xs_ready, 1)

            def root(n):
                for b in range(NB):
                    pool.wait_ge(var_ready, NB * n + b + 1)
                    pool.tensor_tensor(rstd, veps, half_neg, ALU.pow).then_inc(rstd_ready, 1)

            phases(0, 0), phases(0, 1)
            for l in range(DEPTH):
                for b in range(8):
                    states(l, b)
                    if b % 2 and b // 2 + 2 < 4:
                        phases(l, b // 2 + 2)
                root(2 * l)
                load_ln(2 * l + 1)
                if l == 0:
                    phases(1, 0), phases(1, 1)
                    root(1)
                    load_ln(2)
                    pool.wait_ge(res_ready, 1)
                    pool.dma_start(pT[:], pT_in[1].rearrange("(k p) n -> p k n", p=P)).then_inc(pt_dma, 16)
                else:
                    pool.wait_ge(res_ready, 2)
                    pool.dma_start(rt, router.rearrange("(k p) n -> p k n", p=P)).then_inc(rt_dma, 16)
            pool.wait_ge(pass_ready, 1)
            root(3)

        @block.vector
        def _(dve):
            c = Chain(dve, dve_step)
            link = c.link

            def exp_accurate(dst, src, t1, t2, t3):
                link(dve.tensor_scalar(t1, src, -87.0, 88.0, ALU.max, ALU.min))
                link(dve.tensor_scalar(t2, t1, 1.4426950408889634, 12582912.0, ALU.mult, ALU.add))
                link(dve.tensor_scalar(t2, t2, -12582912.0, None, ALU.add))
                link(dve.scalar_tensor_tensor(out=t1, in0=t2, scalar=-0.693359375, in1=t1, op0=ALU.mult, op1=ALU.add))
                link(dve.scalar_tensor_tensor(out=t1, in0=t2, scalar=2.12194440e-4, in1=t1, op0=ALU.mult, op1=ALU.add))
                link(dve.tensor_scalar(t3, t1, 1 / 5040.0, 1 / 720.0, ALU.mult, ALU.add))
                for co in (1 / 120.0, 1 / 24.0, 1 / 6.0, 0.5, 1.0, 1.0):
                    link(dve.tensor_tensor(t3, t3, t1, ALU.mult))
                    link(dve.tensor_scalar(t3, t3, co, None, ALU.add))
                link(dve.tensor_scalar(t2, t2, 127.0, 8388608.0, ALU.add, ALU.mult))
                link(dve.tensor_copy(t1.bitcast(I32), t2))
                link(dve.tensor_tensor(dst, t3, t1, ALU.mult))

            dve.wait_ge(prep_in, 160)
            exp_accurate(sm(DT), sm(LDT), sm(NR), sm(NI), sm(DEN))
            link(dve.tensor_tensor(sm(K1), sm(LRE), sm(DT), ALU.mult))
            exp_accurate(sm(RR), sm(K1), sm(NR), sm(NI), sm(DEN))
            link(dve.tensor_tensor(sm(TH), sm(LIM), sm(DT), ALU.mult))
            link(dve.tensor_scalar(sm(K1), sm(TH), 0.15915494309189535, 12582912.0, ALU.mult, ALU.add))
            link(dve.tensor_scalar(sm(K1), sm(K1), -12582912.0, None, ALU.add))
            for part in (6.28125, 1.9340515136718750e-3, 1.2556659146e-06):
                link(dve.scalar_tensor_tensor(out=sm(TH), in0=sm(K1), scalar=-part, in1=sm(TH), op0=ALU.mult, op1=ALU.add))
            dve.tensor_scalar(sm(TH), sm(TH), -3.1415925, 3.1415925, ALU.max, ALU.min).then_inc(exp_in, 1)
            dve.wait_ge(exp_out, 2)
            link(dve.tensor_tensor(sm(CS), sm(SH), sm(SH), ALU.mult))
            link(dve.tensor_scalar(sm(CS), sm(CS), -2.0, 1.0, ALU.mult, ALU.add))
            link(dve.tensor_tensor(sm(NR), sm(RR), sm(CS), ALU.mult))
            link(dve.tensor_scalar(sm(NR), sm(NR), -1.0, None, ALU.add))
            link(dve.tensor_tensor(sm(NI), sm(RR), sm(SN), ALU.mult))
            link(dve.tensor_tensor(sm(DEN), sm(LRE), sm(LRE), ALU.mult))
            link(dve.tensor_tensor(sm(K1), sm(LIM), sm(LIM), ALU.mult))
            link(dve.tensor_tensor(sm(DEN), sm(DEN), sm(K1), ALU.add))
            link(dve.reciprocal(sm(DEN), sm(DEN)))
            link(dve.tensor_tensor(sm(CRE), sm(NR), sm(LRE), ALU.mult))
            link(dve.tensor_tensor(sm(K1), sm(NI), sm(LIM), ALU.mult))
            link(dve.tensor_tensor(sm(CRE), sm(CRE), sm(K1), ALU.add))
            link(dve.tensor_tensor(sm(CRE), sm(CRE), sm(DEN), ALU.mult))
            link(dve.tensor_tensor(sm(CIM), sm(NI), sm(LRE), ALU.mult))
            link(dve.tensor_tensor(sm(K1), sm(NR), sm(LIM), ALU.mult))
            link(dve.tensor_tensor(sm(CIM), sm(CIM), sm(K1), ALU.subtract))
            link(dve.tensor_tensor(sm(CIM), sm(CIM), sm(DEN), ALU.mult))
            dve.tensor_copy(sm(PWR), sm(CS))
            link(dve.tensor_copy(sm(PWI), sm(SN)))
            for j in range(7):
                a, b = sm(PWR + j), sm(PWI + j)
                dve.tensor_tensor(sm(K1), a, a, ALU.mult)
                dve.tensor_tensor(sm(K2), b, b, ALU.mult)
                link(dve.tensor_tensor(sm(PWI + j + 1), a, b, ALU.mult))
                dve.tensor_tensor(sm(PWR + j + 1), sm(K1), sm(K2), ALU.subtract)
                link(dve.tensor_scalar(sm(PWI + j + 1), sm(PWI + j + 1), 2.0, None, ALU.mult))
            wide = [P, DEPTH * ST, 32]
            cr, ci = (craw[:, r, :].rearrange("p (a b) -> p a b", b=32) for r in range(2))
            kr, ki = (sm(r).unsqueeze(2).to_broadcast(wide) for r in (CRE, CIM))
            sc = prod.rearrange("p a b -> p (a b)")[:, 0:DEPTH * ST * 32].rearrange("p (a b) -> p a b", b=32)
            link(dve.tensor_tensor(cmat[:, 0], cr, kr, ALU.mult))
            link(dve.tensor_tensor(sc, ci, ki, ALU.mult))
            link(dve.tensor_tensor(cmat[:, 0], cmat[:, 0], sc, ALU.subtract))
            link(dve.tensor_tensor(cmat[:, 1], cr, ki, ALU.mult))
            link(dve.tensor_tensor(sc, ci, kr, ALU.mult))
            link(dve.tensor_tensor(cmat[:, 1], cmat[:, 1], sc, ALU.add))
            link(dve.tensor_scalar(cmat[:, 1], cmat[:, 1], -1.0, None, ALU.mult))
            dve.tensor_scalar(sm_hb, sm_hb, 0.5, None, ALU.mult).then_inc(params_ready, 1)
            dve.wait_ge(x_dma, 16)

            def layer_norm(n, src, dst):
                for b in range(NB):
                    for h in range(2):
                        link(dve.bn_stats(stat[:, h, :], src[:, b, h * 512:(h + 1) * 512]))
                    link(dve.bn_aggr(mv, stat))
                    dve.tensor_scalar(veps, mv[:, 1:2], EPS, None, ALU.add).then_inc(var_ready, 1)
                    dve.wait_ge(rstd_ready, NB * n + b + 1)
                    link(dve.tensor_scalar(dst[:, b, :], src[:, b, :], mv[:, 0:1], rstd, ALU.subtract, ALU.mult))
                    if b == 0:
                        dve.wait_ge(ln_dma, 16 * (n + 1))
                    link(dve.tensor_tensor(dst[:, b, :], dst[:, b, :], lnp[:, 0, :], ALU.mult))
                    dve.tensor_tensor(dst[:, b, :], dst[:, b, :], lnp[:, 1, :], ALU.add).then_inc(ln_ready, 1)
                    dve.wait_ge(ln_ready, NB * n + b + 1)
                    dve.nop().then_inc(ln_used, 1)

            for l in range(DEPTH):
                G = l * GEMM_GROUPS
                for g in range(2):
                    dve.wait_ge(g_full, G + g + 1)
                    dve.tensor_copy(uT[:, 2 * g:2 * g + 2, :], halves(g)).then_inc(u_ready, 1)
                    dve.wait_ge(u_ready, 2 * l + g + 1)
                    dve.nop().then_inc(g_free[g], 1)

                def scan_states(b):
                    ch, n = b // 2, 8 * l + b
                    pn = 4 * l + ch
                    if b % 2 == 0:
                        dve.wait_ge(phase_ready, pn + 1)
                    t0 = 2 * (b % 2)
                    co = phase[:, pn % 2, 0, t0:t0 + 2, :].rearrange("p a b -> p (a b)")
                    si = phase[:, pn % 2, 1, t0:t0 + 2, :].rearrange("p a b -> p (a b)")
                    dve.wait_ge(bu_full, n + 1)
                    re, im = psum[:, 2:4, 0:SEQ], psum[:, 2:4, SEQ:2 * SEQ]
                    p4 = prod.rearrange("p a (t n) -> p a t n", t=2)
                    c4, s4 = phase[:, pn % 2, 0, t0:t0 + 2, :], phase[:, pn % 2, 1, t0:t0 + 2, :]
                    dve.tensor_tensor(p4[:, 0], re, c4, ALU.mult)
                    dve.tensor_tensor(p4[:, 1], im, s4, ALU.mult)
                    dve.tensor_tensor(p4[:, 2], im, c4, ALU.mult)
                    dve.tensor_tensor(p4[:, 3], re, s4, ALU.mult).then_inc(bu_free, 1)
                    dve.wait_ge(bu_free, n + 1)
                    dve.tensor_tensor(vw[:, 0, :], prod[:, 0, :], prod[:, 1, :], ALU.add)
                    link(dve.tensor_tensor(vw[:, 1, :], prod[:, 2, :], prod[:, 3, :], ALU.subtract))
                    for t in range(2):
                        i = l * ST + 2 * b + t
                        for ri in range(2):
                            ins = dve.tensor_tensor_scan(vw[:, 2 + ri, t * SEQ:(t + 1) * SEQ], small[:, RR, i:i + 1].to_broadcast([P, SEQ]),
                                                         vw[:, ri, t * SEQ:(t + 1) * SEQ], 0.0, ALU.mult, ALU.add)
                    link(ins)
                    if n:
                        dve.wait_ge(xs_ready, 2 * n)
                    dve.tensor_tensor(rot[:, 0, :], vw[:, 2, :], co, ALU.mult)
                    dve.tensor_tensor(rot[:, 1, :], vw[:, 3, :], si, ALU.mult)
                    dve.tensor_tensor(rot[:, 2, :], vw[:, 2, :], si, ALU.mult)
                    dve.tensor_tensor(rot[:, 3, :], vw[:, 3, :], co, ALU.mult).then_inc(rot_ready, 1)
                    dve.wait_ge(rot_ready, n + 1)
                    dve.nop().then_inc(phase_used, 1)

                def logits(i):
                    n, kv = i // 2, i % 2
                    o = (1 - n) * P
                    dve.wait_ge(sc_full, 4 * l + i + 1)
                    if l == 0 and i == 0:
                        dve.wait_ge(bias_dma, 16 * HEADS)
                    if 4 * l + i >= 1:
                        dve.wait_ge(pt_full, 4 * l + i)
                    for j in range(2):
                        h = 4 * kv + j
                        ins = dve.tensor_tensor(lg[:, j:4:2, o:], halves(5 + j)[:, :, o:], bias[:, h:h + 3:2, o:], ALU.add)
                    link(ins)
                    link(dve.tensor_reduce(mx, lg[:, :, o:], AX, ALU.max))
                    sk = sink[:, 8 * l + 4 * kv:8 * l + 4 * kv + 4]
                    link(dve.tensor_tensor(mx, mx, sk, ALU.max))
                    dve.tensor_tensor(esk, sk, mx, ALU.subtract).then_inc(soft_in, 1)
                    dve.tensor_tensor(lg[:, :, o:], lg[:, :, o:], mx.unsqueeze(2).to_broadcast([P, 4, SEQ - o]),
                                      ALU.subtract).then_inc(soft_in, 1)

                def normalise(i):
                    o = (1 - i // 2) * P
                    dve.wait_ge(soft_exp, 2 * (4 * l + i + 1))
                    link(dve.tensor_reduce(den, lg[:, :, o:], AX, ALU.add))
                    link(dve.tensor_tensor(den, den, esk, ALU.add))
                    link(dve.reciprocal(den, den))
                    dve.tensor_tensor(lg[:, :, o:], lg[:, :, o:], den.unsqueeze(2).to_broadcast([P, 4, SEQ - o]),
                                      ALU.mult).then_inc(probs, 1)

                def skip_term(ch):
                    dve.wait_ge(y_full, 8 * l + 2 * ch + 2)
                    link(dve.scalar_tensor_tensor(out=yT[:, ch, :], in0=uT[:, ch, :], scalar=sm_d[:, 4 * l + ch:4 * l + ch + 1],
                                                  in1=bank[4][:, 0:SEQ], op0=ALU.mult, op1=ALU.add))
                    dve.nop().then_inc(y_free, 1)

                scan_states(0), scan_states(1), logits(0), scan_states(2), normalise(0), scan_states(3)
                logits(1), skip_term(0), scan_states(4), normalise(1), scan_states(5), skip_term(1)
                logits(2), scan_states(6), normalise(2), scan_states(7), skip_term(2)
                logits(3), normalise(3), skip_term(3)

                link(dve.tensor_tensor(ga, yT, yT, ALU.mult))
                link(dve.tensor_scalar(ga, ga, 0.044715, 1.0, ALU.mult, ALU.add))
                dve.tensor_tensor(ga, ga, yT, ALU.mult).then_inc(gelu_in, 1)
                dve.wait_ge(gelu_th, l + 1)
                link(dve.scalar_tensor_tensor(out=ga, in0=ga, scalar=1.0, in1=yT, op0=ALU.add, op1=ALU.mult))
                dve.tensor_scalar(ga, ga, 0.5, None, ALU.mult).then_inc(gelu_ready, 1)
                dve.wait_ge(gelu_ready, l + 1)
                link(dve.tensor_scalar(yT, ga, 0.5, None, ALU.mult))
                dve.wait_ge(glu_th, 4 * (l + 1))
                dve.scalar_tensor_tensor(out=sT, in0=uT, scalar=1.0, in1=yT, op0=ALU.add, op1=ALU.mult).then_inc(s_ready, 1)

                for k in range(KD):
                    g = 16 + k
                    dve.wait_ge(g_full, G + g + 1)
                    a = bank[g % 2]
                    link(dve.scalar_tensor_tensor(out=mtmp[:, 0, :], in0=gth[:, k, :], scalar=1.0, in1=a[:, 0:SEQ],
                                                  op0=ALU.add, op1=ALU.mult))
                    link(dve.scalar_tensor_tensor(out=mtmp[:, 1, :], in0=gth[:, KD + k, :], scalar=1.0, in1=a[:, SEQ:2 * SEQ],
                                                  op0=ALU.add, op1=ALU.mult))
                    dve.nop().then_inc(g_free[g % 2], 1)
                    dve.tensor_tensor(mT[:, k, :], mtmp[:, 0, :], mtmp[:, 1, :], ALU.add).then_inc(m_ready, 1)
                    dve.wait_ge(m_ready, KD * l + k + 1)

                link(dve.tensor_scalar(xa[:], xa[:], ALPHA, None, ALU.mult))
                dve.wait_ge(o_full, (1 if l == 0 else 3))
                for o, b in enumerate(OUT_BANKS):
                    part = xa[:, o // 2, (o % 2) * 512:(o % 2 + 1) * 512]
                    link(dve.scalar_tensor_tensor(out=part, in0=bank[b][:, :], scalar=0.5, in1=part, op0=ALU.mult, op1=ALU.add))
                layer_norm(2 * l, xa, xb)

                link(dve.tensor_scalar(xa[:], xb[:], ALPHA, None, ALU.mult))
                dve.wait_ge(pp_full, l + 1)
                dve.wait_ge(pg_th, l + 1)
                for o, b in enumerate((0, 1, 4, 7)):
                    part = xa[:, o // 2, (o % 2) * 512:(o % 2 + 1) * 512]
                    link(dve.scalar_tensor_tensor(out=hga, in0=pth[:, o, :], scalar=1.0, in1=bank[b][:, :], op0=ALU.add, op1=ALU.mult))
                    link(dve.scalar_tensor_tensor(out=part, in0=hga, scalar=0.5, in1=part, op0=ALU.mult, op1=ALU.add))
                dve.nop().then_inc(res_ready, 1)

                def hidden(i, par, used):
                    dve.wait_ge(h_th, i)
                    link(dve.scalar_tensor_tensor(out=hga, in0=hth[:, par, :], scalar=1.0, in1=bank[HIDDEN_BANKS[par][0]][:, :],
                                                  op0=ALU.add, op1=ALU.mult))
                    if used is not None:
                        dve.wait_ge(h_used, used)
                    dve.scalar_tensor_tensor(out=hid[:, par, :], in0=hga, scalar=0.5, in1=bank[HIDDEN_BANKS[par][1]][:, :],
                                             op0=ALU.mult, op1=ALU.mult).then_inc(h_ready, 1)
                    dve.wait_ge(h_ready, i)

                if l == 0:
                    hidden(1, 0, None), hidden(2, 1, None), hidden(3, 0, 1)
                    n0 = c.n
                    with dve.Fori(1, FSTEPS // 2) as m:
                        c.base = (m - 1) * 2
                        hidden(2 * m + 2, 1, 2 * m)
                        hidden(2 * m + 3, 0, 2 * m + 1)
                    c.base, c.n = 0, n0 + 2 * (FSTEPS // 2 - 1)
                    dve.wait_ge(o_full, 2)
                    for o, b in enumerate(OUT_BANKS):
                        part = xa[:, o // 2, (o % 2) * 512:(o % 2 + 1) * 512]
                        link(dve.tensor_tensor(part, bank[b][:, :], part, ALU.add))
                    layer_norm(1, xa, xa)

            dve.wait_ge(r_full, 1)
            link(dve.tensor_copy(lgt, bank[0][:, 0:16].rearrange("p (a b) -> p a b", a=2)))
            for b in range(NB):
                link(dve.max(top[:, b, :], lgt[:, b, :]))
                link(dve.max_index(topi[:, b, :], top[:, b, :], lgt[:, b, :]))
            link(dve.tensor_copy(topf, topi[:]))
            dve.tensor_tensor(gts[:, 0:2], top[:, :, 1], top[:, :, 0], ALU.subtract).then_inc(soft_in, 1)
            dve.wait_ge(soft_exp, 8 * DEPTH + 1)
            link(dve.tensor_scalar(gts[:, 2:4], gts[:, 0:2], 1.0, None, ALU.add))
            link(dve.reciprocal(gts[:, 2:4], gts[:, 2:4]))
            link(dve.tensor_tensor(gts[:, 4:6], gts[:, 0:2], gts[:, 2:4], ALU.mult))
            for b in range(NB):
                link(dve.tensor_scalar(comb[:, b, :], iota8, topf[:, b, 0:1], gts[:, 2 + b:3 + b], ALU.is_equal, ALU.mult))
                link(dve.tensor_scalar(oh[:, b, :], iota8, topf[:, b, 1:2], gts[:, 4 + b:5 + b], ALU.is_equal, ALU.mult))
                link(dve.tensor_tensor(comb[:, b, :], comb[:, b, :], oh[:, b, :], ALU.add))
                link(dve.tensor_scalar(oh[:, b, :], iota8, topf[:, b, 0:1], None, ALU.is_equal))
                link(dve.tensor_scalar(selm[:, b, :], iota8, topf[:, b, 1:2], None, ALU.is_equal))
                link(dve.tensor_tensor(selm[:, b, :], selm[:, b, :], oh[:, b, :], ALU.add))
            dve.nop().then_inc(sel_ready, 1)
            dve.wait_ge(pos_full, 1)
            link(dve.tensor_tensor(posm, bank[1][:, 0:16].rearrange("p (a b) -> p a b", a=2), selm, ALU.mult))
            link(dve.tensor_scalar(oh, selm, 4096.0, -4096.0, ALU.mult, ALU.add))
            link(dve.tensor_tensor(posm, posm, oh, ALU.add))
            link(dve.tensor_reduce(cnt[:, 0:1], bank[1][:, 16:24], AX, ALU.max))
            link(dve.tensor_scalar(cnt[:, 0:1], cnt[:, 0:1], float(P), 1.0, ALU.is_gt, ALU.add))
            for s in x_free:
                dve.nop().then_inc(s, 1)
            dve.tensor_copy(npass[:], cnt[0:1, 0:1]).then_inc(pass_ready, 1)
            dve.wait_ge(pass_ready, 1)
            passes = dve.value_load(npass[0:1, 0:1], min_val=1, max_val=2)
            n0 = c.n
            per_expert = ESTEPS + 4
            per_pass = NE * per_expert + 1
            with dve.Fori(0, passes) as ps:
                with dve.Fori(0, NE) as e:
                    it = ps * NE + e
                    c.n, c.base = n0, ps * per_pass + e * per_expert
                    F = FSTEPS + it * ESTEPS
                    for b in range(NB):
                        dve.tensor_scalar(pick[:, b, :], iota, posm[:, b, bass.ds(e, 1)], None, ALU.is_equal)
                        ins = dve.tensor_scalar(pickw[:, b, :], iota, posm[:, b, bass.ds(e, 1)], comb[:, b, bass.ds(e, 1)],
                                                ALU.is_equal, ALU.mult)
                    ins.then_inc(pick_ready, 1)
                    for j in range(ESTEPS):
                        dve.wait_ge(h_th, F + j + 1)
                        link(dve.scalar_tensor_tensor(out=hga, in0=hth[:, j % 2, :], scalar=1.0, in1=bank[HIDDEN_BANKS[j % 2][0]][:, :],
                                                      op0=ALU.add, op1=ALU.mult))
                        if j >= 2:
                            dve.wait_ge(hT_ready, it * ESTEPS + j - 1)
                        dve.scalar_tensor_tensor(out=hid[:, j % 2, :], in0=hga, scalar=0.5, in1=bank[HIDDEN_BANKS[j % 2][1]][:, :],
                                                 op0=ALU.mult, op1=ALU.mult).then_inc(h_ready, 1)
                        dve.wait_ge(h_ready, F + j + 1)
                    for o in range(4):
                        x = 10 + o
                        dve.wait_ge(x_full, it * SLOT_GROUPS + x + 1)
                        part = xa[:, o // 2, (o % 2) * 512:(o % 2 + 1) * 512]
                        link(dve.tensor_tensor(part, bank[5 + x % 2][:, :], part, ALU.add))
                        dve.nop().then_inc(x_free[x % 2], 1)
                c.n, c.base = n0 + NE * per_expert, ps * per_pass
                link(dve.tensor_scalar(posm, posm, -float(P), None, ALU.add))
            c.sem, c.n, c.base = final_step, 0, 0
            layer_norm(3, xa, xa)


def kernel(**inputs):
    import concourse.bacc as bacc
    from concourse.bass_utils import run_bass_kernel_spmd

    a = {k: np.asarray(v) for k, v in inputs.items()}
    con, hot = constants()

    def pairs(v):
        return np.ascontiguousarray(v.reshape(DEPTH, ST, 2 * SST).transpose(2, 0, 1)).reshape(P, DEPTH * ST)

    relb = np.ones((BUCKETS + 1, HEADS, P), np.float32)
    relb[:BUCKETS] = a["rel_bias"][:, :, None]
    bm = np.zeros((4, 2, SCH, DEPTH, 2, 4, 2, SST), np.float32)
    cm = np.zeros((2, SST, 2, DEPTH, ST, 2, SCH), np.float32)
    for r, (bn, cn) in enumerate((("ssm_b_re", "ssm_c_re"), ("ssm_b_im", "ssm_c_im"))):
        b = a[bn].reshape(DEPTH, 4, 4, 2, SST, SCH)
        c = a[cn].reshape(DEPTH, ST, 2, SCH, SST)
        for par in range(2):
            bm[:, par, :, :, r, :, par, :] = b[:, :, :, par].transpose(2, 4, 0, 1, 3)
            cm[par, :, r, :, :, par, :] = c[:, :, par].transpose(3, 0, 1, 2)

    def by_channel(v):
        return np.ascontiguousarray(v.reshape(DEPTH, 4, P).transpose(2, 0, 1)).reshape(P, DEPTH * 4)

    ln = np.stack([np.stack([a[g][l], a[b][l]]) for l in range(DEPTH) for g, b in (("ln1_g", "ln1_b"), ("ln2_g", "ln2_b"))])
    arrays = {
        "x": a["x"].reshape(SEQ, D),
        "xT": np.ascontiguousarray(a["x"].reshape(SEQ, D).T),
        "pT": np.ascontiguousarray(a["p"].reshape(DEPTH, SEQ, PLE).transpose(0, 2, 1)),
        "relb": relb, "hot": hot, "const": con,
        "sinks": np.ascontiguousarray(np.broadcast_to(a["attn_sinks"].reshape(1, DEPTH * HEADS), (P, DEPTH * HEADS))),
        "lre": pairs(a["ssm_lambda_re"]), "lim": pairs(a["ssm_lambda_im"]),
        "ldt": pairs(np.repeat(a["ssm_log_dt"][:, :, None], SST, axis=2)),
        "b": bm.reshape(P, -1), "c": cm.reshape(P, -1),
        "d": by_channel(a["ssm_d"]), "bglu": by_channel(a["b_glu"]),
        "w_in": a["w_in"], "w_glu": a["w_glu"], "w_ba": a["w_branch_attn"], "w_bs": a["w_branch_ssm"], "w_out": a["w_out"],
        "ln": np.ascontiguousarray(np.broadcast_to(ln[:, None], (2 * DEPTH, P, 2, D))),
        "w_gu": a["ffn_w_gate_up"][0], "w_dn": a["ffn_w_down"][0], "router": a["moe_router"][0],
        "moe_gu": a["moe_w_gate_up"].reshape(NE * D, 2 * DFE), "moe_dn": a["moe_w_down"].reshape(NE * DFE, D),
        "w_pp": a["ple_w_proj"], "w_pg": a["ple_w_gate"],
    }
    nc = bacc.Bacc("TRN2", target_bir_lowering=False, num_devices=1)
    args, feed = [], {}
    for name, v in arrays.items():
        feed[f"in_{name}"] = v
        args.append(nc.dram_tensor(f"in_{name}", v.shape, F32, kind="ExternalInput").ap())
    scratch = nc.dram_tensor("bias_scratch", (HEADS, P + 1, BIAS_W), F32, kind="Internal").ap()
    out = nc.dram_tensor("out", (SEQ, D), F32, kind="ExternalOutput").ap()
    program(nc, *args, scratch, out)
    r = run_bass_kernel_spmd(nc, [feed], core_ids=[0])
    return r.results[0]["out"].reshape(1, SEQ, D)
```

```python
from contextlib import ExitStack

import numpy as np

import concourse.bass as bass
from concourse import mybir

F32 = mybir.dt.float32
F32R = mybir.dt.float32r
I32 = mybir.dt.int32
U32 = mybir.dt.uint32
ALU = mybir.AluOpType
ACT = mybir.ActivationFunctionType
AX = mybir.AxisListType.X

P = 128
D = 1024
SEQ = 256
DEPTH = 2
KD = D // P
NB = SEQ // P
HEADS, HD, BUCKETS = 8, 64, 32
AW = 512
KA = AW // P
SG, SCH, SST = 32, 16, 64
ST = SG * SST // P
DFF, DFE, NE, PLE = 2816, 3584, 8, 256
ALPHA = (2 * DEPTH) ** 0.25
EPS = 1e-5
NEG = -1e30
UNIT = 2048
RING = 6
SPLIT = 3
FSTEPS = DFF // 256
ESTEPS = DFE // 512
PLAIN_UNITS = 22
DENSE_UNITS = 27
FFN_UNITS = 3 * FSTEPS
EXPERT_UNITS = 6 * ESTEPS
MOE_BASE = 2 * DENSE_UNITS + FFN_UNITS
GEMM_GROUPS = 32
SLOT_GROUPS = 14
GELU_C = 0.7978845608028654
BIAS_W = 3 * P


def constants():
    import math
    c = np.zeros((P, 4 * P + 8), np.float32)
    c[:, 0:P] = np.eye(P)
    c[:, P:2 * P] = np.arange(P)[None, :]
    c[:, 2 * P:3 * P] = np.arange(P)[:, None] < np.arange(P)[None, :]
    c[:, 3 * P:4 * P] = 1.0
    c[:, 4 * P:] = np.arange(8)[None, :]
    hot = np.zeros((BUCKETS + 1, BIAS_W), np.float32)
    for m in range(BIAS_W):
        dist = 2 * P - 1 - m
        if not 0 <= dist < P:
            hot[BUCKETS, m] = NEG
            continue
        half = BUCKETS // 2
        large = half + int(np.float32(np.log(np.float32(max(dist, 1)) / np.float32(half)))
                           / np.float32(math.log(128 / half)) * np.float32(BUCKETS - half))
        hot[dist if dist < half else min(large, BUCKETS - 1), m] = 1.0
    return c, hot


def program(nc, x, xT_in, pT_in, relb, hot_in, const_in, sinks, lre_in, lim_in, ldt_in, b_in, c_in,
            d_in, bglu_in, w_in, w_glu, w_ba, w_bs, w_out, ln_in, w_gu, w_dn, router, moe_gu, moe_dn,
            w_pp, w_pg, bias_scratch, out):
    ctx = ExitStack()
    with ctx:
        BASE, END = 16512, 229344
        top = [0]

        def place(name, shape, dt=F32, at=None):
            n = int(np.prod(shape[1:]))
            if at is None:
                at = top[0]
                top[0] += -(-n // 8) * 8
                assert BASE + 4 * top[0] <= END, (name, top[0])
            return nc.alloc_sbuf_tensor_at(name, shape, dt, offset=BASE + 4 * at)

        def sem(name):
            return ctx.enter_context(nc.semaphore(name))

        ring = place("ring", [P, RING, UNIT])
        xa = place("xa", [P, NB, D])
        xb = place("xb", [P, NB, D])
        lnp = place("lnp", [P, 2, D])
        cst = place("cst", [P, 4 * P + 8])
        small = place("small", [P, 40, 32])
        pT = place("pT", [P, 2, SEQ])
        xT_at = top[0]
        xT = place("xT", [P, KD, SEQ])
        rth, rtl = place("rth", [P, KD, 8], F32R), place("rtl", [P, KD, 8], F32R)
        npass = place("npass", [1, 8], I32)
        topi = place("topi", [P, NB, 8], U32)
        mixers_at = top[0]
        bias = place("bias", [P, HEADS, SEQ])
        phase = place("phase", [P, 2, 2, 4, SEQ])
        bmat = place("bmat", [P, DEPTH, 2, 4, P])
        cmat = place("cmat", [P, 2, DEPTH * ST, 32])
        ptm = place("ptm", [P, 2, 512])
        arena_at = top[0]
        ARENA = (END - BASE) // 4 - arena_at
        arena = place("arena", [P, ARENA // 8 * 8])
        xTh = place("xTh", [P, KD, SEQ], F32R, at=xT_at)
        over = [arena_at]

        def overlay(name, shape, dt=F32):
            t = place(name, shape, dt, at=over[0])
            over[0] += int(np.prod(shape[1:]))
            assert BASE + 4 * over[0] <= END, name
            return t

        xTl = overlay("xTl", [P, KD, SEQ], F32R)
        wh = overlay("wh", [P, SPLIT, UNIT], F32R)
        wl = overlay("wl", [P, SPLIT, UNIT], F32R)
        hidh_at = over[0]
        hidh = overlay("hidh", [P, 2, 512], F32R)
        hidl = overlay("hidl", [P, 2, 512], F32R)
        pTh = place("pTh", [P, 2, SEQ], F32R, at=hidh_at)
        pTl = place("pTl", [P, 2, SEQ], F32R, at=hidh_at + 1024)
        pth_at = over[0]
        hth = overlay("hth", [P, 2, 512])
        hga = overlay("hga", [P, 512])
        hff = overlay("hff", [P, 512])
        pth = place("pth", [P, 4, 512], at=pth_at)
        ptmp = overlay("ptmp", [P, 512])
        over = [mixers_at]
        hid = overlay("hid", [P, 2, 512])
        xgh = overlay("xgh", [P, KD, P], F32R)
        xgl = overlay("xgl", [P, KD, P], F32R)
        ye = overlay("ye", [P, D])
        pick = overlay("pick", [P, 2, P])
        pickw = overlay("pickw", [P, 2, P])
        spread = overlay("spread", [P, 2, P])
        assert over[0] <= arena_at
        rt = pT[:, 0, 0:KD * 8].rearrange("p (a b) -> p a b", a=KD)

        ident, iota = cst[:, 0:P], cst[:, P:2 * P]
        below, ones = cst[:, 2 * P:3 * P], cst[:, 3 * P:4 * P]
        iota8 = cst[:, 4 * P:4 * P + 8]

        at = [0]

        def cut(n, *dims, reset=None):
            if reset is not None:
                at[0] = reset
            v = arena[:, at[0]:at[0] + n]
            at[0] += n
            if len(dims) == 1:
                return v.rearrange("p (a b) -> p a b", a=dims[0])
            if len(dims) == 2:
                return v.rearrange("p (a b c) -> p a b c", a=dims[0], b=dims[1])
            return v

        gth = cut(16 * SEQ, 16, reset=0)
        qT = cut(4 * SEQ, 4)
        kT = cut(2 * SEQ, 2)
        vt = cut(2 * P, 2)
        uT = cut(4 * SEQ, 4)
        lg = cut(4 * SEQ, 4)
        pr = cut(8 * P, 8)
        aT = cut(4 * SEQ, 4)
        yT = cut(4 * SEQ, 4)
        ga = qT
        sT = lg
        prod = cut(4 * 2 * SEQ, 4)
        vw = cut(4 * 2 * SEQ, 4)
        rot = cut(4 * 2 * SEQ, 4)
        xs = cut(2 * 2 * SEQ, 2)
        mT = rot.rearrange("p a b -> p (a b)").rearrange("p (a b) -> p a b", a=KD)
        mtmp = prod.rearrange("p a b -> p (a b)")[:, 0:2 * SEQ].rearrange("p (a b) -> p a b", a=2)
        assert at[0] <= ARENA
        craw = cut(2 * DEPTH * ST * 32, 2, reset=0)
        relb_sb = cut(HEADS * P, HEADS)
        hot_sb = cut(BIAS_W)
        rows = cut(BIAS_W)

        def sm(i, n=32, j=0):
            return small[:, i, j:j + n]

        (LRE, LIM, LDT, DT, RR, TH, K1, K2, SN, SH, CS, NR, NI, DEN, CRE, CIM) = range(16)
        PWR, PWI = 16, 24
        sm_d, sm_hb = sm(32, 8), sm(33, 8)
        sink = sm(34, 16)
        stat = small[:, 35, 0:12].rearrange("p (a b) -> p a b", a=2)
        mv, veps, rstd, half_neg = sm(35, 2, 12), sm(35, 1, 14), sm(35, 1, 15), sm(35, 1, 16)
        mx, esk, den = sm(36, 4), sm(36, 4, 4), sm(36, 4, 8)
        sm_t = small[:, 37, 0:32]
        lgt = small[:, 38, 0:16].rearrange("p (a b) -> p a b", a=2)
        top = small[:, 38, 16:32].rearrange("p (a b) -> p a b", a=2)
        selm = small[:, 39, 0:16].rearrange("p (a b) -> p a b", a=2)
        comb = small[:, 39, 16:32].rearrange("p (a b) -> p a b", a=2)
        posm = small[:, 34, 16:32].rearrange("p (a b) -> p a b", a=2)
        oh = small[:, 33, 8:24].rearrange("p (a b) -> p a b", a=2)
        topf = small[:, 32, 8:24].rearrange("p (a b) -> p a b", a=2)
        gts = sm(35, 6, 20)
        cnt = sm(36, 2, 12)

        psum = ctx.enter_context(nc.psum_tensor("psum", [P, 8, 512], F32))
        bank = [psum[:, i, :] for i in range(8)]

        def halves(b):
            return bank[b][:, :].rearrange("p (a b) -> p a b", a=2)

        OUT_BANKS = (2, 3, 5, 6)
        HIDDEN_BANKS = ((0, 1), (4, 7))

        landed = [sem(f"unit_landed{i}") for i in range(RING)]
        unit_used, halves_used = sem("unit_used"), sem("unit_halves_used")
        hi_ready, lo_ready = sem("unit_hi_ready"), sem("unit_lo_ready")
        xT_hi, xT_lo, pT_hi, pT_lo = sem("xT_hi_ready"), sem("xT_lo_ready"), sem("pT_hi_ready"), sem("pT_lo_ready")
        rt_hi, rt_lo = sem("router_hi_ready"), sem("router_lo_ready")
        hid_full, hid_hi, hT_lo, xg_lo = sem("hidden_product_ready"), sem("hidden_hi_ready"), sem("hiddenT_lo_ready"), sem("gathered_lo_ready")
        prep_in, const_dma, x_dma, bias_dma = sem("prep_landed"), sem("const_landed"), sem("x_landed"), sem("bias_moved")
        bias_ps, bias_row, bias_out = sem("bias_row_ready"), sem("bias_row_copied"), sem("bias_row_stored")
        pt_dma, ln_dma, rt_dma, out_dma = sem("ple_input_landed"), sem("ln_landed"), sem("router_landed"), sem("out_stored")
        dve_step, pool_step, final_step = sem("vector_step"), sem("pool_step"), sem("vector_final_step")
        exp_in, exp_out = sem("prep_for_scalar"), sem("prep_from_scalar")
        params_ready, phase_ready, phase_used = sem("params_ready"), sem("phase_ready"), sem("phase_used")
        g_full = sem("gemm_group_full")
        g_free = [sem("gemm_bank0_free"), sem("gemm_bank1_free")]
        u_ready, bu_full, bu_free = sem("u_ready"), sem("bu_full"), sem("bu_free")
        rot_ready, rot_used, xs_ready, y_full, y_free = (sem("rotated_back"), sem("rotated_back_used"), sem("states_ready"),
                                                         sem("y_full"), sem("y_free"))
        gelu_in, gelu_th, gelu_ready = sem("gelu_arg_ready"), sem("gelu_tanh_ready"), sem("gelu_ready")
        glu_th, s_ready = sem("glu_tanh_ready"), sem("s_ready")
        qk_ready = sem("qkv_ready")
        sc_full, sc_read = sem("scores_full"), sem("scores_read")
        soft_in, soft_exp, probs = sem("logits_ready"), sem("exp_ready"), sem("probs_ready")
        pt_full, pt_ready, av_full, a_ready = sem("probsT_full"), sem("probsT_ready"), sem("av_full"), sem("a_ready")
        m_ready, o_full, var_ready, rstd_ready = sem("merged_ready"), sem("out_full"), sem("var_ready"), sem("rstd_ready")
        ln_ready, xT_ready, ln_used = sem("ln_ready"), sem("xT_ready"), sem("ln_used")
        pg_full, pg_th, pp_full, res_ready = sem("ple_gate_full"), sem("ple_tanh_ready"), sem("ple_proj_full"), sem("residual_ready")
        h_full, h_th, h_ready, h_used = sem("hidden_full"), sem("hidden_tanh_ready"), sem("hidden_ready"), sem("hidden_used")
        r_full, sel_ready, pos_full, pass_ready = sem("router_full"), sem("selection_ready"), sem("positions_full"), sem("passes_ready")
        pick_ready, x_free = sem("pick_ready"), [sem("slot_bank5_free"), sem("slot_bank6_free")]
        x_full, xg_ready, hT_ready, spread_ready = sem("slot_group_full"), sem("gathered_ready"), sem("hiddenT_ready"), sem("spread_ready")
        ye_full, ye_ready = sem("expert_out_full"), sem("expert_out_ready")

        block = ctx.enter_context(nc.Block())

        def arrived(eng, u):
            eng.wait_ge(landed[u % RING], 16 * (u // RING + 1))

        def split_index(u):
            l = 0 if u < DENSE_UNITS + FFN_UNITS else 1
            return u - PLAIN_UNITS * (l + 1)

        def make_hi(eng, u, laps=0):
            n = split_index(u)
            eng.wait_ge(landed[u % RING], 16 * (u // RING + 1) + laps * 16)
            if n >= SPLIT:
                eng.wait_ge(halves_used, n - SPLIT + 1 + laps * RING)
            eng.activation(wh[:, u % SPLIT, :], ring[:, u % RING, :], ACT.Copy).then_inc(hi_ready, 1)

        def make_lo(eng, u, laps=0):
            eng.wait_ge(hi_ready, split_index(u) + 1 + laps * RING)
            eng.tensor_tensor(wl[:, u % SPLIT, :], ring[:, u % RING, :], wh[:, u % SPLIT, :].bitcast(F32),
                              ALU.subtract).then_inc(lo_ready, 1)

        class Chain:

            def __init__(self, eng, s):
                self.eng, self.sem, self.n, self.base = eng, s, 0, 0

            def link(self, ins):
                ins.then_inc(self.sem, 1)
                self.n += 1
                self.eng.wait_ge(self.sem, self.base + self.n)

        def dense_units(l):
            def cols(w, c, n=256):
                return w.rearrange("(k p) n -> p k n", p=P)[:, :, c:c + n]
            def krows(w, k, n=2):
                return w.rearrange("(k p) n -> p k n", p=P)[:, k:k + n, :]
            wi = w_in[l]
            yield from (cols(wi, c) for c in (768, 1024, 0, 256, 512))
            yield from (cols(wi, c) for c in range(1280, 3328, 256))
            yield cols(w_glu[l], 0, 512)
            yield from (cols(w_ba[l], c, 512) for c in (0, 512))
            yield from (cols(w_bs[l], c, 512) for c in (0, 512))
            yield from (krows(w_out[l], k) for k in range(0, KD, 2))
            yield krows(w_pp[l], 0)
            yield from (krows(w_pg[l], k) for k in range(0, KD, 2))

        @block.sync
        def _(sp):
            sp.dma_start(xT[:], xT_in.rearrange("(k p) n -> p k n", p=P)).then_inc(const_dma, 16)
            sp.dma_start(cst[:], const_in[:, :]).then_inc(const_dma, 16)

            def load(u, src, slot):
                if not isinstance(u, int):
                    sp.wait_ge(lo_ready, u - RING + 1 - PLAIN_UNITS * (1 if not in_moe[0] else 2))
                elif u >= RING:
                    before = u - RING
                    l, i = divmod(before, DENSE_UNITS + FFN_UNITS)
                    if i < PLAIN_UNITS:
                        sp.wait_ge(unit_used, l * PLAIN_UNITS + i + 1)
                    else:
                        sp.wait_ge(lo_ready, split_index(before) + 1)
                a, b = src.shape[-2:]
                sp.dma_start(ring[:, slot, :].rearrange("p (a b) -> p a b", a=a), src).then_inc(landed[slot], 16)

            in_moe = [False]

            def small_loads():
                for dst, src in ((relb_sb[0:BUCKETS + 1], relb), (hot_sb[0:BUCKETS + 1], hot_in),
                                 (craw.rearrange("p a b -> p (a b)"), c_in), (bmat[:].rearrange("p a b c d -> p (a b c d)"), b_in),
                                 (small[:, LRE, :], lre_in), (small[:, LIM, :], lim_in), (small[:, LDT, :], ldt_in),
                                 (sm_d, d_in), (sm_hb, bglu_in), (sink, sinks)):
                    sp.dma_start(dst, src).then_inc(prep_in, 16)

            u = 0
            for l in range(DEPTH):
                for src in dense_units(l):
                    load(u, src, u % RING)
                    u += 1
                    if u == 2:
                        small_loads()
                        sp.dma_start(xa[:], x.rearrange("(b p) d -> p b d", p=P)).then_inc(x_dma, 16)
                if l == 0:
                    gu = w_gu.rearrange("(k p) n -> p k n", p=P)
                    dn = w_dn.rearrange("(k p) n -> p k n", p=P)
                    def hidden(u, i, slot):
                        load(u, gu[:, :, bass.ds(i * 256, 256)], slot)
                        load(u + 1, gu[:, :, bass.ds(DFF + i * 256, 256)], (slot + 1) % RING)
                    def down(u, i, slot):
                        load(u, dn[:, bass.ds(i * 2, 2), :], slot)
                    hidden(u, 0, u % RING)
                    hidden(u + 2, 1, (u + 2) % RING)
                    down(u + 4, 0, (u + 4) % RING)
                    hidden(u + 5, 2, (u + 5) % RING)
                    down(u + 7, 1, (u + 7) % RING)
                    u += 8
                    with sp.Fori(1, FSTEPS // 2) as m:
                        v = u + (m - 1) * 6
                        hidden(v, 2 * m + 1, u % RING)
                        down(v + 2, 2 * m, (u + 2) % RING)
                        hidden(v + 3, 2 * m + 2, (u + 3) % RING)
                        down(v + 5, 2 * m + 1, (u + 5) % RING)
                    u += (FSTEPS // 2 - 1) * 6
                    down(u, FSTEPS - 1, u % RING)
                    u += 1
            assert u == MOE_BASE
            in_moe[0] = True
            sp.wait_ge(unit_used, DEPTH * PLAIN_UNITS)
            sp.wait_ge(pass_ready, 1)
            passes = sp.value_load(npass[0:1, 0:1], min_val=1, max_val=2)
            with sp.Fori(0, passes) as ps:
                with sp.Fori(0, NE) as e:
                    v = MOE_BASE + (ps * NE + e) * EXPERT_UNITS
                    gu = moe_gu.rearrange("(m p) n -> p m n", p=P)
                    dn = moe_dn.rearrange("(m p) n -> p m n", p=P)
                    q = 0
                    for j in range(ESTEPS + 1):
                        if j < ESTEPS:
                            for c in (j * 512, DFE + j * 512):
                                for k in (0, 4):
                                    load(v + q, gu[:, bass.ds(e * KD + k, 4), c:c + 512], (MOE_BASE + q) % RING)
                                    q += 1
                        if j >= 1:
                            for k in (0, 2):
                                load(v + q, dn[:, bass.ds(e * (DFE // P) + (j - 1) * 4 + k, 2), :], (MOE_BASE + q) % RING)
                                q += 1
            for b in range(NB):
                sp.wait_ge(ln_ready, 3 * NB + b + 1)
                sp.dma_start(out.rearrange("(b p) d -> p b d", p=P)[:, b, :], xa[:, b, :]).then_inc(out_dma, 16)
            sp.wait_ge(out_dma, 16 * NB)

        @block.tensor
        def _(pe):
            def slot(u, k):
                return ring[:, u % RING, :].rearrange("p (k n) -> p k n", k=k)

            def weights(u, rows, k, c, n):
                return (w[:, u % SPLIT, :].rearrange("p (k n) -> p k n", k=rows)[:, k, c:c + n] for w in (wh, wl))

            def product(dst, ah, al, u, rows, k, c, n, first, last):
                bh, bl = weights(u, rows, k, c, n)
                pe.matmul(dst, ah, bh, start=first, stop=False, skip_group_check=True)
                pe.matmul(dst, ah, bl, start=False, stop=False, skip_group_check=True)
                return pe.matmul(dst, al, bh, start=False, stop=last, skip_group_check=True)

            def product_by_column(dst, bh, bl, u, rows, k, c, first, last):
                ah, al = weights(u, rows, k, c, P)
                pe.matmul(dst, ah, bh, start=first, stop=False, skip_group_check=True)
                pe.matmul(dst, ah, bl, start=False, stop=False, skip_group_check=True)
                return pe.matmul(dst, al, bh, start=False, stop=last, skip_group_check=True)

            def open_group(g):
                if g >= 2:
                    pe.wait_ge(g_free[g % 2], g // 2)
                return bank[g % 2]

            pe.wait_ge(prep_in, 160)
            for h in range(HEADS):
                if h:
                    pe.wait_ge(bias_row, h)
                pe.matmul(bank[7][:, 0:BIAS_W], relb_sb[0:BUCKETS + 1, h, :], hot_sb[0:BUCKETS + 1, :],
                          start=True, stop=True).then_inc(bias_ps, 1)
            pe.wait_ge(const_dma, 32)

            for l in range(DEPTH):
                U, G = l * (DENSE_UNITS + FFN_UNITS), l * GEMM_GROUPS
                state = {"u": U, "g": G}
                if l:
                    pe.wait_ge(xT_ready, 4)

                def project(kind):
                    u, g = state["u"], state["g"]
                    w = slot(u, KD)
                    arrived(pe, u)
                    b = open_group(g)
                    for t in range(2):
                        for q, m in ((0, HD), (HD, HD)) if kind == "kv" else ((0, P),):
                            for k in range(KD):
                                mm = pe.matmul(b[q:q + m, t * SEQ:(t + 1) * SEQ], w[:, k, t * m:(t + 1) * m], xT[:, k, :],
                                               start=(k == 0), stop=(k == KD - 1))
                    mm.then_inc(g_full, 1)
                    state["g"] += 1
                    if kind == "kv":
                        b = open_group(g + 1)
                        for t in range(NB):
                            for k in range(KD):
                                mm = pe.matmul(b[:, t * P:(t + 1) * P], xT[:, k, t * P:(t + 1) * P], w[:, k, P:2 * P],
                                               start=(k == 0), stop=(k == KD - 1))
                        mm.then_inc(g_full, 1)
                        state["g"] += 1
                    pe.drain().then_inc(unit_used, 1)
                    state["u"] += 1

                def input_states(b):
                    if b == 0:
                        pe.wait_ge(u_ready, 2 * (l + 1))
                        pe.wait_ge(params_ready, 1)
                    if 8 * l + b >= 1:
                        pe.wait_ge(bu_free, 8 * l + b)
                    for t in range(2):
                        i = 2 * b + t
                        q, c = 32 * (i % 4), i // 4
                        for ri in range(2):
                            mm = pe.matmul(bank[2 + t][:, ri * SEQ:(ri + 1) * SEQ], bmat[q:q + 32, l, ri, c, :],
                                           uT[q:q + 32, c, :], start=True, stop=True)
                    mm.then_inc(bu_full, 1)

                def output_states(b):
                    c = b // 2
                    pe.wait_ge(xs_ready, 2 * (8 * l + b + 1))
                    if b % 2 == 0 and 4 * l + c >= 1:
                        pe.wait_ge(y_free, 4 * l + c)
                    for t in range(2):
                        i = 2 * b + t
                        q = 32 * (i % 4)
                        for ri in range(2):
                            mm = pe.matmul(bank[4][q:q + 32, 0:SEQ], cmat[:, ri, l * ST + i, :],
                                           xs[:, ri, t * SEQ:(t + 1) * SEQ], start=(ri == 0), stop=(ri == 1))
                    mm.then_inc(y_full, 1)

                def scores(i):
                    n, kv = i // 2, i % 2
                    if i == 0:
                        pe.wait_ge(qk_ready, 4 * (l + 1))
                    if 4 * l + i >= 1:
                        pe.wait_ge(pt_ready, 4 * l + i)
                    keys = SEQ if n else P
                    for j in range(4):
                        h = 4 * kv + j
                        q = HD * (h % 2)
                        mm = pe.matmul(halves(5 + j % 2)[:, j // 2, SEQ - keys:SEQ], qT[q:q + HD, h // 2, n * P:(n + 1) * P],
                                       kT[q:q + HD, kv, 0:keys], start=True, stop=True)
                    mm.then_inc(sc_full, 1)

                def transpose_probs(i):
                    n = i // 2
                    pe.wait_ge(probs, 4 * l + i + 1)
                    for j in range(4):
                        for s in range(1 - n, 2):
                            mm = pe.transpose(bank[5 + j // 2][:, (2 * (j % 2) + s) * P:(2 * (j % 2) + s + 1) * P],
                                              lg[:, j, s * P:(s + 1) * P], ident)
                    mm.then_inc(pt_full, 1)

                def attend(i):
                    n, kv = i // 2, i % 2
                    pe.wait_ge(pt_ready, 4 * l + i + 1)
                    if 4 * l + i >= 1:
                        pe.wait_ge(a_ready, 4 * l + i)
                    for j in range(4):
                        blocks = range(1 - n, 2)
                        for s in blocks:
                            mm = pe.matmul(bank[7][HD * (j % 2):HD * (j % 2) + HD, (j // 2) * P:(j // 2 + 1) * P],
                                           vt[:, s - 1 + n, kv * HD:(kv + 1) * HD], pr[:, 2 * j + s, :],
                                           start=(s == blocks[0]), stop=(s == 1))
                    mm.then_inc(av_full, 1)

                project("u"), project("u")
                input_states(0)
                project("q"), project("q"), project("kv")
                input_states(1)
                scores(0)
                project("g")
                output_states(0), input_states(2)
                project("g")
                transpose_probs(0), output_states(1), input_states(3)
                project("g")
                attend(0), scores(1)
                project("g")
                output_states(2), input_states(4)
                project("g")
                transpose_probs(1), output_states(3), input_states(5)
                project("g")
                attend(1), scores(2)
                project("g")
                output_states(4), input_states(6)
                project("g")
                transpose_probs(2), output_states(5), input_states(7)
                attend(2), scores(3)
                output_states(6), output_states(7)
                transpose_probs(3), attend(3)

                u, g = state["u"], state["g"]
                arrived(pe, u)
                pe.wait_ge(gelu_ready, l + 1)
                w = slot(u, KA)
                for m in range(4):
                    if m % 2 == 0:
                        b = open_group(g + m // 2)
                    for k in range(KA):
                        mm = pe.matmul(b[:, (m % 2) * SEQ:(m % 2 + 1) * SEQ], w[:, k, m * P:(m + 1) * P], ga[:, k, :],
                                       start=(k == 0), stop=(k == KA - 1))
                    if m % 2:
                        mm.then_inc(g_full, 1)
                pe.drain().then_inc(unit_used, 1)
                u, g = u + 1, g + 2

                pe.wait_ge(a_ready, 4 * (l + 1))
                pe.wait_ge(s_ready, l + 1)
                for i in range(4):
                    arrived(pe, u + i)
                for c in range(KD):
                    b = open_group(g + c)
                    for s, act in ((0, aT), (1, sT)):
                        w = slot(u + 2 * s + c // 4, KA)
                        for k in range(KA):
                            mm = pe.matmul(b[:, s * SEQ:(s + 1) * SEQ], w[:, k, (c % 4) * P:(c % 4 + 1) * P], act[:, k, :],
                                           start=(k == 0), stop=(k == KA - 1))
                    mm.then_inc(g_full, 1)
                pe.drain().then_inc(unit_used, 4)
                u, g = u + 4, g + KD

                def by_token(u, n, banks, act, parts):
                    for i in range(n):
                        arrived(pe, u + i)
                        w = slot(u + i, 2)
                        for k in range(2):
                            for o, b in enumerate(banks):
                                mm = pe.matmul(bank[b][:, :], act[:, 2 * i + k, (o // 2) * P:(o // 2 + 1) * P],
                                               w[:, k, (o % 2) * 512:(o % 2 + 1) * 512],
                                               start=(i == 0 and k == 0), stop=(i == n - 1 and k == 1))
                        if i == n - 1:
                            mm.then_inc(parts, 1)
                            pe.drain().then_inc(unit_used, 1)
                        else:
                            mm.then_inc(unit_used, 1)

                def by_token_halves(u, n, banks, hi, lo, parts):
                    for i in range(n):
                        pe.wait_ge(lo_ready, split_index(u + i) + 1)
                        for k in range(2):
                            for o, b in enumerate(banks):
                                t, c = (o // 2) * P, (o % 2) * 512
                                mm = product(bank[b], hi[:, 2 * i + k, t:t + P], lo[:, 2 * i + k, t:t + P], u + i, 2, k, c, 512,
                                             i == 0 and k == 0, i == n - 1 and k == 1)
                        if i == n - 1:
                            mm.then_inc(parts, 1)
                            pe.drain().then_inc(halves_used, 1)
                        else:
                            mm.then_inc(halves_used, 1)

                pe.wait_ge(m_ready, KD * (l + 1))
                by_token(u, 4, OUT_BANKS, mT, o_full)
                u += 4

                def turn(src, which):
                    nonlocal g
                    for b in range(NB):
                        pe.wait_ge(ln_ready, which * NB + b + 1)
                        for q in range(2):
                            ps = open_group(g)
                            for k in range(4):
                                mm = pe.transpose(ps[:, k * P:(k + 1) * P], src[:, b, (4 * q + k) * P:(4 * q + k + 1) * P], ident)
                            mm.then_inc(g_full, 1)
                            g += 1

                turn(xb, 2 * l)
                for par in range(2):
                    pe.wait_ge(g_free[par], g // 2)
                pe.wait_ge(pT_lo, l + 1)
                by_token_halves(u, 1, (0, 1, 4, 7), pTh, pTl, pp_full)
                pe.wait_ge(xT_lo, 4 * (l + 1))
                by_token_halves(u + 1, 4, OUT_BANKS, xTh, xTl, pg_full)
                u += 5
                pe.wait_ge(res_ready, l + 1)

                if l == 0:
                    def up(s, lap, par, free):
                        if free is not None:
                            pe.wait_ge(h_ready, free)
                        for o in range(2):
                            pe.wait_ge(lo_ready, split_index(s + o) + 1 + lap)
                            for f in range(2):
                                for k in range(KD):
                                    mm = product_by_column(bank[HIDDEN_BANKS[par][o]][:, f * SEQ:(f + 1) * SEQ], xTh[:, k, :], xTl[:, k, :],
                                                           s + o, KD, k, f * P, k == 0, k == KD - 1)
                            if o:
                                mm.then_inc(h_full, 1)
                                pe.drain().then_inc(halves_used, 1)
                            else:
                                mm.then_inc(halves_used, 1)

                    def down(s, lap, par, ready, first=False, last=False):
                        pe.wait_ge(h_ready, ready)
                        pe.wait_ge(lo_ready, split_index(s) + 1 + lap)
                        for k in range(2):
                            for o, b in enumerate(OUT_BANKS):
                                t = k * SEQ + (o // 2) * P
                                mm = product(bank[b], hidh[:, par, t:t + P], hidl[:, par, t:t + P], s, 2, k, (o % 2) * 512, 512,
                                             first and k == 0, last and k == 1)
                        mm.then_inc(h_used, 1)
                        pe.drain().then_inc(halves_used, 1)

                    up(u, 0, 0, None)
                    up(u + 2, 0, 1, None)
                    down(u + 4, 0, 0, 1, first=True)
                    up(u + 5, 0, 0, 1)
                    down(u + 7, 0, 1, 2)
                    u += 8
                    with pe.Fori(1, FSTEPS // 2) as m:
                        lap = (m - 1) * 6
                        up(u, lap, 1, 2 * m)
                        down(u + 2, lap, 0, 2 * m + 1)
                        up(u + 3, lap, 0, 2 * m + 1)
                        down(u + 5, lap, 1, 2 * m + 2)
                    u += (FSTEPS // 2 - 1) * 6
                    down(u, 0, 0, FSTEPS, last=True)
                    pe.nop().then_inc(o_full, 1)
                    u += 1
                    turn(xa, 1)
                    assert g == GEMM_GROUPS

            pe.wait_ge(rt_lo, 1)
            for b in range(NB):
                for k in range(KD):
                    dst, t = bank[0][:, b * 8:b * 8 + 8], slice(b * P, (b + 1) * P)
                    pe.matmul(dst, xTh[:, k, t], rth[:, k, :], start=(k == 0), stop=False)
                    pe.matmul(dst, xTh[:, k, t], rtl[:, k, :], start=False, stop=False)
                    mm = pe.matmul(dst, xTl[:, k, t], rth[:, k, :], start=False, stop=(k == KD - 1))
            mm.then_inc(r_full, 1)
            pe.wait_ge(sel_ready, 1)
            pe.matmul(bank[1][:, 0:8], below, selm[:, 0, :], start=True, stop=True)
            pe.matmul(bank[1][:, 8:16], below, selm[:, 1, :], start=True, stop=False)
            pe.matmul(bank[1][:, 8:16], ones, selm[:, 0, :], start=False, stop=True)
            pe.matmul(bank[1][:, 16:24], ones, selm[:, 0, :], start=True, stop=False)
            pe.matmul(bank[1][:, 16:24], ones, selm[:, 1, :], start=False, stop=True).then_inc(pos_full, 1)

            pe.wait_ge(pass_ready, 1)
            passes = pe.value_load(npass[0:1, 0:1], min_val=1, max_val=2)
            with pe.Fori(0, passes) as ps:
                with pe.Fori(0, NE) as e:
                    it = ps * NE + e
                    lap = it * EXPERT_UNITS

                    def slot_group(x):
                        pe.wait_ge(x_free[x % 2], it * (SLOT_GROUPS // 2) + x // 2 + 1)
                        return bank[5 + x % 2]

                    def take(q):
                        pe.wait_ge(lo_ready, split_index(MOE_BASE + q) + 1 + lap)
                        return MOE_BASE + q

                    pe.wait_ge(pick_ready, it + 1)
                    ps5 = slot_group(0)
                    for b in range(NB):
                        mm = pe.transpose(ps5[:, b * P:(b + 1) * P], pickw[:, b, :], ident)
                    mm.then_inc(x_full, 1)
                    for x in (1, 2):
                        psx = slot_group(x)
                        for k in range(4):
                            for b in range(NB):
                                dc = 4 * (x - 1) + k
                                mm = pe.matmul(psx[:, k * P:(k + 1) * P], xb[:, b, dc * P:(dc + 1) * P], pick[:, b, :],
                                               start=(b == 0), stop=(b == NB - 1))
                        mm.then_inc(x_full, 1)
                    pe.wait_ge(xg_lo, 2 * it + 2)

                    def project(j, o, q):
                        for kk in (0, 4):
                            v = take(q)
                            for k in range(4):
                                mm = product(bank[HIDDEN_BANKS[j % 2][o]], xgh[:, kk + k, :], xgl[:, kk + k, :], v, 4, k, 0, 512,
                                             kk + k == 0, kk + k == KD - 1)
                            if o and kk:
                                mm.then_inc(h_full, 1)
                                pe.drain().then_inc(halves_used, 1)
                            else:
                                mm.then_inc(halves_used, 1)
                            q += 1

                    def turn_hidden(i):
                        pe.wait_ge(h_ready, FSTEPS + it * ESTEPS + i + 1)
                        psx = slot_group(3 + i)
                        for k in range(4):
                            mm = pe.transpose(psx[:, k * P:(k + 1) * P], hid[:, i % 2, k * P:(k + 1) * P], ident)
                        mm.then_inc(x_full, 1)

                    def down(i, q):
                        pe.wait_ge(hT_lo, it * ESTEPS + i + 1)
                        for kk in range(2):
                            v = take(q)
                            for k in range(2):
                                c = 2 * kk + k
                                for o in range(2):
                                    mm = product(bank[2 + o], hidh[:, i % 2, c * P:(c + 1) * P], hidl[:, i % 2, c * P:(c + 1) * P],
                                                 v, 2, k, o * 512, 512, i == 0 and c == 0, i == ESTEPS - 1 and c == 3)
                            if i == ESTEPS - 1 and kk:
                                mm.then_inc(ye_full, 1)
                                pe.drain().then_inc(halves_used, 1)
                            else:
                                mm.then_inc(halves_used, 1)
                            q += 1

                    project(0, 0, 0), project(0, 1, 2)
                    for j in range(1, ESTEPS):
                        project(j, 0, 6 * j - 2)
                        turn_hidden(j - 1)
                        project(j, 1, 6 * j)
                        down(j - 1, 6 * j + 2)
                    turn_hidden(ESTEPS - 1)
                    down(ESTEPS - 1, 6 * ESTEPS - 2)
                    pe.wait_ge(ye_ready, it + 1)
                    pe.wait_ge(spread_ready, it + 1)
                    for o in range(4):
                        psx = slot_group(10 + o)
                        pe.matmul(psx[:, :], spread[:, o // 2, :], ye[:, (o % 2) * 512:(o % 2 + 1) * 512],
                                  start=True, stop=True).then_inc(x_full, 1)

        @block.scalar
        def _(act):
            act.wait_ge(exp_in, 1)
            act.activation(sm(SN), sm(TH), ACT.Sin).then_inc(exp_out, 1)
            act.activation(sm(SH), sm(TH), ACT.Sin, scale=0.5).then_inc(exp_out, 1)
            for h in range(HEADS):
                act.wait_ge(bias_ps, h + 1)
                if h:
                    act.wait_ge(bias_out, 16 * h)
                act.activation(rows, bank[7][:, 0:BIAS_W], ACT.Copy).then_inc(bias_row, 1)
            for l in range(DEPTH):
                G = l * GEMM_GROUPS
                gate = [0]

                def group(g):
                    act.wait_ge(g_full, G + g + 1)
                    return halves(g % 2)

                def gates():
                    g = 6 + gate[0]
                    act.activation(gth[:, 2 * gate[0]:2 * gate[0] + 2, :], group(g), ACT.Tanh, scale=0.5).then_inc(g_free[g % 2], 1)
                    gate[0] += 1

                def exp_probs(i):
                    act.wait_ge(soft_in, 2 * (4 * l + i + 1))
                    act.activation(esk, esk, ACT.Exp).then_inc(soft_exp, 1)
                    act.activation(lg[:, :, (1 - i // 2) * P:], lg[:, :, (1 - i // 2) * P:], ACT.Exp).then_inc(soft_exp, 1)

                def copy_probs(i):
                    act.wait_ge(pt_full, 4 * l + i + 1)
                    if 4 * l + i >= 1:
                        act.wait_ge(av_full, 4 * l + i)
                    n = i // 2
                    for j in range(2):
                        src = bank[5 + j][:, :].rearrange("p (h s n) -> p h s n", h=2, s=2)
                        dst = pr[:, 4 * j:4 * j + 4, :].rearrange("p (h s) n -> p h s n", h=2)
                        ins = act.activation(dst[:, :, 1 - n:, :], src[:, :, 1 - n:, :], ACT.Copy)
                    ins.then_inc(pt_ready, 1)

                def copy_attended(i):
                    n, kv = i // 2, i % 2
                    act.wait_ge(av_full, 4 * l + i + 1)
                    src = bank[7][:, 0:2 * P].rearrange("p (c n) -> p c n", c=2)
                    act.activation(aT[:, 2 * kv:2 * kv + 2, n * P:(n + 1) * P], src, ACT.Copy).then_inc(a_ready, 1)

                for g in (2, 3):
                    src = group(g)
                    act.activation(qT[:, 2 * (g - 2):2 * (g - 1), :], src, ACT.Copy, scale=HD ** -0.5).then_inc(qk_ready, 1)
                    act.wait_ge(qk_ready, 4 * l + g - 1)
                    act.nop().then_inc(g_free[g % 2], 1)
                act.activation(kT, group(4), ACT.Copy).then_inc(qk_ready, 1)
                act.wait_ge(qk_ready, 4 * l + 3)
                act.nop().then_inc(g_free[0], 1)
                act.wait_ge(g_full, G + 6)
                act.activation(vt, bank[1][:, 0:2 * P].rearrange("p (a b) -> p a b", a=2), ACT.Copy).then_inc(qk_ready, 1)
                act.wait_ge(qk_ready, 4 * l + 4)
                act.nop().then_inc(g_free[1], 1)
                gates(), exp_probs(0), gates(), copy_probs(0), gates(), copy_attended(0), gates(), exp_probs(1), gates()
                copy_probs(1), gates(), copy_attended(1), gates(), exp_probs(2), gates(), copy_probs(2), copy_attended(2)
                exp_probs(3), copy_probs(3), copy_attended(3)

                act.wait_ge(gelu_in, l + 1)
                act.activation(ga, ga, ACT.Tanh, scale=GELU_C).then_inc(gelu_th, 1)
                for m in range(4):
                    g = 14 + m // 2
                    act.wait_ge(g_full, G + g + 1)
                    ins = act.activation(uT[:, m, :], bank[g % 2][:, (m % 2) * SEQ:(m % 2 + 1) * SEQ], ACT.Tanh,
                                         bias=sm_hb[:, 4 * l + m:4 * l + m + 1], scale=0.5)
                    ins.then_inc(glu_th, 1)
                    if m % 2:
                        act.wait_ge(glu_th, 4 * l + m + 1)
                        act.nop().then_inc(g_free[g % 2], 1)

                def turned(g0, dst, done, n0, next_reader=None):
                    for i in range(4):
                        g = G + g0 + i
                        act.wait_ge(g_full, g + 1)
                        b, q = i // 2, i % 2
                        src = bank[g % 2][:, :].rearrange("p (k n) -> p k n", k=4)
                        act.activation(dst[:, 4 * q:4 * q + 4, b * P:(b + 1) * P], src, ACT.Copy).then_inc(done, 1)
                        if done is xT_ready:
                            act.wait_ge(done, n0 + i + 1)
                            act.nop().then_inc(g_free[g % 2], 1)

                U = l * (DENSE_UNITS + FFN_UNITS) + PLAIN_UNITS
                act.wait_ge(o_full, 1 if l == 0 else 3)
                act.wait_ge(pt_dma, 16 * (l + 1))
                act.activation(pTh[:], pT[:], ACT.Copy).then_inc(pT_hi, 1)
                for u in range(U, U + 3):
                    make_hi(act, u)
                turned(24, xTh, xT_hi, 4 * l)
                make_hi(act, U + 3), make_hi(act, U + 4)
                if l == 0:
                    make_hi(act, U + 5)
                    act.wait_ge(pg_full, 1)
                else:
                    act.wait_ge(rt_dma, 16)
                    act.activation(rth[:], rt, ACT.Copy).then_inc(rt_hi, 1)
                    act.wait_ge(pg_full, 2)
                for o, b in enumerate(OUT_BANKS):
                    ins = act.activation(pth[:, o, :], bank[b][:, :], ACT.Tanh, scale=0.5)
                ins.then_inc(pg_th, 1)
                if l == 0:
                    def hidden_tanh(i, par):
                        act.wait_ge(h_full, i)
                        if not isinstance(i, int) or i >= 3:
                            act.wait_ge(h_ready, i - 2)
                        act.activation(hth[:, par, :], bank[HIDDEN_BANKS[par][0]][:, :], ACT.Tanh, scale=0.5).then_inc(h_th, 1)

                    def hidden_hi(i, par):
                        act.wait_ge(hid_full, i)
                        if not isinstance(i, int) or i >= 3:
                            act.wait_ge(h_used, i - 2)
                        act.activation(hidh[:, par, :], hff[:], ACT.Copy).then_inc(hid_hi, 1)

                    make_hi(act, U + 6)
                    act.wait_ge(res_ready, 1)
                    V = U + 7
                    make_hi(act, V), hidden_tanh(1, 0), make_hi(act, V + 1), hidden_hi(1, 0), make_hi(act, V + 2)
                    make_hi(act, V + 3), hidden_tanh(2, 1), make_hi(act, V + 4), hidden_hi(2, 1), make_hi(act, V + 5)
                    V += 6
                    with act.Fori(1, FSTEPS // 2) as m:
                        laps = m - 1
                        for t in range(2):
                            make_hi(act, V + 3 * t, laps)
                            hidden_tanh(2 * m + 1 + t, t)
                            make_hi(act, V + 3 * t + 1, laps)
                            hidden_hi(2 * m + 1 + t, t)
                            make_hi(act, V + 3 * t + 2, laps)
                    V += 6 * (FSTEPS // 2 - 1)
                    hidden_tanh(FSTEPS, 0), hidden_hi(FSTEPS, 0), make_hi(act, V)
                    assert V + 1 == DENSE_UNITS + FFN_UNITS
                    turned(28, xT, xT_ready, 0)

            act.wait_ge(soft_in, 2 * 4 * DEPTH + 1)
            act.activation(gts[:, 0:2], gts[:, 0:2], ACT.Exp).then_inc(soft_exp, 1)
            act.wait_ge(pass_ready, 1)
            passes = act.value_load(npass[0:1, 0:1], min_val=1, max_val=2)
            with act.Fori(0, passes) as ps:
                with act.Fori(0, NE) as e:
                    it = ps * NE + e
                    F = it * ESTEPS

                    def slot_group(x):
                        act.wait_ge(x_full, it * SLOT_GROUPS + x + 1)
                        return bank[5 + x % 2]

                    laps = it * (EXPERT_UNITS // RING)
                    for k in range(SPLIT):
                        make_hi(act, MOE_BASE + k, laps)
                    act.activation(spread[:], slot_group(0)[:, 0:2 * P].rearrange("p (a b) -> p a b", a=2),
                                   ACT.Copy).then_inc(spread_ready, 1)
                    act.wait_ge(spread_ready, it + 1)
                    act.nop().then_inc(x_free[0], 1)
                    for x in (1, 2):
                        act.activation(xgh[:, 4 * (x - 1):4 * x, :], slot_group(x)[:, :].rearrange("p (a b) -> p a b", a=4),
                                       ACT.Copy).then_inc(xg_ready, 1)
                    laps = it * (EXPERT_UNITS // RING)
                    for j in range(ESTEPS + 1):
                        q = MOE_BASE + max(6 * j - 2, 0)
                        if j < ESTEPS:
                            for k in range(0 if j else SPLIT, 4):
                                make_hi(act, q + k, laps)
                            q += 4
                        if j >= 1:
                            i = j - 1
                            act.activation(hidh[:, i % 2, :], slot_group(3 + i)[:, :], ACT.Copy).then_inc(hT_ready, 1)
                            make_hi(act, q, laps), make_hi(act, q + 1, laps)
                        if j < ESTEPS:
                            act.wait_ge(h_full, FSTEPS + F + j + 1)
                            act.wait_ge(h_ready, FSTEPS + F + max(j - 1, 0))
                            act.activation(hth[:, j % 2, :], bank[HIDDEN_BANKS[j % 2][0]][:, :], ACT.Tanh, scale=0.5).then_inc(h_th, 1)
                    act.wait_ge(ye_full, it + 1)
                    act.activation(ye[:, 0:512], bank[2][:, :], ACT.Copy)
                    act.activation(ye[:, 512:1024], bank[3][:, :], ACT.Copy).then_inc(ye_ready, 1)

        @block.gpsimd
        def _(pool):
            c = Chain(pool, pool_step)
            c.link(pool.memset(half_neg, -0.5))

            def load_ln(n):
                if n:
                    pool.wait_ge(ln_used, 2 * n)
                pool.dma_start(lnp[:], ln_in[n]).then_inc(ln_dma, 16)

            pool.dma_start(pT[:], pT_in[0].rearrange("(k p) n -> p k n", p=P)).then_inc(pt_dma, 16)
            load_ln(0)
            for h in range(HEADS):
                pool.wait_ge(bias_row, h + 1)
                pool.dma_start(bias_scratch[h, 0:P, :], rows).then_inc(bias_out, 16)
            pool.wait_ge(bias_out, 16 * HEADS)
            for h in range(HEADS):
                flat = bias_scratch[h].rearrange("q m -> (q m)")
                band = flat[P - 1:P - 1 + P * (BIAS_W - 1)].rearrange("(q m) -> q m", m=BIAS_W - 1)[:, 0:SEQ]
                pool.dma_start(bias[:, h, :], band).then_inc(bias_dma, 16)
            pool.wait_ge(params_ready, 1)

            def phases(l, ch):
                n = 4 * l + ch
                if n >= 2:
                    pool.wait_ge(phase_used, 2 * (n - 1))
                co, si = phase[:, n % 2, 0], phase[:, n % 2, 1]
                pool.memset(co[:, :, 0:1], 1.0)
                c.link(pool.memset(si[:, :, 0:1], 0.0))
                for j in range(8):
                    k = 1 << j
                    s0 = l * ST + 4 * ch
                    wr = small[:, PWR + j, s0:s0 + 4].unsqueeze(2).to_broadcast([P, 4, k])
                    wi = small[:, PWI + j, s0:s0 + 4].unsqueeze(2).to_broadcast([P, 4, k])
                    t1, t2 = ptm[:, 0, 0:4 * k].rearrange("p (a b) -> p a b", a=4), ptm[:, 1, 0:4 * k].rearrange("p (a b) -> p a b", a=4)
                    pool.tensor_tensor(co[:, :, k:2 * k], co[:, :, 0:k], wr, ALU.mult)
                    pool.tensor_tensor(t1, si[:, :, 0:k], wi, ALU.mult)
                    pool.tensor_tensor(si[:, :, k:2 * k], si[:, :, 0:k], wr, ALU.mult)
                    c.link(pool.tensor_tensor(t2, co[:, :, 0:k], wi, ALU.mult))
                    pool.tensor_tensor(co[:, :, k:2 * k], co[:, :, k:2 * k], t1, ALU.subtract)
                    c.link(pool.tensor_tensor(si[:, :, k:2 * k], si[:, :, k:2 * k], t2, ALU.add))
                pool.nop().then_inc(phase_ready, 1)

            def states(l, b):
                n = 8 * l + b
                pool.wait_ge(rot_ready, n + 1)
                if n:
                    pool.wait_ge(y_full, n)
                pool.tensor_tensor(xs[:, 0, :], rot[:, 0, :], rot[:, 1, :], ALU.subtract).then_inc(xs_ready, 1)
                pool.tensor_tensor(xs[:, 1, :], rot[:, 2, :], rot[:, 3, :], ALU.add).then_inc(xs_ready, 1)

            def root(n):
                for b in range(NB):
                    pool.wait_ge(var_ready, NB * n + b + 1)
                    pool.tensor_tensor(rstd, veps, half_neg, ALU.pow).then_inc(rstd_ready, 1)

            phases(0, 0), phases(0, 1)
            for l in range(DEPTH):
                for b in range(8):
                    states(l, b)
                    if b % 2 and b // 2 + 2 < 4:
                        phases(l, b // 2 + 2)
                root(2 * l)
                load_ln(2 * l + 1)
                if l == 0:
                    phases(1, 0), phases(1, 1)
                    root(1)
                    load_ln(2)
                    pool.wait_ge(pT_lo, 1)
                    pool.dma_start(pT[:], pT_in[1].rearrange("(k p) n -> p k n", p=P)).then_inc(pt_dma, 16)
                else:
                    pool.wait_ge(pT_lo, 2)
                    pool.dma_start(rt, router.rearrange("(k p) n -> p k n", p=P)).then_inc(rt_dma, 16)
            pool.wait_ge(pass_ready, 1)
            root(3)

        @block.vector
        def _(dve):
            c = Chain(dve, dve_step)
            link = c.link

            def exp_accurate(dst, src, t1, t2, t3):
                link(dve.tensor_scalar(t1, src, -87.0, 88.0, ALU.max, ALU.min))
                link(dve.tensor_scalar(t2, t1, 1.4426950408889634, 12582912.0, ALU.mult, ALU.add))
                link(dve.tensor_scalar(t2, t2, -12582912.0, None, ALU.add))
                link(dve.scalar_tensor_tensor(out=t1, in0=t2, scalar=-0.693359375, in1=t1, op0=ALU.mult, op1=ALU.add))
                link(dve.scalar_tensor_tensor(out=t1, in0=t2, scalar=2.12194440e-4, in1=t1, op0=ALU.mult, op1=ALU.add))
                link(dve.tensor_scalar(t3, t1, 1 / 5040.0, 1 / 720.0, ALU.mult, ALU.add))
                for co in (1 / 120.0, 1 / 24.0, 1 / 6.0, 0.5, 1.0, 1.0):
                    link(dve.tensor_tensor(t3, t3, t1, ALU.mult))
                    link(dve.tensor_scalar(t3, t3, co, None, ALU.add))
                link(dve.tensor_scalar(t2, t2, 127.0, 8388608.0, ALU.add, ALU.mult))
                link(dve.tensor_copy(t1.bitcast(I32), t2))
                link(dve.tensor_tensor(dst, t3, t1, ALU.mult))

            dve.wait_ge(prep_in, 160)
            exp_accurate(sm(DT), sm(LDT), sm(NR), sm(NI), sm(DEN))
            link(dve.tensor_tensor(sm(K1), sm(LRE), sm(DT), ALU.mult))
            exp_accurate(sm(RR), sm(K1), sm(NR), sm(NI), sm(DEN))
            link(dve.tensor_tensor(sm(TH), sm(LIM), sm(DT), ALU.mult))
            link(dve.tensor_scalar(sm(K1), sm(TH), 0.15915494309189535, 12582912.0, ALU.mult, ALU.add))
            link(dve.tensor_scalar(sm(K1), sm(K1), -12582912.0, None, ALU.add))
            for part in (6.28125, 1.9340515136718750e-3, 1.2556659146e-06):
                link(dve.scalar_tensor_tensor(out=sm(TH), in0=sm(K1), scalar=-part, in1=sm(TH), op0=ALU.mult, op1=ALU.add))
            dve.tensor_scalar(sm(TH), sm(TH), -3.1415925, 3.1415925, ALU.max, ALU.min).then_inc(exp_in, 1)
            dve.wait_ge(exp_out, 2)
            link(dve.tensor_tensor(sm(CS), sm(SH), sm(SH), ALU.mult))
            link(dve.tensor_scalar(sm(CS), sm(CS), -2.0, 1.0, ALU.mult, ALU.add))
            link(dve.tensor_tensor(sm(NR), sm(RR), sm(CS), ALU.mult))
            link(dve.tensor_scalar(sm(NR), sm(NR), -1.0, None, ALU.add))
            link(dve.tensor_tensor(sm(NI), sm(RR), sm(SN), ALU.mult))
            link(dve.tensor_tensor(sm(DEN), sm(LRE), sm(LRE), ALU.mult))
            link(dve.tensor_tensor(sm(K1), sm(LIM), sm(LIM), ALU.mult))
            link(dve.tensor_tensor(sm(DEN), sm(DEN), sm(K1), ALU.add))
            link(dve.reciprocal(sm(DEN), sm(DEN)))
            link(dve.tensor_tensor(sm(CRE), sm(NR), sm(LRE), ALU.mult))
            link(dve.tensor_tensor(sm(K1), sm(NI), sm(LIM), ALU.mult))
            link(dve.tensor_tensor(sm(CRE), sm(CRE), sm(K1), ALU.add))
            link(dve.tensor_tensor(sm(CRE), sm(CRE), sm(DEN), ALU.mult))
            link(dve.tensor_tensor(sm(CIM), sm(NI), sm(LRE), ALU.mult))
            link(dve.tensor_tensor(sm(K1), sm(NR), sm(LIM), ALU.mult))
            link(dve.tensor_tensor(sm(CIM), sm(CIM), sm(K1), ALU.subtract))
            link(dve.tensor_tensor(sm(CIM), sm(CIM), sm(DEN), ALU.mult))
            dve.tensor_copy(sm(PWR), sm(CS))
            link(dve.tensor_copy(sm(PWI), sm(SN)))
            for j in range(7):
                a, b = sm(PWR + j), sm(PWI + j)
                dve.tensor_tensor(sm(K1), a, a, ALU.mult)
                dve.tensor_tensor(sm(K2), b, b, ALU.mult)
                link(dve.tensor_tensor(sm(PWI + j + 1), a, b, ALU.mult))
                dve.tensor_tensor(sm(PWR + j + 1), sm(K1), sm(K2), ALU.subtract)
                link(dve.tensor_scalar(sm(PWI + j + 1), sm(PWI + j + 1), 2.0, None, ALU.mult))
            wide = [P, DEPTH * ST, 32]
            cr, ci = (craw[:, r, :].rearrange("p (a b) -> p a b", b=32) for r in range(2))
            kr, ki = (sm(r).unsqueeze(2).to_broadcast(wide) for r in (CRE, CIM))
            sc = prod.rearrange("p a b -> p (a b)")[:, 0:DEPTH * ST * 32].rearrange("p (a b) -> p a b", b=32)
            link(dve.tensor_tensor(cmat[:, 0], cr, kr, ALU.mult))
            link(dve.tensor_tensor(sc, ci, ki, ALU.mult))
            link(dve.tensor_tensor(cmat[:, 0], cmat[:, 0], sc, ALU.subtract))
            link(dve.tensor_tensor(cmat[:, 1], cr, ki, ALU.mult))
            link(dve.tensor_tensor(sc, ci, kr, ALU.mult))
            link(dve.tensor_tensor(cmat[:, 1], cmat[:, 1], sc, ALU.add))
            link(dve.tensor_scalar(cmat[:, 1], cmat[:, 1], -1.0, None, ALU.mult))
            dve.tensor_scalar(sm_hb, sm_hb, 0.5, None, ALU.mult).then_inc(params_ready, 1)
            dve.wait_ge(x_dma, 16)

            def layer_norm(n, src, dst):
                for b in range(NB):
                    for h in range(2):
                        link(dve.bn_stats(stat[:, h, :], src[:, b, h * 512:(h + 1) * 512]))
                    link(dve.bn_aggr(mv, stat))
                    dve.tensor_scalar(veps, mv[:, 1:2], EPS, None, ALU.add).then_inc(var_ready, 1)
                    dve.wait_ge(rstd_ready, NB * n + b + 1)
                    link(dve.tensor_scalar(dst[:, b, :], src[:, b, :], mv[:, 0:1], rstd, ALU.subtract, ALU.mult))
                    if b == 0:
                        dve.wait_ge(ln_dma, 16 * (n + 1))
                    link(dve.tensor_tensor(dst[:, b, :], dst[:, b, :], lnp[:, 0, :], ALU.mult))
                    dve.tensor_tensor(dst[:, b, :], dst[:, b, :], lnp[:, 1, :], ALU.add).then_inc(ln_ready, 1)
                    dve.wait_ge(ln_ready, NB * n + b + 1)
                    dve.nop().then_inc(ln_used, 1)

            for l in range(DEPTH):
                G = l * GEMM_GROUPS
                for g in range(2):
                    dve.wait_ge(g_full, G + g + 1)
                    dve.tensor_copy(uT[:, 2 * g:2 * g + 2, :], halves(g)).then_inc(u_ready, 1)
                    dve.wait_ge(u_ready, 2 * l + g + 1)
                    dve.nop().then_inc(g_free[g], 1)

                def scan_states(b):
                    ch, n = b // 2, 8 * l + b
                    pn = 4 * l + ch
                    if b % 2 == 0:
                        dve.wait_ge(phase_ready, pn + 1)
                    t0 = 2 * (b % 2)
                    co = phase[:, pn % 2, 0, t0:t0 + 2, :].rearrange("p a b -> p (a b)")
                    si = phase[:, pn % 2, 1, t0:t0 + 2, :].rearrange("p a b -> p (a b)")
                    dve.wait_ge(bu_full, n + 1)
                    re, im = psum[:, 2:4, 0:SEQ], psum[:, 2:4, SEQ:2 * SEQ]
                    p4 = prod.rearrange("p a (t n) -> p a t n", t=2)
                    c4, s4 = phase[:, pn % 2, 0, t0:t0 + 2, :], phase[:, pn % 2, 1, t0:t0 + 2, :]
                    dve.tensor_tensor(p4[:, 0], re, c4, ALU.mult)
                    dve.tensor_tensor(p4[:, 1], im, s4, ALU.mult)
                    dve.tensor_tensor(p4[:, 2], im, c4, ALU.mult)
                    dve.tensor_tensor(p4[:, 3], re, s4, ALU.mult).then_inc(bu_free, 1)
                    dve.wait_ge(bu_free, n + 1)
                    dve.tensor_tensor(vw[:, 0, :], prod[:, 0, :], prod[:, 1, :], ALU.add)
                    link(dve.tensor_tensor(vw[:, 1, :], prod[:, 2, :], prod[:, 3, :], ALU.subtract))
                    for t in range(2):
                        i = l * ST + 2 * b + t
                        for ri in range(2):
                            ins = dve.tensor_tensor_scan(vw[:, 2 + ri, t * SEQ:(t + 1) * SEQ], small[:, RR, i:i + 1].to_broadcast([P, SEQ]),
                                                         vw[:, ri, t * SEQ:(t + 1) * SEQ], 0.0, ALU.mult, ALU.add)
                    link(ins)
                    if n:
                        dve.wait_ge(xs_ready, 2 * n)
                    dve.tensor_tensor(rot[:, 0, :], vw[:, 2, :], co, ALU.mult)
                    dve.tensor_tensor(rot[:, 1, :], vw[:, 3, :], si, ALU.mult)
                    dve.tensor_tensor(rot[:, 2, :], vw[:, 2, :], si, ALU.mult)
                    dve.tensor_tensor(rot[:, 3, :], vw[:, 3, :], co, ALU.mult).then_inc(rot_ready, 1)
                    dve.wait_ge(rot_ready, n + 1)
                    dve.nop().then_inc(phase_used, 1)

                def logits(i):
                    n, kv = i // 2, i % 2
                    o = (1 - n) * P
                    dve.wait_ge(sc_full, 4 * l + i + 1)
                    if l == 0 and i == 0:
                        dve.wait_ge(bias_dma, 16 * HEADS)
                    if 4 * l + i >= 1:
                        dve.wait_ge(pt_full, 4 * l + i)
                    for j in range(2):
                        h = 4 * kv + j
                        ins = dve.tensor_tensor(lg[:, j:4:2, o:], halves(5 + j)[:, :, o:], bias[:, h:h + 3:2, o:], ALU.add)
                    link(ins)
                    link(dve.tensor_reduce(mx, lg[:, :, o:], AX, ALU.max))
                    sk = sink[:, 8 * l + 4 * kv:8 * l + 4 * kv + 4]
                    link(dve.tensor_tensor(mx, mx, sk, ALU.max))
                    dve.tensor_tensor(esk, sk, mx, ALU.subtract).then_inc(soft_in, 1)
                    dve.tensor_tensor(lg[:, :, o:], lg[:, :, o:], mx.unsqueeze(2).to_broadcast([P, 4, SEQ - o]),
                                      ALU.subtract).then_inc(soft_in, 1)

                def normalise(i):
                    o = (1 - i // 2) * P
                    dve.wait_ge(soft_exp, 2 * (4 * l + i + 1))
                    link(dve.tensor_reduce(den, lg[:, :, o:], AX, ALU.add))
                    link(dve.tensor_tensor(den, den, esk, ALU.add))
                    link(dve.reciprocal(den, den))
                    dve.tensor_tensor(lg[:, :, o:], lg[:, :, o:], den.unsqueeze(2).to_broadcast([P, 4, SEQ - o]),
                                      ALU.mult).then_inc(probs, 1)

                def skip_term(ch):
                    dve.wait_ge(y_full, 8 * l + 2 * ch + 2)
                    link(dve.scalar_tensor_tensor(out=yT[:, ch, :], in0=uT[:, ch, :], scalar=sm_d[:, 4 * l + ch:4 * l + ch + 1],
                                                  in1=bank[4][:, 0:SEQ], op0=ALU.mult, op1=ALU.add))
                    dve.nop().then_inc(y_free, 1)

                scan_states(0), scan_states(1), logits(0), scan_states(2), normalise(0), scan_states(3)
                logits(1), skip_term(0), scan_states(4), normalise(1), scan_states(5), skip_term(1)
                logits(2), scan_states(6), normalise(2), scan_states(7), skip_term(2)
                logits(3), normalise(3), skip_term(3)

                link(dve.tensor_tensor(ga, yT, yT, ALU.mult))
                link(dve.tensor_scalar(ga, ga, 0.044715, 1.0, ALU.mult, ALU.add))
                dve.tensor_tensor(ga, ga, yT, ALU.mult).then_inc(gelu_in, 1)
                dve.wait_ge(gelu_th, l + 1)
                link(dve.scalar_tensor_tensor(out=ga, in0=ga, scalar=1.0, in1=yT, op0=ALU.add, op1=ALU.mult))
                dve.tensor_scalar(ga, ga, 0.5, None, ALU.mult).then_inc(gelu_ready, 1)
                dve.wait_ge(gelu_ready, l + 1)
                link(dve.tensor_scalar(yT, ga, 0.5, None, ALU.mult))
                dve.wait_ge(glu_th, 4 * (l + 1))
                dve.scalar_tensor_tensor(out=sT, in0=uT, scalar=1.0, in1=yT, op0=ALU.add, op1=ALU.mult).then_inc(s_ready, 1)

                for k in range(KD):
                    g = 16 + k
                    dve.wait_ge(g_full, G + g + 1)
                    a = bank[g % 2]
                    link(dve.scalar_tensor_tensor(out=mtmp[:, 0, :], in0=gth[:, k, :], scalar=1.0, in1=a[:, 0:SEQ],
                                                  op0=ALU.add, op1=ALU.mult))
                    link(dve.scalar_tensor_tensor(out=mtmp[:, 1, :], in0=gth[:, KD + k, :], scalar=1.0, in1=a[:, SEQ:2 * SEQ],
                                                  op0=ALU.add, op1=ALU.mult))
                    dve.nop().then_inc(g_free[g % 2], 1)
                    dve.tensor_tensor(mT[:, k, :], mtmp[:, 0, :], mtmp[:, 1, :], ALU.add).then_inc(m_ready, 1)
                    dve.wait_ge(m_ready, KD * l + k + 1)

                link(dve.tensor_scalar(xa[:], xa[:], ALPHA, None, ALU.mult))
                dve.wait_ge(o_full, (1 if l == 0 else 3))
                for o, b in enumerate(OUT_BANKS):
                    part = xa[:, o // 2, (o % 2) * 512:(o % 2 + 1) * 512]
                    link(dve.scalar_tensor_tensor(out=part, in0=bank[b][:, :], scalar=0.5, in1=part, op0=ALU.mult, op1=ALU.add))
                U = l * (DENSE_UNITS + FFN_UNITS) + PLAIN_UNITS
                dve.wait_ge(pT_hi, l + 1)
                dve.tensor_tensor(pTl[:], pT[:], pTh[:].bitcast(F32), ALU.subtract).then_inc(pT_lo, 1)
                make_lo(dve, U)
                layer_norm(2 * l, xa, xb)
                for i in range(4):
                    g = G + 24 + i
                    dve.wait_ge(xT_hi, 4 * l + i + 1)
                    b, q = i // 2, i % 2
                    part = (slice(None), slice(4 * q, 4 * q + 4), slice(b * P, (b + 1) * P))
                    dve.tensor_tensor(xTl[part], bank[g % 2][:, :].rearrange("p (k n) -> p k n", k=4), xTh[part].bitcast(F32),
                                      ALU.subtract).then_inc(xT_lo, 1)
                    dve.wait_ge(xT_lo, 4 * l + i + 1)
                    dve.nop().then_inc(g_free[g % 2], 1)
                for u in range(U + 1, U + 5):
                    make_lo(dve, u)

                link(dve.tensor_scalar(xa[:], xb[:], ALPHA, None, ALU.mult))
                dve.wait_ge(pp_full, l + 1)
                dve.wait_ge(pg_th, l + 1)
                for o, b in enumerate((0, 1, 4, 7)):
                    part = xa[:, o // 2, (o % 2) * 512:(o % 2 + 1) * 512]
                    link(dve.scalar_tensor_tensor(out=ptmp[:], in0=pth[:, o, :], scalar=1.0, in1=bank[b][:, :], op0=ALU.add, op1=ALU.mult))
                    link(dve.scalar_tensor_tensor(out=part, in0=ptmp[:], scalar=0.5, in1=part, op0=ALU.mult, op1=ALU.add))
                dve.nop().then_inc(res_ready, 1)

                if l == 1:
                    dve.wait_ge(rt_hi, 1)
                    dve.tensor_tensor(rtl[:], rt, rth[:].bitcast(F32), ALU.subtract).then_inc(rt_lo, 1)

                def hidden(i, par):
                    dve.wait_ge(h_th, i)
                    link(dve.scalar_tensor_tensor(out=hga[:], in0=hth[:, par, :], scalar=1.0, in1=bank[HIDDEN_BANKS[par][0]][:, :],
                                                  op0=ALU.add, op1=ALU.mult))
                    dve.scalar_tensor_tensor(out=hff[:], in0=hga[:], scalar=0.5, in1=bank[HIDDEN_BANKS[par][1]][:, :],
                                             op0=ALU.mult, op1=ALU.mult).then_inc(hid_full, 1)

                def hidden_lo(i, par):
                    dve.wait_ge(hid_hi, i)
                    dve.tensor_tensor(hidl[:, par, :], hff[:], hidh[:, par, :].bitcast(F32), ALU.subtract).then_inc(h_ready, 1)
                    dve.wait_ge(h_ready, i)

                if l == 0:
                    make_lo(dve, U + 5), make_lo(dve, U + 6)
                    V = U + 7
                    make_lo(dve, V), hidden(1, 0), make_lo(dve, V + 1), hidden_lo(1, 0), make_lo(dve, V + 2)
                    make_lo(dve, V + 3), hidden(2, 1), make_lo(dve, V + 4), hidden_lo(2, 1), make_lo(dve, V + 5)
                    V += 6
                    n0 = c.n
                    with dve.Fori(1, FSTEPS // 2) as m:
                        c.base, laps = (m - 1) * 2, m - 1
                        for t in range(2):
                            make_lo(dve, V + 3 * t, laps)
                            hidden(2 * m + 1 + t, t)
                            make_lo(dve, V + 3 * t + 1, laps)
                            hidden_lo(2 * m + 1 + t, t)
                            make_lo(dve, V + 3 * t + 2, laps)
                    c.base, c.n = 0, n0 + 2 * (FSTEPS // 2 - 1)
                    V += 6 * (FSTEPS // 2 - 1)
                    hidden(FSTEPS, 0), hidden_lo(FSTEPS, 0), make_lo(dve, V)
                    dve.wait_ge(o_full, 2)
                    for o, b in enumerate(OUT_BANKS):
                        part = xa[:, o // 2, (o % 2) * 512:(o % 2 + 1) * 512]
                        link(dve.tensor_tensor(part, bank[b][:, :], part, ALU.add))
                    layer_norm(1, xa, xa)

            dve.wait_ge(r_full, 1)
            link(dve.tensor_copy(lgt, bank[0][:, 0:16].rearrange("p (a b) -> p a b", a=2)))
            for b in range(NB):
                link(dve.max(top[:, b, :], lgt[:, b, :]))
                link(dve.max_index(topi[:, b, :], top[:, b, :], lgt[:, b, :]))
            link(dve.tensor_copy(topf, topi[:]))
            dve.tensor_tensor(gts[:, 0:2], top[:, :, 1], top[:, :, 0], ALU.subtract).then_inc(soft_in, 1)
            dve.wait_ge(soft_exp, 8 * DEPTH + 1)
            link(dve.tensor_scalar(gts[:, 2:4], gts[:, 0:2], 1.0, None, ALU.add))
            link(dve.reciprocal(gts[:, 2:4], gts[:, 2:4]))
            link(dve.tensor_tensor(gts[:, 4:6], gts[:, 0:2], gts[:, 2:4], ALU.mult))
            for b in range(NB):
                link(dve.tensor_scalar(comb[:, b, :], iota8, topf[:, b, 0:1], gts[:, 2 + b:3 + b], ALU.is_equal, ALU.mult))
                link(dve.tensor_scalar(oh[:, b, :], iota8, topf[:, b, 1:2], gts[:, 4 + b:5 + b], ALU.is_equal, ALU.mult))
                link(dve.tensor_tensor(comb[:, b, :], comb[:, b, :], oh[:, b, :], ALU.add))
                link(dve.tensor_scalar(oh[:, b, :], iota8, topf[:, b, 0:1], None, ALU.is_equal))
                link(dve.tensor_scalar(selm[:, b, :], iota8, topf[:, b, 1:2], None, ALU.is_equal))
                link(dve.tensor_tensor(selm[:, b, :], selm[:, b, :], oh[:, b, :], ALU.add))
            dve.nop().then_inc(sel_ready, 1)
            dve.wait_ge(pos_full, 1)
            link(dve.tensor_tensor(posm, bank[1][:, 0:16].rearrange("p (a b) -> p a b", a=2), selm, ALU.mult))
            link(dve.tensor_scalar(oh, selm, 4096.0, -4096.0, ALU.mult, ALU.add))
            link(dve.tensor_tensor(posm, posm, oh, ALU.add))
            link(dve.tensor_reduce(cnt[:, 0:1], bank[1][:, 16:24], AX, ALU.max))
            link(dve.tensor_scalar(cnt[:, 0:1], cnt[:, 0:1], float(P), 1.0, ALU.is_gt, ALU.add))
            for s in x_free:
                dve.nop().then_inc(s, 1)
            dve.tensor_copy(npass[0:1, 0:1], cnt[0:1, 0:1]).then_inc(pass_ready, 1)
            dve.wait_ge(pass_ready, 1)
            passes = dve.value_load(npass[0:1, 0:1], min_val=1, max_val=2)
            n0 = c.n
            per_expert = ESTEPS + 4
            per_pass = NE * per_expert + 1
            with dve.Fori(0, passes) as ps:
                with dve.Fori(0, NE) as e:
                    it = ps * NE + e
                    c.n, c.base = n0, ps * per_pass + e * per_expert
                    F = FSTEPS + it * ESTEPS
                    for b in range(NB):
                        dve.tensor_scalar(pick[:, b, :], iota, posm[:, b, bass.ds(e, 1)], None, ALU.is_equal)
                        ins = dve.tensor_scalar(pickw[:, b, :], iota, posm[:, b, bass.ds(e, 1)], comb[:, b, bass.ds(e, 1)],
                                                ALU.is_equal, ALU.mult)
                    ins.then_inc(pick_ready, 1)
                    laps = it * (EXPERT_UNITS // RING)
                    make_lo(dve, MOE_BASE, laps)
                    for x in (1, 2):
                        dve.wait_ge(xg_ready, it * 2 + x)
                        dve.tensor_tensor(xgl[:, 4 * (x - 1):4 * x, :], bank[5 + x % 2][:, :].rearrange("p (a b) -> p a b", a=4),
                                          xgh[:, 4 * (x - 1):4 * x, :].bitcast(F32), ALU.subtract).then_inc(xg_lo, 1)
                        dve.wait_ge(xg_lo, it * 2 + x)
                        dve.nop().then_inc(x_free[x % 2], 1)
                    laps = it * (EXPERT_UNITS // RING)
                    for j in range(ESTEPS + 1):
                        q = MOE_BASE + max(6 * j - 2, 0)
                        if j >= 1:
                            i = j - 1
                            dve.wait_ge(h_th, F + i + 1)
                            link(dve.scalar_tensor_tensor(out=hga[:], in0=hth[:, i % 2, :], scalar=1.0, in1=bank[HIDDEN_BANKS[i % 2][0]][:, :],
                                                          op0=ALU.add, op1=ALU.mult))
                            dve.scalar_tensor_tensor(out=hid[:, i % 2, :], in0=hga[:], scalar=0.5, in1=bank[HIDDEN_BANKS[i % 2][1]][:, :],
                                                     op0=ALU.mult, op1=ALU.mult).then_inc(h_ready, 1)
                        if j < ESTEPS:
                            for k in range(0 if j else 1, 4):
                                make_lo(dve, q + k, laps)
                            q += 4
                        if j >= 1:
                            x = 3 + i
                            dve.wait_ge(hT_ready, it * ESTEPS + i + 1)
                            dve.tensor_tensor(hidl[:, i % 2, :], bank[5 + x % 2][:, :], hidh[:, i % 2, :].bitcast(F32),
                                              ALU.subtract).then_inc(hT_lo, 1)
                            dve.wait_ge(hT_lo, it * ESTEPS + i + 1)
                            dve.nop().then_inc(x_free[x % 2], 1)
                            make_lo(dve, q, laps), make_lo(dve, q + 1, laps)
                    for o in range(4):
                        x = 10 + o
                        dve.wait_ge(x_full, it * SLOT_GROUPS + x + 1)
                        part = xa[:, o // 2, (o % 2) * 512:(o % 2 + 1) * 512]
                        link(dve.tensor_tensor(part, bank[5 + x % 2][:, :], part, ALU.add))
                        dve.nop().then_inc(x_free[x % 2], 1)
                c.n, c.base = n0 + NE * per_expert, ps * per_pass
                link(dve.tensor_scalar(posm, posm, -float(P), None, ALU.add))
            c.sem, c.n, c.base = final_step, 0, 0
            layer_norm(3, xa, xa)


def kernel(**inputs):
    import concourse.bacc as bacc
    from concourse.bass_utils import run_bass_kernel_spmd

    a = {k: np.asarray(v) for k, v in inputs.items()}
    con, hot = constants()

    def pairs(v):
        return np.ascontiguousarray(v.reshape(DEPTH, ST, 2 * SST).transpose(2, 0, 1)).reshape(P, DEPTH * ST)

    relb = np.ones((BUCKETS + 1, HEADS, P), np.float32)
    relb[:BUCKETS] = a["rel_bias"][:, :, None]
    bm = np.zeros((4, 2, SCH, DEPTH, 2, 4, 2, SST), np.float32)
    cm = np.zeros((2, SST, 2, DEPTH, ST, 2, SCH), np.float32)
    for r, (bn, cn) in enumerate((("ssm_b_re", "ssm_c_re"), ("ssm_b_im", "ssm_c_im"))):
        b = a[bn].reshape(DEPTH, 4, 4, 2, SST, SCH)
        c = a[cn].reshape(DEPTH, ST, 2, SCH, SST)
        for par in range(2):
            bm[:, par, :, :, r, :, par, :] = b[:, :, :, par].transpose(2, 4, 0, 1, 3)
            cm[par, :, r, :, :, par, :] = c[:, :, par].transpose(3, 0, 1, 2)

    def by_channel(v):
        return np.ascontiguousarray(v.reshape(DEPTH, 4, P).transpose(2, 0, 1)).reshape(P, DEPTH * 4)

    ln = np.stack([np.stack([a[g][l], a[b][l]]) for l in range(DEPTH) for g, b in (("ln1_g", "ln1_b"), ("ln2_g", "ln2_b"))])
    arrays = {
        "x": a["x"].reshape(SEQ, D),
        "xT": np.ascontiguousarray(a["x"].reshape(SEQ, D).T),
        "pT": np.ascontiguousarray(a["p"].reshape(DEPTH, SEQ, PLE).transpose(0, 2, 1)),
        "relb": relb, "hot": hot, "const": con,
        "sinks": np.ascontiguousarray(np.broadcast_to(a["attn_sinks"].reshape(1, DEPTH * HEADS), (P, DEPTH * HEADS))),
        "lre": pairs(a["ssm_lambda_re"]), "lim": pairs(a["ssm_lambda_im"]),
        "ldt": pairs(np.repeat(a["ssm_log_dt"][:, :, None], SST, axis=2)),
        "b": bm.reshape(P, -1), "c": cm.reshape(P, -1),
        "d": by_channel(a["ssm_d"]), "bglu": by_channel(a["b_glu"]),
        "w_in": a["w_in"], "w_glu": a["w_glu"], "w_ba": a["w_branch_attn"], "w_bs": a["w_branch_ssm"], "w_out": a["w_out"],
        "ln": np.ascontiguousarray(np.broadcast_to(ln[:, None], (2 * DEPTH, P, 2, D))),
        "w_gu": a["ffn_w_gate_up"][0], "w_dn": a["ffn_w_down"][0], "router": a["moe_router"][0],
        "moe_gu": a["moe_w_gate_up"].reshape(NE * D, 2 * DFE), "moe_dn": a["moe_w_down"].reshape(NE * DFE, D),
        "w_pp": a["ple_w_proj"], "w_pg": a["ple_w_gate"],
    }
    nc = bacc.Bacc("TRN2", target_bir_lowering=False, num_devices=1)
    args, feed = [], {}
    for name, v in arrays.items():
        feed[f"in_{name}"] = v
        args.append(nc.dram_tensor(f"in_{name}", v.shape, F32, kind="ExternalInput").ap())
    scratch = nc.dram_tensor("bias_scratch", (HEADS, P + 1, BIAS_W), F32, kind="Internal").ap()
    out = nc.dram_tensor("out", (SEQ, D), F32, kind="ExternalOutput").ap()
    program(nc, *args, scratch, out)
    r = run_bass_kernel_spmd(nc, [feed], core_ids=[0])
    return r.results[0]["out"].reshape(1, SEQ, D)
```

```python
from contextlib import ExitStack

import numpy as np

import concourse.bass as bass
from concourse import mybir

F32 = mybir.dt.float32
F32R = mybir.dt.float32r
I32 = mybir.dt.int32
U32 = mybir.dt.uint32
ALU = mybir.AluOpType
ACT = mybir.ActivationFunctionType
AX = mybir.AxisListType.X

P = 128
D = 1024
SEQ = 256
DEPTH = 2
KD = D // P
NB = SEQ // P
HEADS, HD, BUCKETS = 8, 64, 32
AW = 512
KA = AW // P
SG, SCH, SST = 32, 16, 64
ST = SG * SST // P
DFF, DFE, NE, PLE = 2816, 3584, 8, 256
ALPHA = (2 * DEPTH) ** 0.25
EPS = 1e-5
NEG = -1e30
UNIT = 2048
RING = 6
SPLIT = 3
FSTEPS = DFF // 256
ESTEPS = DFE // 512
PLAIN_UNITS = 22
DENSE_UNITS = 27
FFN_UNITS = 3 * FSTEPS
EXPERT_UNITS = 6 * ESTEPS
MOE_BASE = 2 * DENSE_UNITS + FFN_UNITS
GEMM_GROUPS = 28
SLOT_GROUPS = 12
EARLY = 2
GELU_C = 0.7978845608028654
BIAS_W = 3 * P


def constants():
    import math
    c = np.zeros((P, 4 * P + 8), np.float32)
    c[:, 0:P] = np.eye(P)
    c[:, P:2 * P] = np.arange(P)[None, :]
    c[:, 2 * P:3 * P] = np.arange(P)[:, None] < np.arange(P)[None, :]
    c[:, 3 * P:4 * P] = 1.0
    c[:, 4 * P:] = np.arange(8)[None, :]
    hot = np.zeros((BUCKETS + 1, BIAS_W), np.float32)
    for m in range(BIAS_W):
        dist = 2 * P - 1 - m
        if not 0 <= dist < P:
            hot[BUCKETS, m] = NEG
            continue
        half = BUCKETS // 2
        large = half + int(np.float32(np.log(np.float32(max(dist, 1)) / np.float32(half)))
                           / np.float32(math.log(128 / half)) * np.float32(BUCKETS - half))
        hot[dist if dist < half else min(large, BUCKETS - 1), m] = 1.0
    return c, hot


def program(nc, x, xT_in, pT_in, relb, hot_in, const_in, sinks, lre_in, lim_in, ldt_in, b_in, c_in,
            d_in, bglu_in, w_in, w_glu, w_ba, w_bs, w_out, ln_in, w_gu, w_dn, router, moe_gu, moe_dn,
            w_pp, w_pg, bias_scratch, out):
    ctx = ExitStack()
    with ctx:
        BASE, END = 16512, 229344
        top = [0]

        def place(name, shape, dt=F32, at=None):
            n = int(np.prod(shape[1:]))
            if at is None:
                at = top[0]
                top[0] += -(-n // 8) * 8
                assert BASE + 4 * top[0] <= END, (name, top[0])
            return nc.alloc_sbuf_tensor_at(name, shape, dt, offset=BASE + 4 * at)

        def sem(name):
            return ctx.enter_context(nc.semaphore(name))

        ring = place("ring", [P, RING, UNIT])
        xa = place("xa", [P, NB, D])
        xb = place("xb", [P, NB, D])
        lnp = place("lnp", [P, 2, D])
        cst = place("cst", [P, 4 * P + 8])
        small = place("small", [P, 40, 32])
        pT = place("pT", [P, 2, SEQ])
        xT_at = top[0]
        xT = place("xT", [P, KD, SEQ])
        rth, rtl = place("rth", [P, KD, 8], F32R), place("rtl", [P, KD, 8], F32R)
        npass = place("npass", [1, 8], I32)
        posm = place("posm", [P, NB, 2 * NE])
        comb = place("comb", [P, NB, 2 * NE])
        mixers_at = top[0]
        bias = place("bias", [P, HEADS, SEQ])
        phase = place("phase", [P, 2, 2, 4, SEQ])
        bmat = place("bmat", [P, DEPTH, 2, 4, P])
        cmat = place("cmat", [P, 2, DEPTH * ST, 32])
        ptm_at = top[0]
        ptm = place("ptm", [P, 2, 512])
        arena_at = top[0]
        ARENA = (END - BASE) // 4 - arena_at
        arena = place("arena", [P, ARENA // 8 * 8])
        xTh = place("xTh", [P, KD, SEQ], F32R, at=xT_at)
        over = [arena_at]

        def overlay(name, shape, dt=F32):
            t = place(name, shape, dt, at=over[0])
            over[0] += int(np.prod(shape[1:]))
            assert BASE + 4 * over[0] <= END, name
            return t

        xTl = overlay("xTl", [P, KD, SEQ], F32R)
        wh = overlay("wh", [P, SPLIT, UNIT], F32R)
        wl = overlay("wl", [P, SPLIT, UNIT], F32R)
        hidh_at = over[0]
        hidh = overlay("hidh", [P, 2, 512], F32R)
        hidl = overlay("hidl", [P, 2, 512], F32R)
        pTh = place("pTh", [P, 2, SEQ], F32R, at=hidh_at)
        pTl = place("pTl", [P, 2, SEQ], F32R, at=ptm_at)
        pth_at = over[0]
        hth = overlay("hth", [P, 2, 512])
        hga = overlay("hga", [P, 512])
        hff = overlay("hff", [P, 512])
        pth = place("pth", [P, 4, 512], at=pth_at)
        over = [mixers_at]
        hid = overlay("hid", [P, 2, 512])
        xgh = overlay("xgh", [P, KD, P], F32R)
        xgl = overlay("xgl", [P, KD, P], F32R)
        ye = overlay("ye", [P, D])
        pick = overlay("pick", [P, 2, P])
        pickw = overlay("pickw", [P, 2, P])
        spread = overlay("spread", [P, 2, P])
        rl = overlay("rl", [NE, SEQ])
        topi = overlay("topi", [P, NB, 8], U32)
        assert over[0] <= arena_at
        rt = pT[:, 0, 0:KD * 8].rearrange("p (a b) -> p a b", a=KD)

        ident, iota = cst[:, 0:P], cst[:, P:2 * P]
        below, ones = cst[:, 2 * P:3 * P], cst[:, 3 * P:4 * P]
        iota8 = cst[:, 4 * P:4 * P + 8]

        at = [0]

        def cut(n, *dims, reset=None):
            if reset is not None:
                at[0] = reset
            v = arena[:, at[0]:at[0] + n]
            at[0] += n
            if len(dims) == 1:
                return v.rearrange("p (a b) -> p a b", a=dims[0])
            if len(dims) == 2:
                return v.rearrange("p (a b c) -> p a b c", a=dims[0], b=dims[1])
            return v

        gth = cut(16 * SEQ, 16, reset=0)
        qT = cut(4 * SEQ, 4)
        kT = cut(2 * SEQ, 2)
        vt = cut(2 * P, 2)
        uT = cut(4 * SEQ, 4)
        PROBS_AT = at[0]
        lg = cut(4 * SEQ, 4)
        pr = cut(8 * P, 8)
        aT = cut(4 * SEQ, 4)
        assert at[0] - PROBS_AT >= HEADS * BIAS_W
        yT = cut(4 * SEQ, 4)
        prod = cut(4 * 2 * SEQ, 4)
        vw = cut(4 * 2 * SEQ, 4)
        rot = cut(4 * 2 * SEQ, 4)
        ga, sT = (prod[:, 2 * i:2 * i + 2, :].rearrange("p a (t n) -> p (a t) n", t=2) for i in range(2))
        xs = cut(2 * 2 * SEQ, 2)
        mT = rot.rearrange("p a b -> p (a b)").rearrange("p (a b) -> p a b", a=KD)
        mtmp = prod.rearrange("p a b -> p (a b)")[:, 0:2 * SEQ].rearrange("p (a b) -> p a b", a=2)
        assert at[0] <= ARENA
        craw = cut(2 * DEPTH * ST * 32, 2, reset=0)
        relb_sb = cut(HEADS * P, HEADS)
        hot_sb = cut(BIAS_W)
        rows = arena[:, PROBS_AT:PROBS_AT + HEADS * BIAS_W].rearrange("p (h m) -> p h m", h=HEADS)

        def sm(i, n=32, j=0):
            return small[:, i, j:j + n]

        (LRE, LIM, LDT, DT, RR, TH, K1, K2, SN, SH, CS, NR, NI, DEN, CRE, CIM) = range(16)
        PWR, PWI = 16, 24
        sm_d, sm_hb = sm(32, 8), sm(33, 8)
        sink = sm(34, 16)
        stat = small[:, 35, 0:12].rearrange("p (a b) -> p a b", a=2)
        mv, veps, rstd, half_neg = sm(35, 2, 12), sm(35, 1, 14), sm(35, 1, 15), sm(35, 1, 16)
        mx, esk, den, neg_mx = sm(36, 4), sm(36, 4, 4), sm(36, 4, 8), sm(36, 4, 16)
        sm_t = small[:, 37, 0:32]
        lgt = small[:, 38, 0:16].rearrange("p (a b) -> p a b", a=2)
        top = small[:, 38, 16:32].rearrange("p (a b) -> p a b", a=2)
        selm = small[:, 39, 0:16].rearrange("p (a b) -> p a b", a=2)
        oh = small[:, 33, 8:24].rearrange("p (a b) -> p a b", a=2)
        topf = small[:, 32, 8:24].rearrange("p (a b) -> p a b", a=2)
        gts = sm(35, 6, 20)
        cnt = sm(36, 2, 12)

        psum = ctx.enter_context(nc.psum_tensor("psum", [P, 8, 512], F32))
        bank = [psum[:, i, :] for i in range(8)]

        def halves(b):
            return bank[b][:, :].rearrange("p (a b) -> p a b", a=2)

        OUT_BANKS = (2, 3, 5, 6)
        HIDDEN_BANKS = ((0, 1), (4, 7))

        landed = [sem(f"unit_landed{i}") for i in range(RING)]
        unit_used, halves_used = sem("unit_used"), sem("unit_halves_used")
        hi_ready, lo_ready = sem("unit_hi_ready"), sem("unit_lo_ready")
        xT_hi, xT_lo, pT_hi, pT_lo = sem("xT_hi_ready"), sem("xT_lo_ready"), sem("pT_hi_ready"), sem("pT_lo_ready")
        rt_hi, rt_lo = sem("router_hi_ready"), sem("router_lo_ready")
        hid_full, hid_hi, hT_lo, xg_lo = sem("hidden_product_ready"), sem("hidden_hi_ready"), sem("hiddenT_lo_ready"), sem("gathered_lo_ready")
        prep_in, const_dma, x_dma, bias_dma = sem("prep_landed"), sem("const_landed"), sem("x_landed"), sem("bias_moved")
        angle_dma, table_dma, xT_dma = sem("state_parameters_landed"), sem("bias_tables_landed"), sem("transposed_input_landed")
        powers_ready, bias_banks = sem("powers_ready"), (7, 6, 5, 4)
        bias_ps, bias_row, bias_out = sem("bias_row_ready"), sem("bias_row_copied"), sem("bias_row_stored")
        pt_dma, ln_dma, rt_dma, out_dma = sem("ple_input_landed"), sem("ln_landed"), sem("router_landed"), sem("out_stored")
        dve_step, pool_step, final_step = sem("vector_step"), sem("pool_step"), sem("vector_final_step")
        exp_in, exp_out = sem("prep_for_scalar"), sem("prep_from_scalar")
        params_ready, phase_ready, phase_used = sem("params_ready"), sem("phase_ready"), sem("phase_used")
        g_full = sem("gemm_group_full")
        g_free = [sem("gemm_bank0_free"), sem("gemm_bank1_free")]
        u_ready, bu_full, bu_free = sem("u_ready"), sem("bu_full"), sem("bu_free")
        rot_ready, rot_used, xs_ready, y_full, y_free = (sem("rotated_back"), sem("rotated_back_used"), sem("states_ready"),
                                                         sem("y_full"), sem("y_free"))
        gelu_in, gelu_th, gelu_ready = sem("gelu_arg_ready"), sem("gelu_tanh_ready"), sem("gelu_ready")
        glu_th, s_ready = sem("glu_tanh_ready"), sem("s_ready")
        qk_ready = sem("qkv_ready")
        sc_full, sc_read = sem("scores_full"), sem("scores_read")
        soft_in, soft_exp, probs = sem("logits_ready"), sem("exp_ready"), sem("probs_ready")
        pt_full, pt_ready, av_full, a_ready = sem("probsT_full"), sem("probsT_ready"), sem("av_full"), sem("a_ready")
        m_ready, o_full, var_ready, rstd_ready = sem("merged_ready"), sem("out_full"), sem("var_ready"), sem("rstd_ready")
        ln_ready, xT_ready, ln_used = sem("ln_ready"), sem("xT_ready"), sem("ln_used")
        rl_copied = sem("router_logits_copied")
        t_full, pp_read = sem("normed_turned"), sem("ple_proj_read")
        pg_full, pg_th, pp_full, res_ready = sem("ple_gate_full"), sem("ple_tanh_ready"), sem("ple_proj_full"), sem("residual_ready")
        h_full, h_th, h_ready, h_used = sem("hidden_full"), sem("hidden_tanh_ready"), sem("hidden_ready"), sem("hidden_used")
        routed = sem("router_banks_read")
        r_full, sel_ready, pos_full, pass_ready = sem("router_full"), sem("selection_ready"), sem("positions_full"), sem("passes_ready")
        pick_ready, x_free = sem("pick_ready"), [sem("slot_bank5_free"), sem("slot_bank6_free")]
        x_full, xg_ready, hT_ready, spread_ready = sem("slot_group_full"), sem("gathered_ready"), sem("hiddenT_ready"), sem("spread_ready")
        spread_full, outer_added = sem("spread_out_full"), sem("expert_out_added")
        ye_full, ye_ready = sem("expert_out_full"), sem("expert_out_ready")

        block = ctx.enter_context(nc.Block())

        def arrived(eng, u):
            eng.wait_ge(landed[u % RING], 16 * (u // RING + 1))

        FIRST = (("g", 0), ("u", 0), ("g", 1))
        STEPS = (("u", 1), ("d", 0)) + tuple(x for j in range(2, ESTEPS) for x in (("g", j), ("u", j), ("d", j - 1)))
        AHEAD = (("g", 0), ("u", 0), ("d", ESTEPS - 1), ("g", 1))
        EXPERT_BASE = MOE_BASE + 2 * len(FIRST)
        order = {x: EXPERT_BASE + 2 * n for n, x in enumerate(STEPS)}
        order_ahead = {x: EXPERT_BASE + 2 * (len(STEPS) + n) for n, x in enumerate(AHEAD)}
        order_first = {x: MOE_BASE + 2 * n for n, x in enumerate(FIRST)}
        order_last = dict(order) | {("d", ESTEPS - 1): EXPERT_BASE + 2 * len(STEPS)}
        assert 2 * (len(STEPS) + len(AHEAD)) == EXPERT_UNITS and EXPERT_BASE % RING == MOE_BASE % RING

        def split_index(u):
            l = 0 if u < DENSE_UNITS + FFN_UNITS else 1
            return u - PLAIN_UNITS * (l + 1)

        def make_hi(eng, u, laps=0):
            n = split_index(u)
            eng.wait_ge(landed[u % RING], 16 * (u // RING + 1) + laps * 16)
            if n >= SPLIT:
                eng.wait_ge(halves_used, n - SPLIT + 1 + laps * RING)
            eng.activation(wh[:, u % SPLIT, :], ring[:, u % RING, :], ACT.Copy).then_inc(hi_ready, 1)

        def make_lo(eng, u, laps=0):
            eng.wait_ge(hi_ready, split_index(u) + 1 + laps * RING)
            eng.tensor_tensor(wl[:, u % SPLIT, :], ring[:, u % RING, :], wh[:, u % SPLIT, :].bitcast(F32),
                              ALU.subtract).then_inc(lo_ready, 1)

        class Chain:

            def __init__(self, eng, s):
                self.eng, self.sem, self.n, self.base = eng, s, 0, 0

            def link(self, ins):
                ins.then_inc(self.sem, 1)
                self.n += 1
                self.eng.wait_ge(self.sem, self.base + self.n)

        def phases(eng, link, tmp, l, ch):
            n = 4 * l + ch
            co, si = phase[:, n % 2, 0], phase[:, n % 2, 1]
            eng.memset(co[:, :, 0:1], 1.0)
            link(eng.memset(si[:, :, 0:1], 0.0))
            for j in range(8):
                k = 1 << j
                s0 = l * ST + 4 * ch
                wr = small[:, PWR + j, s0:s0 + 4].unsqueeze(2).to_broadcast([P, 4, k])
                wi = small[:, PWI + j, s0:s0 + 4].unsqueeze(2).to_broadcast([P, 4, k])
                t1, t2 = (tmp[:, i, 0:4 * k].rearrange("p (a b) -> p a b", a=4) for i in range(2))
                eng.tensor_tensor(co[:, :, k:2 * k], co[:, :, 0:k], wr, ALU.mult)
                eng.tensor_tensor(t1, si[:, :, 0:k], wi, ALU.mult)
                eng.tensor_tensor(si[:, :, k:2 * k], si[:, :, 0:k], wr, ALU.mult)
                link(eng.tensor_tensor(t2, co[:, :, 0:k], wi, ALU.mult))
                eng.tensor_tensor(co[:, :, k:2 * k], co[:, :, k:2 * k], t1, ALU.subtract)
                link(eng.tensor_tensor(si[:, :, k:2 * k], si[:, :, k:2 * k], t2, ALU.add))

        def states(eng, l, b):
            n = 8 * l + b
            eng.wait_ge(rot_ready, n + 1)
            if n:
                eng.wait_ge(y_full, n)
            eng.tensor_tensor(xs[:, 0, :], rot[:, 0, :], rot[:, 1, :], ALU.subtract).then_inc(xs_ready, 1)
            eng.tensor_tensor(xs[:, 1, :], rot[:, 2, :], rot[:, 3, :], ALU.add).then_inc(xs_ready, 1)

        def vector_states(b):
            return 2 <= b <= 5

        def dense_units(l):
            def cols(w, c, n=256):
                return w.rearrange("(k p) n -> p k n", p=P)[:, :, c:c + n]
            def krows(w, k, n=2):
                return w.rearrange("(k p) n -> p k n", p=P)[:, k:k + n, :]
            wi = w_in[l]
            yield from (cols(wi, c) for c in (768, 1024, 0, 256, 512))
            yield from (cols(wi, c) for c in range(1280, 3072, 256))
            yield cols(w_glu[l], 0, 512)
            yield cols(wi, 3072)
            yield from (cols(w_ba[l], c, 512) for c in (0, 512))
            yield from (cols(w_bs[l], c, 512) for c in (0, 512))
            yield from (krows(w_out[l], k) for k in range(0, KD, 2))
            yield krows(w_pp[l], 0)
            yield from (krows(w_pg[l], k) for k in range(0, KD, 2))

        @block.sync
        def _(sp):
            for row, src in ((LDT, ldt_in), (LIM, lim_in), (LRE, lre_in)):
                sp.dma_start(small[:, row, :], src).then_inc(angle_dma, 16)
            sp.dma_start(xT[:], xT_in.rearrange("(k p) n -> p k n", p=P)).then_inc(xT_dma, 16)

            def load(u, src, slot):
                if not isinstance(u, int):
                    sp.wait_ge(lo_ready, u - RING + 1 - PLAIN_UNITS * (1 if not in_moe[0] else 2))
                elif u >= RING:
                    before = u - RING
                    l, i = divmod(before, DENSE_UNITS + FFN_UNITS)
                    if i < PLAIN_UNITS:
                        sp.wait_ge(unit_used, l * PLAIN_UNITS + i + 1)
                    else:
                        sp.wait_ge(lo_ready, split_index(before) + 1)
                a, b = src.shape[-2:]
                sp.dma_start(ring[:, slot, :].rearrange("p (a b) -> p a b", a=a), src).then_inc(landed[slot], 16)

            in_moe = [False]

            def small_loads():
                for dst, src in ((bmat[:].rearrange("p a b c d -> p (a b c d)"), b_in), (craw.rearrange("p a b -> p (a b)"), c_in),
                                 (sm_d, d_in), (sm_hb, bglu_in), (sink, sinks)):
                    sp.dma_start(dst, src).then_inc(prep_in, 16)
                sp.dma_start(cst[:], const_in[:, :]).then_inc(const_dma, 16)

            def skew_bias():
                sp.wait_ge(bias_row, HEADS)
                sp.dma_start(bias_scratch[:, 0:P, :].rearrange("h q m -> q h m"), rows).then_inc(bias_out, 16)
                sp.wait_ge(bias_out, 16)
                flat = bias_scratch.rearrange("h q m -> h (q m)")[:, P - 1:P - 1 + P * (BIAS_W - 1)]
                sp.dma_start(bias[:], flat.rearrange("h (q m) -> q h m", m=BIAS_W - 1)[:, :, 0:SEQ]).then_inc(bias_dma, 16)

            u = 0
            for l in range(DEPTH):
                for src in dense_units(l):
                    load(u, src, u % RING)
                    u += 1
                    if u == 1:
                        sp.dma_start(relb_sb[0:BUCKETS + 1], relb).then_inc(table_dma, 16)
                        sp.dma_start(hot_sb[0:BUCKETS + 1], hot_in).then_inc(table_dma, 16)
                    if u == 2:
                        small_loads()
                    if u == RING:
                        skew_bias()
                        sp.dma_start(xa[:], x.rearrange("(b p) d -> p b d", p=P)).then_inc(x_dma, 16)
                if l == 0:
                    gu = w_gu.rearrange("(k p) n -> p k n", p=P)
                    dn = w_dn.rearrange("(k p) n -> p k n", p=P)
                    def hidden(u, i, slot):
                        load(u, gu[:, :, bass.ds(i * 256, 256)], slot)
                        load(u + 1, gu[:, :, bass.ds(DFF + i * 256, 256)], (slot + 1) % RING)
                    def down(u, i, slot):
                        load(u, dn[:, bass.ds(i * 2, 2), :], slot)
                    hidden(u, 0, u % RING)
                    hidden(u + 2, 1, (u + 2) % RING)
                    down(u + 4, 0, (u + 4) % RING)
                    hidden(u + 5, 2, (u + 5) % RING)
                    down(u + 7, 1, (u + 7) % RING)
                    u += 8
                    with sp.Fori(1, FSTEPS // 2) as m:
                        v = u + (m - 1) * 6
                        hidden(v, 2 * m + 1, u % RING)
                        down(v + 2, 2 * m, (u + 2) % RING)
                        hidden(v + 3, 2 * m + 2, (u + 3) % RING)
                        down(v + 5, 2 * m + 1, (u + 5) % RING)
                    u += (FSTEPS // 2 - 1) * 6
                    down(u, FSTEPS - 1, u % RING)
                    u += 1
            assert u == MOE_BASE
            in_moe[0] = True
            sp.wait_ge(unit_used, DEPTH * PLAIN_UNITS)
            gu = moe_gu.rearrange("(m p) n -> p m n", p=P)
            dn = moe_dn.rearrange("(m p) n -> p m n", p=P)

            def expert_units(kind, j, e, u, shift=0):
                for n in range(2):
                    if kind == "d":
                        src = dn[:, bass.ds(e * (DFE // P) + j * 4 + 2 * n, 2), :]
                    else:
                        c = j * 512 + (DFE if kind == "u" else 0)
                        src = gu[:, bass.ds(e * KD + 4 * n, 4), c:c + 512]
                    load(u + n + shift, src, (u + n) % RING)

            for (kind, j), u in order_first.items():
                expert_units(kind, j, 0, u)
            sp.wait_ge(pass_ready, 1)
            more = sp.value_load(npass[0:1, 0:1], min_val=NE - 1, max_val=2 * NE - 1)
            with sp.Fori(0, more) as it:
                e, after, shift = it % NE, (it + 1) % NE, it * EXPERT_UNITS
                for (kind, j), u in order.items():
                    expert_units(kind, j, e, u, shift)
                for (kind, j), u in order_ahead.items():
                    expert_units(kind, j, e if kind == "d" else after, u, shift)
            for (kind, j), u in order_last.items():
                expert_units(kind, j, NE - 1, u, more * EXPERT_UNITS)
            for b in range(NB):
                sp.wait_ge(ln_ready, 3 * NB + b + 1)
                sp.dma_start(out.rearrange("(b p) d -> p b d", p=P)[:, b, :], xa[:, b, :]).then_inc(out_dma, 16)
            sp.wait_ge(out_dma, 16 * NB)

        @block.tensor
        def _(pe):
            def slot(u, k):
                return ring[:, u % RING, :].rearrange("p (k n) -> p k n", k=k)

            def weights(u, rows, k, c, n):
                return (w[:, u % SPLIT, :].rearrange("p (k n) -> p k n", k=rows)[:, k, c:c + n] for w in (wh, wl))

            def product(dst, ah, al, u, rows, k, c, n, first, last):
                bh, bl = weights(u, rows, k, c, n)
                pe.matmul(dst, ah, bh, start=first, stop=False, skip_group_check=True)
                pe.matmul(dst, ah, bl, start=False, stop=False, skip_group_check=True)
                return pe.matmul(dst, al, bh, start=False, stop=last, skip_group_check=True)

            def product_by_column(dst, bh, bl, u, rows, k, c, first, last):
                ah, al = weights(u, rows, k, c, P)
                pe.matmul(dst, ah, bh, start=first, stop=False, skip_group_check=True)
                pe.matmul(dst, ah, bl, start=False, stop=False, skip_group_check=True)
                return pe.matmul(dst, al, bh, start=False, stop=last, skip_group_check=True)

            def open_group(g):
                if g >= 2:
                    pe.wait_ge(g_free[g % 2], g // 2)
                return bank[g % 2]

            def bias_rows(turn):
                if turn == 0:
                    pe.wait_ge(table_dma, 32)
                for n, b in enumerate(bias_banks):
                    h = 4 * turn + n
                    if turn:
                        pe.wait_ge(bias_row, h - 3)
                    pe.matmul(bank[b][:, 0:BIAS_W], relb_sb[0:BUCKETS + 1, h, :], hot_sb[0:BUCKETS + 1, :],
                              start=True, stop=True).then_inc(bias_ps, 1)

            pe.wait_ge(xT_dma, 16)
            for l in range(DEPTH):
                U, G = l * (DENSE_UNITS + FFN_UNITS), l * GEMM_GROUPS
                state = {"u": U, "g": G}
                if l:
                    pe.wait_ge(xT_ready, 4)

                def project(kind):
                    u, g = state["u"], state["g"]
                    w = slot(u, KD)
                    arrived(pe, u)
                    b = open_group(g)
                    for t in range(2):
                        for q, m in ((0, HD), (HD, HD)) if kind == "kv" else ((0, P),):
                            for k in range(KD):
                                mm = pe.matmul(b[q:q + m, t * SEQ:(t + 1) * SEQ], w[:, k, t * m:(t + 1) * m], xT[:, k, :],
                                               start=(k == 0), stop=(k == KD - 1))
                    mm.then_inc(g_full, 1)
                    state["g"] += 1
                    if kind == "kv":
                        b = open_group(g + 1)
                        for t in range(NB):
                            for k in range(KD):
                                mm = pe.matmul(b[:, t * P:(t + 1) * P], xT[:, k, t * P:(t + 1) * P], w[:, k, P:2 * P],
                                               start=(k == 0), stop=(k == KD - 1))
                        mm.then_inc(g_full, 1)
                        state["g"] += 1
                    pe.drain().then_inc(unit_used, 1)
                    state["u"] += 1

                def input_states(b):
                    if b == 0:
                        pe.wait_ge(u_ready, 2 * (l + 1))
                        pe.wait_ge(prep_in, 80)
                    if 8 * l + b >= 1:
                        pe.wait_ge(bu_free, 8 * l + b)
                    for t in range(2):
                        i = 2 * b + t
                        q, c = 32 * (i % 4), i // 4
                        for ri in range(2):
                            mm = pe.matmul(bank[2 + t][:, ri * SEQ:(ri + 1) * SEQ], bmat[q:q + 32, l, ri, c, :],
                                           uT[q:q + 32, c, :], start=True, stop=True)
                    mm.then_inc(bu_full, 1)

                def output_states(b):
                    c = b // 2
                    if b == 0:
                        pe.wait_ge(params_ready, 1)
                        pe.wait_ge(bias_row, HEADS)
                    pe.wait_ge(xs_ready, 2 * (8 * l + b + 1))
                    if b % 2 == 0 and 4 * l + c >= 1:
                        pe.wait_ge(y_free, 4 * l + c)
                    for t in range(2):
                        i = 2 * b + t
                        q = 32 * (i % 4)
                        for ri in range(2):
                            mm = pe.matmul(bank[4][q:q + 32, 0:SEQ], cmat[:, ri, l * ST + i, :],
                                           xs[:, ri, t * SEQ:(t + 1) * SEQ], start=(ri == 0), stop=(ri == 1))
                    mm.then_inc(y_full, 1)

                def scores(i):
                    n, kv = i // 2, i % 2
                    if i == 0:
                        pe.wait_ge(qk_ready, 4 * (l + 1))
                    if 4 * l + i >= 1:
                        pe.wait_ge(pt_ready, 4 * l + i)
                    keys = SEQ if n else P
                    for j in range(4):
                        h = 4 * kv + j
                        q = HD * (h % 2)
                        mm = pe.matmul(halves(5 + j % 2)[:, j // 2, SEQ - keys:SEQ], qT[q:q + HD, h // 2, n * P:(n + 1) * P],
                                       kT[q:q + HD, kv, 0:keys], start=True, stop=True)
                    mm.then_inc(sc_full, 1)

                def transpose_probs(i):
                    n = i // 2
                    if i == 0:
                        pe.wait_ge(const_dma, 16)
                    pe.wait_ge(probs, 4 * l + i + 1)
                    for j in range(4):
                        for s in range(1 - n, 2):
                            mm = pe.transpose(bank[5 + j // 2][:, (2 * (j % 2) + s) * P:(2 * (j % 2) + s + 1) * P],
                                              lg[:, j, s * P:(s + 1) * P], ident)
                    mm.then_inc(pt_full, 1)

                def attend(i):
                    n, kv = i // 2, i % 2
                    pe.wait_ge(pt_ready, 4 * l + i + 1)
                    if 4 * l + i >= 1:
                        pe.wait_ge(a_ready, 4 * l + i)
                    for j in range(4):
                        blocks = range(1 - n, 2)
                        for s in blocks:
                            mm = pe.matmul(bank[7][HD * (j % 2):HD * (j % 2) + HD, (j // 2) * P:(j // 2 + 1) * P],
                                           vt[:, s - 1 + n, kv * HD:(kv + 1) * HD], pr[:, 2 * j + s, :],
                                           start=(s == blocks[0]), stop=(s == 1))
                    mm.then_inc(av_full, 1)

                project("u")
                if l == 0:
                    bias_rows(0)
                project("u")
                if l == 0:
                    bias_rows(1)
                input_states(0)
                project("q")
                input_states(1)
                project("q")
                input_states(2), output_states(0)
                project("kv")
                input_states(3), output_states(1), scores(0)
                project("g")
                input_states(4), output_states(2)
                project("g")
                transpose_probs(0), input_states(5), output_states(3)
                project("g")
                attend(0), scores(1), input_states(6), output_states(4)
                project("g")
                transpose_probs(1), input_states(7), output_states(5)
                project("g")
                attend(1), scores(2), output_states(6)
                project("g")
                transpose_probs(2), output_states(7)
                project("g")
                attend(2), scores(3)

                u, g = state["u"], state["g"]
                arrived(pe, u)
                pe.wait_ge(gelu_ready, l + 1)
                w = slot(u, KA)
                for m in range(4):
                    if m % 2 == 0:
                        b = open_group(g + m // 2)
                    for k in range(KA):
                        mm = pe.matmul(b[:, (m % 2) * SEQ:(m % 2 + 1) * SEQ], w[:, k, m * P:(m + 1) * P], ga[:, k, :],
                                       start=(k == 0), stop=(k == KA - 1))
                    if m % 2:
                        mm.then_inc(g_full, 1)
                pe.drain().then_inc(unit_used, 1)
                state["u"], state["g"] = u + 1, g + 2
                transpose_probs(3)
                project("g")
                attend(3)
                u, g = state["u"], state["g"]

                pe.wait_ge(a_ready, 4 * (l + 1))
                pe.wait_ge(s_ready, l + 1)
                for i in range(4):
                    arrived(pe, u + i)
                for c in range(KD):
                    b = open_group(g + c)
                    for s, act in ((0, aT), (1, sT)):
                        w = slot(u + 2 * s + c // 4, KA)
                        for k in range(KA):
                            mm = pe.matmul(b[:, s * SEQ:(s + 1) * SEQ], w[:, k, (c % 4) * P:(c % 4 + 1) * P], act[:, k, :],
                                           start=(k == 0), stop=(k == KA - 1))
                    mm.then_inc(g_full, 1)
                pe.drain().then_inc(unit_used, 4)
                u, g = u + 4, g + KD

                def by_token(u, n, banks, act, parts):
                    for t in range(NB):
                        for i in range(n):
                            if t == 0:
                                arrived(pe, u + i)
                            w = slot(u + i, 2)
                            for k in range(2):
                                for o in range(2):
                                    mm = pe.matmul(bank[banks[2 * t + o]][:, :], act[:, 2 * i + k, t * P:(t + 1) * P],
                                                   w[:, k, o * 512:(o + 1) * 512],
                                                   start=(i == 0 and k == 0), stop=(i == n - 1 and k == 1))
                            if i == n - 1:
                                mm.then_inc(parts, 1)
                            elif t == NB - 1:
                                mm.then_inc(unit_used, 1)
                    pe.drain().then_inc(unit_used, 1)

                def by_token_halves(u, n, banks, hi, lo, parts, before={}):
                    for i in range(n):
                        if before.get(i) is not None:
                            before[i]()
                        pe.wait_ge(lo_ready, split_index(u + i) + 1)
                        for k in range(2):
                            for o, b in enumerate(banks):
                                t, c = (o // 2) * P, (o % 2) * 512
                                mm = product(bank[b], hi[:, 2 * i + k, t:t + P], lo[:, 2 * i + k, t:t + P], u + i, 2, k, c, 512,
                                             i == 0 and k == 0, i == n - 1 and k == 1)
                        if i == n - 1:
                            mm.then_inc(parts, 1)
                            pe.drain().then_inc(halves_used, 1)
                        else:
                            mm.then_inc(halves_used, 1)

                pe.wait_ge(m_ready, KD * (l + 1))
                by_token(u, 4, OUT_BANKS, mT, o_full)
                u += 4

                def turn(src, b):
                    pe.wait_ge(ln_ready, b + 1 + (NB if src is xa else 2 * NB * l))
                    for q in range(2):
                        if src is xa:
                            ps = open_group(g + 2 * b + q)
                        else:
                            ps = bank[OUT_BANKS[2 * b + q]]
                        for k in range(4):
                            mm = pe.transpose(ps[:, k * P:(k + 1) * P], src[:, b, (4 * q + k) * P:(4 * q + k + 1) * P], ident)
                        mm.then_inc(g_full if src is xa else t_full, 1)

                turn(xb, 0)
                for par in range(2):
                    pe.wait_ge(g_free[par], g // 2)
                pe.wait_ge(pT_lo, l + 1)
                by_token_halves(u, 1, (0, 1, 4, 7), pTh, pTl, pp_full)
                turn(xb, 1)
                pe.wait_ge(xT_lo, 4 * (l + 1))
                count_tokens = turn_logits = None
                if l == 1:
                    pe.wait_ge(rt_lo, 1)
                    pe.wait_ge(pp_read, 3)
                    dst = bank[0][0:NE, 0:SEQ]
                    for k in range(KD):
                        pe.matmul(dst, rth[:, k, :], xTh[:, k, :], start=(k == 0), stop=False)
                        pe.matmul(dst, rtl[:, k, :], xTh[:, k, :], start=False, stop=False)
                        mm = pe.matmul(dst, rth[:, k, :], xTl[:, k, :], start=False, stop=(k == KD - 1))
                    mm.then_inc(r_full, 1)

                    def turn_logits():
                        pe.wait_ge(rl_copied, 1)
                        for b in range(NB):
                            mm = pe.transpose(bank[0][:, b * NE:(b + 1) * NE], rl[:, b * P:(b + 1) * P], ident[0:NE, 0:NE])
                        mm.then_inc(r_full, 1)

                    def count_tokens():
                        pe.wait_ge(sel_ready, 1)
                        pe.matmul(bank[0][:, 0:8], below, selm[:, 0, :], start=True, stop=True)
                        pe.matmul(bank[0][:, 8:16], below, selm[:, 1, :], start=True, stop=False)
                        pe.matmul(bank[0][:, 8:16], ones, selm[:, 0, :], start=False, stop=True)
                        pe.matmul(bank[0][:, 16:24], ones, selm[:, 0, :], start=True, stop=False)
                        pe.matmul(bank[0][:, 16:24], ones, selm[:, 1, :], start=False, stop=True).then_inc(pos_full, 1)

                by_token_halves(u + 1, 4, OUT_BANKS, xTh, xTl, pg_full, {1: turn_logits, 3: count_tokens})
                u += 5
                pe.wait_ge(pp_read, 2 * (l + 1))

                if l == 0:
                    def up(s, lap, par, free):
                        if free is not None:
                            pe.wait_ge(h_ready, free)
                        for o in range(2):
                            pe.wait_ge(lo_ready, split_index(s + o) + 1 + lap)
                            for f in range(2):
                                for k in range(KD):
                                    mm = product_by_column(bank[HIDDEN_BANKS[par][o]][:, f * SEQ:(f + 1) * SEQ], xTh[:, k, :], xTl[:, k, :],
                                                           s + o, KD, k, f * P, k == 0, k == KD - 1)
                            if o:
                                mm.then_inc(h_full, 1)
                                pe.drain().then_inc(halves_used, 1)
                            else:
                                mm.then_inc(halves_used, 1)

                    def down(s, lap, par, ready, first=False, last=False):
                        pe.wait_ge(h_ready, ready)
                        pe.wait_ge(lo_ready, split_index(s) + 1 + lap)
                        if first:
                            pe.wait_ge(pg_th, 2)
                        for n in range(2):
                            for m in range(4):
                                k, o = (n, m) if not last else (m // 2, 2 * n + m % 2)
                                t = k * SEQ + (o // 2) * P
                                mm = product(bank[OUT_BANKS[o]], hidh[:, par, t:t + P], hidl[:, par, t:t + P], s, 2, k,
                                             (o % 2) * 512, 512, first and k == 0, last and k == 1)
                            if last:
                                mm.then_inc(o_full, 1)
                        if not last:
                            mm.then_inc(h_used, 1)
                        pe.drain().then_inc(halves_used, 1)

                    up(u, 0, 0, None)
                    up(u + 2, 0, 1, None)
                    down(u + 4, 0, 0, 1, first=True)
                    up(u + 5, 0, 0, 1)
                    down(u + 7, 0, 1, 2)
                    u += 8
                    with pe.Fori(1, FSTEPS // 2) as m:
                        lap = (m - 1) * 6
                        up(u, lap, 1, 2 * m)
                        down(u + 2, lap, 0, 2 * m + 1)
                        up(u + 3, lap, 0, 2 * m + 1)
                        down(u + 5, lap, 1, 2 * m + 2)
                    u += (FSTEPS // 2 - 1) * 6
                    down(u, 0, 0, FSTEPS, last=True)
                    u += 1
                    turn(xa, 0), turn(xa, 1)
                    assert g + 4 == GEMM_GROUPS

            def slot_group(x, it):
                if it is None:
                    pe.wait_ge(x_free[x % 2], 1)
                else:
                    pe.wait_ge(x_free[x % 2], it * (SLOT_GROUPS // 2) + x // 2 + 1 + EARLY // 2)
                return bank[5 + x % 2]

            def gather(x, it, n):
                pe.wait_ge(pick_ready, n)
                for half in range(2):
                    psx = slot_group(x + half, it)
                    for k in range(4):
                        for b in range(NB):
                            dc = 4 * half + k
                            mm = pe.matmul(psx[:, k * P:(k + 1) * P], xb[:, b, dc * P:(dc + 1) * P], pick[:, b, :],
                                           start=(b == 0), stop=(b == NB - 1))
                    mm.then_inc(x_full, 1)

            def project(j, o, u, it):
                for kk in (0, 4):
                    pe.wait_ge(lo_ready, split_index(u) + 1 + it * EXPERT_UNITS)
                    for k in range(4):
                        mm = product(bank[HIDDEN_BANKS[j % 2][o]], xgh[:, kk + k, :], xgl[:, kk + k, :], u, 4, k, 0, 512,
                                     kk + k == 0, kk + k == KD - 1)
                    if o and kk:
                        mm.then_inc(h_full, 1)
                        pe.drain().then_inc(halves_used, 1)
                    else:
                        mm.then_inc(halves_used, 1)
                    u += 1

            def turn_hidden(i, x, it):
                pe.wait_ge(h_ready, FSTEPS + it * ESTEPS + i + 1)
                psx = slot_group(x, it)
                for k in range(4):
                    mm = pe.transpose(psx[:, k * P:(k + 1) * P], hid[:, i % 2, k * P:(k + 1) * P], ident)
                mm.then_inc(x_full, 1)

            def down(i, u, it):
                pe.wait_ge(hT_lo, it * ESTEPS + i + 1)
                if i == 0:
                    pe.wait_ge(outer_added, 2 * it + 1)
                for kk in range(2):
                    pe.wait_ge(lo_ready, split_index(u) + 1 + it * EXPERT_UNITS)
                    for k in range(2):
                        c = 2 * kk + k
                        for o in range(2):
                            mm = product(bank[2 + o], hidh[:, i % 2, c * P:(c + 1) * P], hidl[:, i % 2, c * P:(c + 1) * P],
                                         u, 2, k, o * 512, 512, i == 0 and c == 0, i == ESTEPS - 1 and c == 3)
                    if i == ESTEPS - 1 and kk:
                        mm.then_inc(ye_full, 1)
                        pe.drain().then_inc(halves_used, 1)
                    else:
                        mm.then_inc(halves_used, 1)
                    u += 1

            def expert(it, last):
                turn_hidden(0, 0, it)
                project(1, 1, order[("u", 1)], it)
                down(0, order[("d", 0)], it)
                psx = slot_group(1, it)
                for b in range(NB):
                    mm = pe.transpose(psx[:, b * P:(b + 1) * P], pickw[:, b, :], ident)
                mm.then_inc(x_full, 1)
                for j in range(2, ESTEPS):
                    project(j, 0, order[("g", j)], it)
                    turn_hidden(j - 1, j, it)
                    project(j, 1, order[("u", j)], it)
                    if j == ESTEPS - 1 and not last:
                        gather(ESTEPS, it, it + 2)
                    down(j - 1, order[("d", j - 1)], it)
                x = ESTEPS if last else ESTEPS + 2
                if not last:
                    pe.wait_ge(h_ready, FSTEPS + it * ESTEPS + ESTEPS)
                    pe.wait_ge(xg_lo, 2 * it + 4)
                    project(0, 0, order_ahead[("g", 0)], it)
                turn_hidden(ESTEPS - 1, x, it)
                if not last:
                    project(0, 1, order_ahead[("u", 0)], it)
                down(ESTEPS - 1, (order_last if last else order_ahead)[("d", ESTEPS - 1)], it)
                if not last:
                    project(1, 0, order_ahead[("g", 1)], it)
                pe.wait_ge(ye_ready, it + 1)
                pe.wait_ge(spread_ready, it + 1)
                for o in range(2):
                    pe.matmul(slot_group(x + 1 + o, it)[:, :], spread[:, 0, :], ye[:, o * 512:(o + 1) * 512],
                              start=True, stop=True).then_inc(x_full, 1)
                for o in range(2):
                    pe.matmul(bank[2 + o][:, :], spread[:, 1, :], ye[:, o * 512:(o + 1) * 512],
                              start=True, stop=True).then_inc(spread_full, 1)

            gather(0, None, 1)
            pe.wait_ge(xg_lo, 2)
            project(0, 0, order_first[("g", 0)], 0)
            project(0, 1, order_first[("u", 0)], 0)
            project(1, 0, order_first[("g", 1)], 0)
            pe.wait_ge(pass_ready, 1)
            more = pe.value_load(npass[0:1, 0:1], min_val=NE - 1, max_val=2 * NE - 1)
            with pe.Fori(0, more) as it:
                expert(it, False)
            expert(more, True)

        @block.scalar
        def _(act):
            act.wait_ge(exp_in, 1)
            act.activation(sm(SN), sm(TH), ACT.Sin).then_inc(exp_out, 1)
            act.activation(sm(SH), sm(TH), ACT.Sin, scale=0.5).then_inc(exp_out, 1)

            def copy_rows(turn):
                for n, b in enumerate(bias_banks):
                    h = 4 * turn + n
                    act.wait_ge(bias_ps, h + 1)
                    act.activation(rows[:, h, :], bank[b][:, 0:BIAS_W], ACT.Copy).then_inc(bias_row, 1)

            for l in range(DEPTH):
                G = l * GEMM_GROUPS
                gate = [0]

                def group(g):
                    act.wait_ge(g_full, G + g + 1)
                    return halves(g % 2)

                def gates():
                    g = 6 + gate[0] if gate[0] < 7 else 15
                    act.activation(gth[:, 2 * gate[0]:2 * gate[0] + 2, :], group(g), ACT.Tanh, scale=0.5).then_inc(g_free[g % 2], 1)
                    gate[0] += 1

                def exp_probs(i):
                    act.wait_ge(soft_in, 2 * (4 * l + i + 1))
                    act.activation(esk, esk, ACT.Exp).then_inc(soft_exp, 1)
                    for j in range(4):
                        part = lg[:, j, (1 - i // 2) * P:]
                        ins = act.activation(part, part, ACT.Exp, bias=neg_mx[:, j:j + 1], accum_out=den[:, j:j + 1])
                    ins.then_inc(soft_exp, 1)

                def copy_probs(i):
                    act.wait_ge(pt_full, 4 * l + i + 1)
                    if 4 * l + i >= 1:
                        act.wait_ge(av_full, 4 * l + i)
                    n = i // 2
                    for j in range(2):
                        src = bank[5 + j][:, :].rearrange("p (h s n) -> p h s n", h=2, s=2)
                        dst = pr[:, 4 * j:4 * j + 4, :].rearrange("p (h s) n -> p h s n", h=2)
                        ins = act.activation(dst[:, :, 1 - n:, :], src[:, :, 1 - n:, :], ACT.Copy)
                    ins.then_inc(pt_ready, 1)

                def copy_attended(i):
                    n, kv = i // 2, i % 2
                    act.wait_ge(av_full, 4 * l + i + 1)
                    src = bank[7][:, 0:2 * P].rearrange("p (c n) -> p c n", c=2)
                    act.activation(aT[:, 2 * kv:2 * kv + 2, n * P:(n + 1) * P], src, ACT.Copy).then_inc(a_ready, 1)

                for g in (0, 1):
                    act.activation(uT[:, 2 * g:2 * g + 2, :], group(g), ACT.Copy).then_inc(u_ready, 1)
                    act.wait_ge(u_ready, 2 * l + g + 1)
                    act.nop().then_inc(g_free[g], 1)
                    if l == 0:
                        copy_rows(g)
                for g in (2, 3):
                    src = group(g)
                    act.activation(qT[:, 2 * (g - 2):2 * (g - 1), :], src, ACT.Copy, scale=HD ** -0.5).then_inc(qk_ready, 1)
                    act.wait_ge(qk_ready, 4 * l + g - 1)
                    act.nop().then_inc(g_free[g % 2], 1)
                act.activation(kT, group(4), ACT.Copy).then_inc(qk_ready, 1)
                act.wait_ge(qk_ready, 4 * l + 3)
                act.nop().then_inc(g_free[0], 1)
                act.wait_ge(g_full, G + 6)
                act.activation(vt, bank[1][:, 0:2 * P].rearrange("p (a b) -> p a b", a=2), ACT.Copy).then_inc(qk_ready, 1)
                act.wait_ge(qk_ready, 4 * l + 4)
                act.nop().then_inc(g_free[1], 1)
                gates()
                exp_probs(0), gates(), copy_probs(0), gates(), copy_attended(0)
                exp_probs(1), gates(), copy_probs(1), gates(), copy_attended(1)
                exp_probs(2), gates(), copy_probs(2)
                act.wait_ge(gelu_in, l + 1)
                act.activation(ga, ga, ACT.Tanh, scale=GELU_C).then_inc(gelu_th, 1)
                gates(), copy_attended(2)
                exp_probs(3)
                for m in range(4):
                    g = 13 + m // 2
                    act.wait_ge(g_full, G + g + 1)
                    ins = act.activation(uT[:, m, :], bank[g % 2][:, (m % 2) * SEQ:(m % 2 + 1) * SEQ], ACT.Tanh,
                                         bias=sm_hb[:, 4 * l + m:4 * l + m + 1], scale=0.5)
                    ins.then_inc(glu_th, 1)
                    if m % 2:
                        act.wait_ge(glu_th, 4 * l + m + 1)
                        act.nop().then_inc(g_free[g % 2], 1)
                copy_probs(3), gates(), copy_attended(3)

                U = l * (DENSE_UNITS + FFN_UNITS) + PLAIN_UNITS
                act.wait_ge(m_ready, KD * (l + 1))
                act.wait_ge(pt_dma, 16 * (l + 1))
                act.activation(pTh[:], pT[:], ACT.Copy).then_inc(pT_hi, 1)
                make_hi(act, U), make_hi(act, U + 1)

                def turned(b):
                    for q in range(2):
                        act.wait_ge(t_full, 4 * l + 2 * b + q + 1)
                        src = bank[OUT_BANKS[2 * b + q]][:, :].rearrange("p (k n) -> p k n", k=4)
                        act.activation(xTh[:, 4 * q:4 * q + 4, b * P:(b + 1) * P], src, ACT.Copy).then_inc(xT_hi, 1)

                def copy_projection(b):
                    act.wait_ge(pp_full, l + 1)
                    act.wait_ge(ln_ready, 2 * NB * l + b + 1)
                    for o in range(2):
                        ins = act.activation(xa[:, b, o * 512:(o + 1) * 512], bank[(0, 1, 4, 7)[2 * b + o]][:, :], ACT.Copy, scale=0.5)
                    ins.then_inc(pp_read, 1)

                make_hi(act, U + 2)
                turned(0)
                if l == 1:
                    act.wait_ge(rt_dma, 16)
                    act.activation(rth[:], rt, ACT.Copy).then_inc(rt_hi, 1)
                copy_projection(0)
                turned(1)
                copy_projection(1)
                make_hi(act, U + 3)
                if l == 1:
                    act.wait_ge(soft_in, 2 * 4 * DEPTH + 1)
                    act.activation(gts[:, 0:2], gts[:, 0:2], ACT.Exp).then_inc(soft_exp, 1)
                make_hi(act, U + 4)
                make_hi(act, U + 5), make_hi(act, U + 6)
                act.wait_ge(pg_full, l + 1)
                for b in (1, 0):
                    for o in (2 * b, 2 * b + 1):
                        ins = act.activation(pth[:, o, :], bank[OUT_BANKS[o]][:, :], ACT.Tanh, scale=0.5)
                    ins.then_inc(pg_th, 1)
                if l == 0:
                    def hidden_tanh(i, par):
                        act.wait_ge(h_full, i)
                        if not isinstance(i, int) or i >= 3:
                            act.wait_ge(h_ready, i - 2)
                        act.activation(hth[:, par, :], bank[HIDDEN_BANKS[par][0]][:, :], ACT.Tanh, scale=0.5).then_inc(h_th, 1)

                    def hidden_hi(i, par):
                        act.wait_ge(hid_full, i)
                        if not isinstance(i, int) or i >= 3:
                            act.wait_ge(h_used, i - 2)
                        act.activation(hidh[:, par, :], hff[:], ACT.Copy).then_inc(hid_hi, 1)

                    V = U + 7
                    make_hi(act, V)
                    act.wait_ge(res_ready, 1)
                    hidden_tanh(1, 0), make_hi(act, V + 1), hidden_hi(1, 0), make_hi(act, V + 2)
                    make_hi(act, V + 3), hidden_tanh(2, 1), make_hi(act, V + 4), hidden_hi(2, 1), make_hi(act, V + 5)
                    V += 6
                    with act.Fori(1, FSTEPS // 2) as m:
                        laps = m - 1
                        for t in range(2):
                            make_hi(act, V + 3 * t, laps)
                            hidden_tanh(2 * m + 1 + t, t)
                            make_hi(act, V + 3 * t + 1, laps)
                            hidden_hi(2 * m + 1 + t, t)
                            make_hi(act, V + 3 * t + 2, laps)
                    V += 6 * (FSTEPS // 2 - 1)
                    hidden_tanh(FSTEPS, 0), hidden_hi(FSTEPS, 0), make_hi(act, V)
                    assert V + 1 == DENSE_UNITS + FFN_UNITS
                    for i in range(4):
                        g = 24 + i
                        act.wait_ge(g_full, g + 1)
                        b, q = i // 2, i % 2
                        src = bank[g % 2][:, :].rearrange("p (k n) -> p k n", k=4)
                        act.activation(xT[:, 4 * q:4 * q + 4, b * P:(b + 1) * P], src, ACT.Copy).then_inc(xT_ready, 1)
                        act.wait_ge(xT_ready, i + 1)
                        act.nop().then_inc(g_free[g % 2], 1)

            def slot_group(x, it):
                act.wait_ge(x_full, it * SLOT_GROUPS + x + 1 + EARLY)
                return bank[5 + x % 2]

            def copy_gathered(x0, n0, it):
                for half in range(2):
                    if it is None:
                        act.wait_ge(x_full, half + 1)
                        b = bank[5 + half]
                    else:
                        b = slot_group(x0 + half, it)
                    act.activation(xgh[:, 4 * half:4 * half + 4, :], b[:, :].rearrange("p (a b) -> p a b", a=4),
                                   ACT.Copy).then_inc(xg_ready, 1)

            def two_hi(u, it):
                for n in range(2):
                    make_hi(act, u + n, it * (EXPERT_UNITS // RING))

            def hidden_tanh(j, it):
                act.wait_ge(h_full, FSTEPS + it * ESTEPS + j + 1)
                act.wait_ge(h_ready, FSTEPS + it * ESTEPS + max(j - 1, 0))
                act.activation(hth[:, j % 2, :], bank[HIDDEN_BANKS[j % 2][0]][:, :], ACT.Tanh, scale=0.5).then_inc(h_th, 1)

            def hidden_hi(i, x, it):
                act.activation(hidh[:, i % 2, :], slot_group(x, it)[:, :], ACT.Copy).then_inc(hT_ready, 1)

            def expert(it, last):
                hidden_hi(0, 0, it)
                two_hi(order[("d", 0)], it)
                hidden_tanh(1, it)
                two_hi(order[("g", 2)], it)
                act.activation(spread[:], slot_group(1, it)[:, 0:2 * P].rearrange("p (a b) -> p a b", a=2),
                               ACT.Copy).then_inc(spread_ready, 1)
                act.wait_ge(spread_ready, it + 1)
                act.nop().then_inc(x_free[1], 1)
                for j in range(2, ESTEPS):
                    if j > 2:
                        two_hi(order[("g", j)], it)
                    two_hi(order[("u", j)], it)
                    hidden_hi(j - 1, j, it)
                    two_hi(order[("d", j - 1)], it)
                    hidden_tanh(j, it)
                x = ESTEPS if last else ESTEPS + 2
                if not last:
                    copy_gathered(ESTEPS, None, it)
                    two_hi(order_ahead[("g", 0)], it), two_hi(order_ahead[("u", 0)], it)
                else:
                    two_hi(order_last[("d", ESTEPS - 1)], it)
                hidden_hi(ESTEPS - 1, x, it)
                if not last:
                    two_hi(order_ahead[("d", ESTEPS - 1)], it)
                    hidden_tanh(0, it + 1)
                    two_hi(order_ahead[("g", 1)], it)
                act.wait_ge(ye_full, it + 1)
                act.activation(ye[:, 0:512], bank[2][:, :], ACT.Copy)
                act.activation(ye[:, 512:1024], bank[3][:, :], ACT.Copy).then_inc(ye_ready, 1)
                if not last:
                    two_hi(order[("u", 1)], it + 1)

            copy_gathered(0, 0, None)
            two_hi(order_first[("u", 0)], 0)
            two_hi(order_first[("g", 1)], 0)
            act.wait_ge(res_ready, 2)
            hidden_tanh(0, 0)
            two_hi(order[("u", 1)], 0)
            act.wait_ge(pass_ready, 1)
            more = act.value_load(npass[0:1, 0:1], min_val=NE - 1, max_val=2 * NE - 1)
            with act.Fori(0, more) as it:
                expert(it, False)
            expert(more, True)

        @block.gpsimd
        def _(pool):
            c = Chain(pool, pool_step)
            c.link(pool.memset(half_neg, -0.5))

            def load_ln(n):
                if n:
                    pool.wait_ge(ln_used, 2 * n)
                pool.dma_start(lnp[:], ln_in[n]).then_inc(ln_dma, 16)

            pool.wait_ge(powers_ready, 1)

            def make_phases(l, ch):
                n = 4 * l + ch
                if n >= 2:
                    pool.wait_ge(phase_used, 2 * (n - 1))
                phases(pool, c.link, ptm, l, ch)
                pool.nop().then_inc(phase_ready, 1)

            def root(n):
                for b in range(NB):
                    pool.wait_ge(var_ready, NB * n + b + 1)
                    pool.tensor_tensor(rstd, veps, half_neg, ALU.pow).then_inc(rstd_ready, 1)

            make_phases(0, 1)
            pool.dma_start(pT[:], pT_in[0].rearrange("(k p) n -> p k n", p=P)).then_inc(pt_dma, 16)
            load_ln(0)
            for l in range(DEPTH):
                for b in range(8):
                    if not vector_states(b):
                        states(pool, l, b)
                    if b % 2 and b // 2 + 2 < 4:
                        make_phases(l, b // 2 + 2)
                pool.wait_ge(pT_lo, l + 1)
                if l == 0:
                    root(0)
                    load_ln(1)
                    pool.wait_ge(pp_full, 1)
                    pool.dma_start(pT[:], pT_in[1].rearrange("(k p) n -> p k n", p=P)).then_inc(pt_dma, 16)
                    make_phases(1, 0), make_phases(1, 1)
                    root(1)
                    load_ln(2)
                else:
                    pool.dma_start(rt, router.rearrange("(k p) n -> p k n", p=P)).then_inc(rt_dma, 16)
                    root(2)
                    load_ln(3)
            pool.wait_ge(pass_ready, 1)
            root(3)

        @block.vector
        def _(dve):
            c = Chain(dve, dve_step)
            link = c.link

            def exp_accurate(dst, src, t1, t2, t3):
                link(dve.tensor_scalar(t1, src, -87.0, 88.0, ALU.max, ALU.min))
                link(dve.tensor_scalar(t2, t1, 1.4426950408889634, 12582912.0, ALU.mult, ALU.add))
                link(dve.tensor_scalar(t2, t2, -12582912.0, None, ALU.add))
                link(dve.scalar_tensor_tensor(out=t1, in0=t2, scalar=-0.693359375, in1=t1, op0=ALU.mult, op1=ALU.add))
                link(dve.scalar_tensor_tensor(out=t1, in0=t2, scalar=2.12194440e-4, in1=t1, op0=ALU.mult, op1=ALU.add))
                link(dve.tensor_scalar(t3, t1, 1 / 5040.0, 1 / 720.0, ALU.mult, ALU.add))
                for co in (1 / 120.0, 1 / 24.0, 1 / 6.0, 0.5, 1.0, 1.0):
                    link(dve.tensor_tensor(t3, t3, t1, ALU.mult))
                    link(dve.tensor_scalar(t3, t3, co, None, ALU.add))
                link(dve.tensor_scalar(t2, t2, 127.0, 8388608.0, ALU.add, ALU.mult))
                link(dve.tensor_copy(t1.bitcast(I32), t2))
                link(dve.tensor_tensor(dst, t3, t1, ALU.mult))

            dve.wait_ge(angle_dma, 48)
            exp_accurate(sm(DT), sm(LDT), sm(NR), sm(NI), sm(DEN))
            link(dve.tensor_tensor(sm(TH), sm(LIM), sm(DT), ALU.mult))
            link(dve.tensor_scalar(sm(K1), sm(TH), 0.15915494309189535, 12582912.0, ALU.mult, ALU.add))
            link(dve.tensor_scalar(sm(K1), sm(K1), -12582912.0, None, ALU.add))
            for part in (6.28125, 1.9340515136718750e-3, 1.2556659146e-06):
                link(dve.scalar_tensor_tensor(out=sm(TH), in0=sm(K1), scalar=-part, in1=sm(TH), op0=ALU.mult, op1=ALU.add))
            dve.tensor_scalar(sm(TH), sm(TH), -3.1415925, 3.1415925, ALU.max, ALU.min).then_inc(exp_in, 1)
            dve.wait_ge(exp_out, 2)
            link(dve.tensor_tensor(sm(CS), sm(SH), sm(SH), ALU.mult))
            link(dve.tensor_scalar(sm(CS), sm(CS), -2.0, 1.0, ALU.mult, ALU.add))
            dve.tensor_copy(sm(PWR), sm(CS))
            link(dve.tensor_copy(sm(PWI), sm(SN)))
            for j in range(7):
                a, b = sm(PWR + j), sm(PWI + j)
                dve.tensor_tensor(sm(K1), a, a, ALU.mult)
                dve.tensor_tensor(sm(K2), b, b, ALU.mult)
                link(dve.tensor_tensor(sm(PWI + j + 1), a, b, ALU.mult))
                dve.tensor_tensor(sm(PWR + j + 1), sm(K1), sm(K2), ALU.subtract)
                link(dve.tensor_scalar(sm(PWI + j + 1), sm(PWI + j + 1), 2.0, None, ALU.mult))
            dve.nop().then_inc(powers_ready, 1)
            phases(dve, link, vw, 0, 0)
            link(dve.tensor_tensor(sm(K1), sm(LRE), sm(DT), ALU.mult))
            exp_accurate(sm(RR), sm(K1), sm(NR), sm(NI), sm(DEN))
            link(dve.tensor_tensor(sm(NR), sm(RR), sm(CS), ALU.mult))
            link(dve.tensor_scalar(sm(NR), sm(NR), -1.0, None, ALU.add))
            link(dve.tensor_tensor(sm(NI), sm(RR), sm(SN), ALU.mult))
            link(dve.tensor_tensor(sm(DEN), sm(LRE), sm(LRE), ALU.mult))
            link(dve.tensor_tensor(sm(K1), sm(LIM), sm(LIM), ALU.mult))
            link(dve.tensor_tensor(sm(DEN), sm(DEN), sm(K1), ALU.add))
            link(dve.reciprocal(sm(DEN), sm(DEN)))
            link(dve.tensor_tensor(sm(CRE), sm(NR), sm(LRE), ALU.mult))
            link(dve.tensor_tensor(sm(K1), sm(NI), sm(LIM), ALU.mult))
            link(dve.tensor_tensor(sm(CRE), sm(CRE), sm(K1), ALU.add))
            link(dve.tensor_tensor(sm(CRE), sm(CRE), sm(DEN), ALU.mult))
            link(dve.tensor_tensor(sm(CIM), sm(NI), sm(LRE), ALU.mult))
            link(dve.tensor_tensor(sm(K1), sm(NR), sm(LIM), ALU.mult))
            link(dve.tensor_tensor(sm(CIM), sm(CIM), sm(K1), ALU.subtract))
            link(dve.tensor_tensor(sm(CIM), sm(CIM), sm(DEN), ALU.mult))

            def output_parameters():
                dve.wait_ge(prep_in, 80)
                wide = [P, DEPTH * ST, 32]
                cr, ci = (craw[:, r, :].rearrange("p (a b) -> p a b", b=32) for r in range(2))
                kr, ki = (sm(r).unsqueeze(2).to_broadcast(wide) for r in (CRE, CIM))
                sc = prod.rearrange("p a b -> p (a b)")[:, 0:DEPTH * ST * 32].rearrange("p (a b) -> p a b", b=32)
                link(dve.tensor_tensor(cmat[:, 0], cr, kr, ALU.mult))
                link(dve.tensor_tensor(sc, ci, ki, ALU.mult))
                link(dve.tensor_tensor(cmat[:, 0], cmat[:, 0], sc, ALU.subtract))
                link(dve.tensor_tensor(cmat[:, 1], cr, ki, ALU.mult))
                link(dve.tensor_tensor(sc, ci, kr, ALU.mult))
                link(dve.tensor_tensor(cmat[:, 1], cmat[:, 1], sc, ALU.add))
                link(dve.tensor_scalar(cmat[:, 1], cmat[:, 1], -1.0, None, ALU.mult))
                dve.tensor_scalar(sm_hb, sm_hb, 0.5, None, ALU.mult).then_inc(params_ready, 1)

            def layer_norm(n, src, dst, b):
                for h in range(2):
                    link(dve.bn_stats(stat[:, h, :], src[:, b, h * 512:(h + 1) * 512]))
                link(dve.bn_aggr(mv, stat))
                dve.tensor_scalar(veps, mv[:, 1:2], EPS, None, ALU.add).then_inc(var_ready, 1)
                dve.wait_ge(rstd_ready, NB * n + b + 1)
                link(dve.tensor_scalar(dst[:, b, :], src[:, b, :], mv[:, 0:1], rstd, ALU.subtract, ALU.mult))
                if b == 0:
                    dve.wait_ge(ln_dma, 16 * (n + 1))
                link(dve.tensor_tensor(dst[:, b, :], dst[:, b, :], lnp[:, 0, :], ALU.mult))
                dve.tensor_tensor(dst[:, b, :], dst[:, b, :], lnp[:, 1, :], ALU.add).then_inc(ln_ready, 1)
                dve.wait_ge(ln_ready, NB * n + b + 1)
                dve.nop().then_inc(ln_used, 1)

            def add_input(l, blocks):
                dve.wait_ge(pp_read, 2 * (l + 1))
                for b in blocks:
                    dve.wait_ge(pg_th, 2 * l + 2 - b)
                    gate = pth[:, 2 * b:2 * b + 2, :].rearrange("p o n -> p (o n)")
                    link(dve.scalar_tensor_tensor(out=xa[:, b, :], in0=gate, scalar=1.0, in1=xa[:, b, :], op0=ALU.add, op1=ALU.mult))
                    link(dve.scalar_tensor_tensor(out=xa[:, b, :], in0=xb[:, b, :], scalar=ALPHA, in1=xa[:, b, :],
                                                  op0=ALU.mult, op1=ALU.add))
                if 0 in blocks:
                    dve.nop().then_inc(res_ready, 1)

            def first_picks():
                for b in range(NB):
                    dve.tensor_scalar(pick[:, b, :], iota, posm[:, b, 0:1], None, ALU.is_equal)
                    ins = dve.tensor_scalar(pickw[:, b, :], iota, posm[:, b, 0:1], comb[:, b, 0:1], ALU.is_equal, ALU.mult)
                ins.then_inc(pick_ready, 1)

            def route():
                dve.wait_ge(r_full, 1)
                dve.tensor_copy(rl[:], bank[0][0:NE, 0:SEQ]).then_inc(rl_copied, 1)
                dve.wait_ge(r_full, 2)
                link(dve.tensor_copy(lgt, bank[0][:, 0:16].rearrange("p (a b) -> p a b", a=2)))
                for b in range(NB):
                    link(dve.max(top[:, b, :], lgt[:, b, :]))
                    link(dve.max_index(topi[:, b, :], top[:, b, :], lgt[:, b, :]))
                link(dve.tensor_copy(topf, topi[:]))
                dve.tensor_tensor(gts[:, 0:2], top[:, :, 1], top[:, :, 0], ALU.subtract).then_inc(soft_in, 1)
                dve.wait_ge(soft_exp, 8 * DEPTH + 1)
                link(dve.tensor_scalar(gts[:, 2:4], gts[:, 0:2], 1.0, None, ALU.add))
                link(dve.reciprocal(gts[:, 2:4], gts[:, 2:4]))
                link(dve.tensor_tensor(gts[:, 4:6], gts[:, 0:2], gts[:, 2:4], ALU.mult))
                for b in range(NB):
                    link(dve.tensor_scalar(comb[:, b, 0:NE], iota8, topf[:, b, 0:1], gts[:, 2 + b:3 + b], ALU.is_equal, ALU.mult))
                    link(dve.tensor_scalar(oh[:, b, :], iota8, topf[:, b, 1:2], gts[:, 4 + b:5 + b], ALU.is_equal, ALU.mult))
                    link(dve.tensor_tensor(comb[:, b, 0:NE], comb[:, b, 0:NE], oh[:, b, :], ALU.add))
                    link(dve.tensor_copy(comb[:, b, NE:], comb[:, b, 0:NE]))
                    link(dve.tensor_scalar(oh[:, b, :], iota8, topf[:, b, 0:1], None, ALU.is_equal))
                    link(dve.tensor_scalar(selm[:, b, :], iota8, topf[:, b, 1:2], None, ALU.is_equal))
                    link(dve.tensor_tensor(selm[:, b, :], selm[:, b, :], oh[:, b, :], ALU.add))
                dve.nop().then_inc(sel_ready, 1)

            def assign_slots():
                dve.wait_ge(pos_full, 1)
                link(dve.tensor_tensor(posm[:, :, 0:NE], bank[0][:, 0:16].rearrange("p (a b) -> p a b", a=2), selm, ALU.mult))
                link(dve.tensor_scalar(oh, selm, 4096.0, -4096.0, ALU.mult, ALU.add))
                link(dve.tensor_tensor(posm[:, :, 0:NE], posm[:, :, 0:NE], oh, ALU.add))
                link(dve.tensor_scalar(posm[:, :, NE:], posm[:, :, 0:NE], -float(P), None, ALU.add))
                link(dve.tensor_reduce(cnt[:, 0:1], bank[0][:, 16:24], AX, ALU.max))
                link(dve.tensor_scalar(cnt[:, 0:1], cnt[:, 0:1], float(P), float(NE), ALU.is_gt, ALU.mult))
                link(dve.tensor_scalar(cnt[:, 0:1], cnt[:, 0:1], float(NE - 1), None, ALU.add))
                dve.nop().then_inc(routed, 1)
                dve.tensor_copy(npass[0:1, 0:1], cnt[0:1, 0:1]).then_inc(pass_ready, 1)
                dve.wait_ge(pass_ready, 1)

            for l in range(DEPTH):
                G = l * GEMM_GROUPS
                dve.wait_ge(u_ready, 2 * (l + 1))

                def scan_states(b, between=None):
                    ch, n = b // 2, 8 * l + b
                    pn = 4 * l + ch
                    if b % 2 == 0 and pn:
                        dve.wait_ge(phase_ready, pn)
                    t0 = 2 * (b % 2)
                    co = phase[:, pn % 2, 0, t0:t0 + 2, :].rearrange("p a b -> p (a b)")
                    si = phase[:, pn % 2, 1, t0:t0 + 2, :].rearrange("p a b -> p (a b)")
                    dve.wait_ge(bu_full, n + 1)
                    re, im = psum[:, 2:4, 0:SEQ], psum[:, 2:4, SEQ:2 * SEQ]
                    p4 = prod.rearrange("p a (t n) -> p a t n", t=2)
                    c4, s4 = phase[:, pn % 2, 0, t0:t0 + 2, :], phase[:, pn % 2, 1, t0:t0 + 2, :]
                    dve.tensor_tensor(p4[:, 0], re, c4, ALU.mult)
                    dve.tensor_tensor(p4[:, 1], im, s4, ALU.mult)
                    dve.tensor_tensor(p4[:, 2], im, c4, ALU.mult)
                    dve.tensor_tensor(p4[:, 3], re, s4, ALU.mult).then_inc(bu_free, 1)
                    dve.wait_ge(bu_free, n + 1)
                    dve.tensor_tensor(vw[:, 0, :], prod[:, 0, :], prod[:, 1, :], ALU.add)
                    link(dve.tensor_tensor(vw[:, 1, :], prod[:, 2, :], prod[:, 3, :], ALU.subtract))
                    for t in range(2):
                        i = l * ST + 2 * b + t
                        for ri in range(2):
                            ins = dve.tensor_tensor_scan(vw[:, 2 + ri, t * SEQ:(t + 1) * SEQ], small[:, RR, i:i + 1].to_broadcast([P, SEQ]),
                                                         vw[:, ri, t * SEQ:(t + 1) * SEQ], 0.0, ALU.mult, ALU.add)
                    link(ins)
                    if between is not None:
                        normalise(between)
                    if n:
                        dve.wait_ge(xs_ready, 2 * n)
                    dve.tensor_tensor(rot[:, 0, :], vw[:, 2, :], co, ALU.mult)
                    dve.tensor_tensor(rot[:, 1, :], vw[:, 3, :], si, ALU.mult)
                    dve.tensor_tensor(rot[:, 2, :], vw[:, 2, :], si, ALU.mult)
                    dve.tensor_tensor(rot[:, 3, :], vw[:, 3, :], co, ALU.mult).then_inc(rot_ready, 1)
                    dve.wait_ge(rot_ready, n + 1)
                    dve.nop().then_inc(phase_used, 1)
                    if vector_states(b):
                        states(dve, l, b)

                def logits(i):
                    n, kv = i // 2, i % 2
                    o = (1 - n) * P
                    dve.wait_ge(sc_full, 4 * l + i + 1)
                    if l == 0 and i == 0:
                        dve.wait_ge(bias_dma, 16)
                    if 4 * l + i >= 1:
                        dve.wait_ge(pt_full, 4 * l + i)
                    for j in range(2):
                        h = 4 * kv + j
                        ins = dve.tensor_tensor(lg[:, j:4:2, o:], halves(5 + j)[:, :, o:], bias[:, h:h + 3:2, o:], ALU.add)
                    link(ins)
                    link(dve.tensor_reduce(mx, lg[:, :, o:], AX, ALU.max))
                    sk = sink[:, 8 * l + 4 * kv:8 * l + 4 * kv + 4]
                    link(dve.tensor_tensor(mx, mx, sk, ALU.max))
                    dve.tensor_tensor(esk, sk, mx, ALU.subtract).then_inc(soft_in, 1)
                    dve.tensor_scalar(neg_mx, mx, -1.0, None, ALU.mult).then_inc(soft_in, 1)

                def normalise(i):
                    o = (1 - i // 2) * P
                    dve.wait_ge(soft_exp, 2 * (4 * l + i + 1))
                    link(dve.tensor_tensor(den, den, esk, ALU.add))
                    link(dve.reciprocal(den, den))
                    dve.tensor_tensor(lg[:, :, o:], lg[:, :, o:], den.unsqueeze(2).to_broadcast([P, 4, SEQ - o]),
                                      ALU.mult).then_inc(probs, 1)

                def skip_term(ch):
                    dve.wait_ge(y_full, 8 * l + 2 * ch + 2)
                    link(dve.scalar_tensor_tensor(out=yT[:, ch, :], in0=uT[:, ch, :], scalar=sm_d[:, 4 * l + ch:4 * l + ch + 1],
                                                  in1=bank[4][:, 0:SEQ], op0=ALU.mult, op1=ALU.add))
                    dve.nop().then_inc(y_free, 1)

                scan_states(0)
                if l == 0:
                    output_parameters()
                scan_states(1), scan_states(2), skip_term(0), scan_states(3), logits(0)
                scan_states(4, between=0), skip_term(1), scan_states(5), logits(1)
                scan_states(6, between=1), skip_term(2), scan_states(7), logits(2), normalise(2), skip_term(3)

                link(dve.tensor_tensor(ga, yT, yT, ALU.mult))
                link(dve.tensor_scalar(ga, ga, 0.044715, 1.0, ALU.mult, ALU.add))
                dve.tensor_tensor(ga, ga, yT, ALU.mult).then_inc(gelu_in, 1)
                dve.wait_ge(gelu_th, l + 1)
                link(dve.scalar_tensor_tensor(out=ga, in0=ga, scalar=1.0, in1=yT, op0=ALU.add, op1=ALU.mult))
                dve.tensor_scalar(ga, ga, 0.5, None, ALU.mult).then_inc(gelu_ready, 1)
                dve.wait_ge(gelu_ready, l + 1)
                link(dve.tensor_scalar(yT, ga, 0.5, None, ALU.mult))
                logits(3), normalise(3)
                dve.wait_ge(glu_th, 4 * (l + 1))
                dve.scalar_tensor_tensor(out=sT, in0=uT, scalar=1.0, in1=yT, op0=ALU.add, op1=ALU.mult).then_inc(s_ready, 1)

                for k in range(KD):
                    g = 16 + k
                    dve.wait_ge(g_full, G + g + 1)
                    a = bank[g % 2]
                    link(dve.scalar_tensor_tensor(out=mtmp[:, 0, :], in0=gth[:, k, :], scalar=1.0, in1=a[:, 0:SEQ],
                                                  op0=ALU.add, op1=ALU.mult))
                    link(dve.scalar_tensor_tensor(out=mtmp[:, 1, :], in0=gth[:, KD + k, :], scalar=1.0, in1=a[:, SEQ:2 * SEQ],
                                                  op0=ALU.add, op1=ALU.mult))
                    dve.nop().then_inc(g_free[g % 2], 1)
                    dve.tensor_tensor(mT[:, k, :], mtmp[:, 0, :], mtmp[:, 1, :], ALU.add).then_inc(m_ready, 1)
                    dve.wait_ge(m_ready, KD * l + k + 1)

                if l == 0:
                    dve.wait_ge(x_dma, 16)
                link(dve.tensor_scalar(xa[:], xa[:], ALPHA, None, ALU.mult))
                U = l * (DENSE_UNITS + FFN_UNITS) + PLAIN_UNITS
                dve.wait_ge(pT_hi, l + 1)
                dve.tensor_tensor(pTl[:], pT[:], pTh[:].bitcast(F32), ALU.subtract).then_inc(pT_lo, 1)
                make_lo(dve, U), make_lo(dve, U + 1)
                for b in range(NB):
                    dve.wait_ge(o_full, 2 * NB * l + b + 1)
                    for o in range(2):
                        part = xa[:, b, o * 512:(o + 1) * 512]
                        link(dve.scalar_tensor_tensor(out=part, in0=bank[OUT_BANKS[2 * b + o]][:, :], scalar=0.5, in1=part,
                                                      op0=ALU.mult, op1=ALU.add))
                    layer_norm(2 * l, xa, xb, b)
                    if b == 0:
                        make_lo(dve, U + 2)
                        if l == 1:
                            dve.wait_ge(rt_hi, 1)
                            dve.tensor_tensor(rtl[:], rt, rth[:].bitcast(F32), ALU.subtract).then_inc(rt_lo, 1)
                for i in range(4):
                    dve.wait_ge(xT_hi, 4 * l + i + 1)
                    b, q = i // 2, i % 2
                    part = (slice(None), slice(4 * q, 4 * q + 4), slice(b * P, (b + 1) * P))
                    dve.tensor_tensor(xTl[part], bank[OUT_BANKS[i]][:, :].rearrange("p (k n) -> p k n", k=4), xTh[part].bitcast(F32),
                                      ALU.subtract).then_inc(xT_lo, 1)
                make_lo(dve, U + 3)
                if l == 0:
                    make_lo(dve, U + 4), make_lo(dve, U + 5), make_lo(dve, U + 6)
                    add_input(0, (1, 0))
                else:
                    route()
                    make_lo(dve, U + 4), make_lo(dve, U + 5)
                    assign_slots()
                    first_picks()
                    make_lo(dve, U + 6)
                    dve.wait_ge(pg_th, 3)
                    for s in x_free:
                        dve.nop().then_inc(s, 1)
                    dve.wait_ge(pg_th, 4)
                    dve.nop().then_inc(outer_added, 1)

                def hidden(i, par):
                    dve.wait_ge(h_th, i)
                    link(dve.scalar_tensor_tensor(out=hga[:], in0=hth[:, par, :], scalar=1.0, in1=bank[HIDDEN_BANKS[par][0]][:, :],
                                                  op0=ALU.add, op1=ALU.mult))
                    dve.scalar_tensor_tensor(out=hff[:], in0=hga[:], scalar=0.5, in1=bank[HIDDEN_BANKS[par][1]][:, :],
                                             op0=ALU.mult, op1=ALU.mult).then_inc(hid_full, 1)

                def hidden_lo(i, par):
                    dve.wait_ge(hid_hi, i)
                    dve.tensor_tensor(hidl[:, par, :], hff[:], hidh[:, par, :].bitcast(F32), ALU.subtract).then_inc(h_ready, 1)
                    dve.wait_ge(h_ready, i)

                if l == 0:
                    V = U + 7
                    make_lo(dve, V), hidden(1, 0), make_lo(dve, V + 1), hidden_lo(1, 0), make_lo(dve, V + 2)
                    make_lo(dve, V + 3), hidden(2, 1), make_lo(dve, V + 4), hidden_lo(2, 1), make_lo(dve, V + 5)
                    V += 6
                    n0 = c.n
                    with dve.Fori(1, FSTEPS // 2) as m:
                        c.base, laps = (m - 1) * 2, m - 1
                        for t in range(2):
                            make_lo(dve, V + 3 * t, laps)
                            hidden(2 * m + 1 + t, t)
                            make_lo(dve, V + 3 * t + 1, laps)
                            hidden_lo(2 * m + 1 + t, t)
                            make_lo(dve, V + 3 * t + 2, laps)
                    c.base, c.n = 0, n0 + 2 * (FSTEPS // 2 - 1)
                    V += 6 * (FSTEPS // 2 - 1)
                    hidden(FSTEPS, 0), hidden_lo(FSTEPS, 0), make_lo(dve, V)
                    for b in range(NB):
                        dve.wait_ge(o_full, NB + b + 1)
                        for o in range(2):
                            part = xa[:, b, o * 512:(o + 1) * 512]
                            link(dve.tensor_tensor(part, bank[OUT_BANKS[2 * b + o]][:, :], part, ALU.add))
                        layer_norm(1, xa, xa, b)

            def two_lo(u, it):
                for n in range(2):
                    make_lo(dve, u + n, it * (EXPERT_UNITS // RING))

            def picks(n):
                for b in range(NB):
                    slot = posm[:, b, bass.ds(n, 1)]
                    dve.tensor_scalar(pick[:, b, :], iota, slot, None, ALU.is_equal)
                    ins = dve.tensor_scalar(pickw[:, b, :], iota, slot, comb[:, b, bass.ds(n, 1)], ALU.is_equal, ALU.mult)
                ins.then_inc(pick_ready, 1)

            def gathered_lo(x0, n, it):
                for half in range(2):
                    dve.wait_ge(xg_ready, n + half + 1)
                    x = x0 + half
                    dve.tensor_tensor(xgl[:, 4 * half:4 * half + 4, :], bank[5 + x % 2][:, :].rearrange("p (a b) -> p a b", a=4),
                                      xgh[:, 4 * half:4 * half + 4, :].bitcast(F32), ALU.subtract).then_inc(xg_lo, 1)
                    dve.wait_ge(xg_lo, n + half + 1)
                    dve.nop().then_inc(x_free[x % 2], 1)

            def hidden(j, it):
                dve.wait_ge(h_th, FSTEPS + it * ESTEPS + j + 1)
                link(dve.scalar_tensor_tensor(out=hga[:], in0=hth[:, j % 2, :], scalar=1.0, in1=bank[HIDDEN_BANKS[j % 2][0]][:, :],
                                              op0=ALU.add, op1=ALU.mult))
                dve.scalar_tensor_tensor(out=hid[:, j % 2, :], in0=hga[:], scalar=0.5, in1=bank[HIDDEN_BANKS[j % 2][1]][:, :],
                                         op0=ALU.mult, op1=ALU.mult).then_inc(h_ready, 1)

            def hidden_lo(i, x, it):
                dve.wait_ge(hT_ready, it * ESTEPS + i + 1)
                dve.tensor_tensor(hidl[:, i % 2, :], bank[5 + x % 2][:, :], hidh[:, i % 2, :].bitcast(F32),
                                  ALU.subtract).then_inc(hT_lo, 1)
                dve.wait_ge(hT_lo, it * ESTEPS + i + 1)
                dve.nop().then_inc(x_free[x % 2], 1)

            def expert(it, last):
                hidden_lo(0, 0, it)
                two_lo(order[("d", 0)], it)
                hidden(1, it)
                for j in range(2, ESTEPS):
                    two_lo(order[("g", j)], it)
                    two_lo(order[("u", j)], it)
                    hidden_lo(j - 1, j, it)
                    two_lo(order[("d", j - 1)], it)
                    hidden(j, it)
                    if j == ESTEPS - 2 and not last:
                        picks(it + 1)
                x = ESTEPS if last else ESTEPS + 2
                if not last:
                    gathered_lo(ESTEPS, 2 * it + 2, it)
                    two_lo(order_ahead[("g", 0)], it), two_lo(order_ahead[("u", 0)], it)
                else:
                    two_lo(order_last[("d", ESTEPS - 1)], it)
                hidden_lo(ESTEPS - 1, x, it)
                if not last:
                    two_lo(order_ahead[("d", ESTEPS - 1)], it)
                    hidden(0, it + 1)
                    two_lo(order_ahead[("g", 1)], it)
                    two_lo(order[("u", 1)], it + 1)
                for o in range(2):
                    g = x + 1 + o
                    dve.wait_ge(x_full, it * SLOT_GROUPS + g + 1 + EARLY)
                    part = xa[:, 0, o * 512:(o + 1) * 512]
                    link(dve.tensor_tensor(part, bank[5 + g % 2][:, :], part, ALU.add))
                    dve.nop().then_inc(x_free[g % 2], 1)
                for o in range(2):
                    dve.wait_ge(spread_full, 2 * it + o + 1)
                    part = xa[:, 1, o * 512:(o + 1) * 512]
                    dve.tensor_tensor(part, bank[2 + o][:, :], part, ALU.add).then_inc(outer_added, 1)

            gathered_lo(0, 0, None)
            make_lo(dve, order_first[("u", 0)])
            add_input(1, (1,))
            make_lo(dve, order_first[("u", 0)] + 1)
            add_input(1, (0,))
            two_lo(order_first[("g", 1)], 0)
            hidden(0, 0)
            two_lo(order[("u", 1)], 0)
            more = dve.value_load(npass[0:1, 0:1], min_val=NE - 1, max_val=2 * NE - 1)
            per_item = ESTEPS + 2
            n0 = c.n
            with dve.Fori(0, more) as it:
                c.n, c.base = n0, it * per_item
                expert(it, False)
            assert c.n == n0 + per_item
            c.n, c.base = n0, more * per_item
            expert(more, True)
            dve.wait_ge(outer_added, 2 * more + 3)
            c.sem, c.n, c.base = final_step, 0, 0
            for b in range(NB):
                layer_norm(3, xa, xa, b)


def kernel(**inputs):
    import concourse.bacc as bacc
    from concourse.bass_utils import run_bass_kernel_spmd

    a = {k: np.asarray(v) for k, v in inputs.items()}
    con, hot = constants()

    def pairs(v):
        return np.ascontiguousarray(v.reshape(DEPTH, ST, 2 * SST).transpose(2, 0, 1)).reshape(P, DEPTH * ST)

    relb = np.ones((BUCKETS + 1, HEADS, P), np.float32)
    relb[:BUCKETS] = a["rel_bias"][:, :, None]
    bm = np.zeros((4, 2, SCH, DEPTH, 2, 4, 2, SST), np.float32)
    cm = np.zeros((2, SST, 2, DEPTH, ST, 2, SCH), np.float32)
    for r, (bn, cn) in enumerate((("ssm_b_re", "ssm_c_re"), ("ssm_b_im", "ssm_c_im"))):
        b = a[bn].reshape(DEPTH, 4, 4, 2, SST, SCH)
        c = a[cn].reshape(DEPTH, ST, 2, SCH, SST)
        for par in range(2):
            bm[:, par, :, :, r, :, par, :] = b[:, :, :, par].transpose(2, 4, 0, 1, 3)
            cm[par, :, r, :, :, par, :] = c[:, :, par].transpose(3, 0, 1, 2)

    def by_channel(v):
        return np.ascontiguousarray(v.reshape(DEPTH, 4, P).transpose(2, 0, 1)).reshape(P, DEPTH * 4)

    ln = np.stack([np.stack([a[g][l], a[b][l]]) for l in range(DEPTH) for g, b in (("ln1_g", "ln1_b"), ("ln2_g", "ln2_b"))])
    arrays = {
        "x": a["x"].reshape(SEQ, D),
        "xT": np.ascontiguousarray(a["x"].reshape(SEQ, D).T),
        "pT": np.ascontiguousarray(a["p"].reshape(DEPTH, SEQ, PLE).transpose(0, 2, 1)),
        "relb": relb, "hot": hot, "const": con,
        "sinks": np.ascontiguousarray(np.broadcast_to(a["attn_sinks"].reshape(1, DEPTH * HEADS), (P, DEPTH * HEADS))),
        "lre": pairs(a["ssm_lambda_re"]), "lim": pairs(a["ssm_lambda_im"]),
        "ldt": pairs(np.repeat(a["ssm_log_dt"][:, :, None], SST, axis=2)),
        "b": bm.reshape(P, -1), "c": cm.reshape(P, -1),
        "d": by_channel(a["ssm_d"]), "bglu": by_channel(a["b_glu"]),
        "w_in": a["w_in"], "w_glu": a["w_glu"], "w_ba": a["w_branch_attn"], "w_bs": a["w_branch_ssm"], "w_out": a["w_out"],
        "ln": np.ascontiguousarray(np.broadcast_to(ln[:, None], (2 * DEPTH, P, 2, D))),
        "w_gu": a["ffn_w_gate_up"][0], "w_dn": a["ffn_w_down"][0], "router": a["moe_router"][0],
        "moe_gu": a["moe_w_gate_up"].reshape(NE * D, 2 * DFE), "moe_dn": a["moe_w_down"].reshape(NE * DFE, D),
        "w_pp": a["ple_w_proj"], "w_pg": a["ple_w_gate"],
    }
    nc = bacc.Bacc("TRN2", target_bir_lowering=False, num_devices=1)
    args, feed = [], {}
    for name, v in arrays.items():
        feed[f"in_{name}"] = v
        args.append(nc.dram_tensor(f"in_{name}", v.shape, F32, kind="ExternalInput").ap())
    scratch = nc.dram_tensor("bias_scratch", (HEADS, P + 1, BIAS_W), F32, kind="Internal").ap()
    out = nc.dram_tensor("out", (SEQ, D), F32, kind="ExternalOutput").ap()
    program(nc, *args, scratch, out)
    r = run_bass_kernel_spmd(nc, [feed], core_ids=[0])
    return r.results[0]["out"].reshape(1, SEQ, D)
```
